# Optimizing a Trainium2 kernel written in Bass

```python
import math
import jax, jax.numpy as jnp
from jax import lax
import numpy as np

D_MODEL = 1024
BATCH = 1
SEQ = 256
DEPTH = 2

CHUNK = 64
Q_BLOCK = 128
EPS = 1e-6

FOX_HEAD_DIM = 64
FOX_WIDTH = D_MODEL // 4
FOX_HEADS = FOX_WIDTH // FOX_HEAD_DIM
HGRN_KEY_DIM = 128
HGRN_WIDTH = D_MODEL // 2
HGRN_HEADS = HGRN_WIDTH // 128
HGRN_VAL_DIM = HGRN_WIDTH // HGRN_HEADS
HGRN_FORGET_DIM = HGRN_HEADS * HGRN_KEY_DIM
S5_WIDTH = D_MODEL // 4
S5_GROUP = 16
S5_GROUPS = S5_WIDTH // S5_GROUP
S5_STATE = 64

MIX_WIDTH = FOX_WIDTH + HGRN_WIDTH + S5_WIDTH
D_FF = 2816

IN_SIZES = [FOX_WIDTH, FOX_WIDTH, FOX_WIDTH, FOX_HEADS,
            HGRN_FORGET_DIM, HGRN_FORGET_DIM, HGRN_WIDTH, HGRN_WIDTH,
            S5_WIDTH]
IN_WIDTH = sum(IN_SIZES)
IN_SPLITS = [int(v) for v in np.cumsum(IN_SIZES)[:-1]]

kernel_name = "hybrid_fox_hgrn2_s5_macaron"

def rms_norm(x, gain):
    xf = x.astype(jnp.float32)
    y = xf * lax.rsqrt(jnp.mean(xf * xf, axis=-1, keepdims=True) + EPS)
    return (y * gain.astype(jnp.float32)).astype(x.dtype)

def swiglu(x, w_gate, w_up, w_down):
    return (jax.nn.silu(x @ w_gate) * (x @ w_up)) @ w_down

def fox_attention(q, k, v, f_logit):
    L = q.shape[1]
    scale = 1.0 / math.sqrt(q.shape[-1])
    c = jnp.cumsum(jax.nn.log_sigmoid(f_logit.astype(jnp.float32)), axis=1)
    c = c.transpose(0, 2, 1)
    qf = q.astype(jnp.float32).transpose(0, 2, 1, 3)
    kf = k.astype(jnp.float32).transpose(0, 2, 1, 3)
    vf = v.astype(jnp.float32).transpose(0, 2, 1, 3)
    outs = []
    for blk in range(L // Q_BLOCK):
        qs, qe = blk * Q_BLOCK, (blk + 1) * Q_BLOCK
        s = jnp.einsum('bhqd,bhkd->bhqk', qf[:, :, qs:qe], kf[:, :, :qe]) * scale
        s = s + c[:, :, qs:qe, None] - c[:, :, None, :qe]
        mask = jnp.arange(qs, qe)[:, None] >= jnp.arange(qe)[None, :]
        p = jax.nn.softmax(jnp.where(mask, s, -jnp.inf), axis=-1)
        outs.append(jnp.einsum('bhqk,bhkd->bhqd', p, vf[:, :, :qe]))
    return jnp.concatenate(outs, axis=2).transpose(0, 2, 1, 3)

def _to_chunks(t, n_chunks):
    b, _, h, d = t.shape
    return t.reshape(b, n_chunks, CHUNK, h, d).transpose(1, 0, 3, 2, 4)

def hgrn2(q, f_logit, i_in, lb):
    bsz, L, h, kd = q.shape
    vd = i_in.shape[-1]
    n = L // CHUNK
    f = lb + (1.0 - lb) * jax.nn.sigmoid(f_logit.astype(jnp.float32))
    log_f = jnp.log(f)
    key = 1.0 - f
    qc = _to_chunks(q.astype(jnp.float32), n)
    kc = _to_chunks(key, n)
    gc = _to_chunks(log_f, n)
    vc = _to_chunks(i_in.astype(jnp.float32), n)
    mask = (jnp.arange(CHUNK)[:, None] >= jnp.arange(CHUNK)[None, :])[None, None, :, :, None]

    def step(S, inp):
        q_c, k_c, g_c, v_c = inp
        b = jnp.cumsum(g_c, axis=2)
        diff = b[:, :, :, None, :] - b[:, :, None, :, :]
        decay = jnp.exp(jnp.where(mask, diff, -jnp.inf))
        attn = jnp.einsum('bhtk,bhsk,bhtsk->bhts', q_c, k_c, decay)
        o = jnp.einsum('bhts,bhsv->bhtv', attn, v_c)
        o = o + jnp.einsum('bhtk,bhkv->bhtv', q_c * jnp.exp(b), S)
        b_last = b[:, :, -1]
        S_new = jnp.exp(b_last)[..., None] * S + jnp.einsum(
            'bhsk,bhsv->bhkv', k_c * jnp.exp(b_last[:, :, None, :] - b), v_c)
        return S_new, o

    S0 = jnp.zeros((bsz, h, kd, vd), jnp.float32)
    _, o = lax.scan(step, S0, (qc, kc, gc, vc))
    return o.transpose(1, 0, 3, 2, 4).reshape(bsz, L, h, vd)

def _complex_scan_combine(e1, e2):
    a1r, a1i, b1r, b1i = e1
    a2r, a2i, b2r, b2i = e2
    ar = a1r * a2r - a1i * a2i
    ai = a1r * a2i + a1i * a2r
    br = a2r * b1r - a2i * b1i + b2r
    bi = a2r * b1i + a2i * b1r + b2i
    return (ar, ai, br, bi)

def s5_block(u, lam_re, lam_im, log_step, B_re, B_im, C_re, C_im, D, glu_w, glu_b):
    bsz, L, _ = u.shape
    uf = u.astype(jnp.float32).reshape(bsz, L, S5_GROUPS, S5_GROUP)
    lr = lam_re.astype(jnp.float32)
    li = lam_im.astype(jnp.float32)
    dt = jnp.exp(log_step.astype(jnp.float32))[:, None]
    mag = jnp.exp(lr * dt)
    lbar_re = mag * jnp.cos(li * dt)
    lbar_im = mag * jnp.sin(li * dt)
    nr, ni = lbar_re - 1.0, lbar_im
    den = lr * lr + li * li
    coef_re = (nr * lr + ni * li) / den
    coef_im = (ni * lr - nr * li) / den
    Br = B_re.astype(jnp.float32)
    Bi = B_im.astype(jnp.float32)
    bbar_re = coef_re[..., None] * Br - coef_im[..., None] * Bi
    bbar_im = coef_re[..., None] * Bi + coef_im[..., None] * Br
    bu_re = jnp.einsum('blgh,gph->blgp', uf, bbar_re)
    bu_im = jnp.einsum('blgh,gph->blgp', uf, bbar_im)
    a_re = jnp.broadcast_to(lbar_re, bu_re.shape)
    a_im = jnp.broadcast_to(lbar_im, bu_im.shape)
    _, _, x_re, x_im = lax.associative_scan(
        _complex_scan_combine, (a_re, a_im, bu_re, bu_im), axis=1)
    y = (jnp.einsum('blgp,ghp->blgh', x_re, C_re.astype(jnp.float32))
         - jnp.einsum('blgp,ghp->blgh', x_im, C_im.astype(jnp.float32))
         + D.astype(jnp.float32).reshape(S5_GROUPS, S5_GROUP) * uf)
    z = jax.nn.gelu(y.reshape(bsz, L, S5_WIDTH))
    return z * jax.nn.sigmoid(z @ glu_w.astype(jnp.float32) + glu_b.astype(jnp.float32))

def setup_inputs(seed: int = 0) -> dict:
    key = jax.random.key(seed)
    ks = jax.random.split(key, 32)
    f32 = jnp.float32

    def nrm(k, shape, scale):
        return jax.random.normal(k, shape, f32) * scale

    def gain(k, shape):
        return 1.0 + 0.02 * jax.random.normal(k, shape, f32)

    lam_im_base = jnp.pi * jnp.arange(S5_STATE, dtype=f32)
    log_lo, log_hi = math.log(0.001), math.log(0.1)
    return {
        "x": nrm(ks[0], (BATCH, SEQ, D_MODEL), 1.0),
        "ffn1_norm": gain(ks[1], (DEPTH, D_MODEL)),
        "ffn1_w_gate": nrm(ks[2], (DEPTH, D_MODEL, D_FF), D_MODEL ** -0.5),
        "ffn1_w_up": nrm(ks[3], (DEPTH, D_MODEL, D_FF), D_MODEL ** -0.5),
        "ffn1_w_down": nrm(ks[4], (DEPTH, D_FF, D_MODEL), D_FF ** -0.5),
        "mix_norm": gain(ks[5], (DEPTH, D_MODEL)),
        "w_in": nrm(ks[6], (DEPTH, D_MODEL, IN_WIDTH), D_MODEL ** -0.5),
        "fox_f_bias": nrm(ks[7], (DEPTH, FOX_HEADS), 0.1),
        "fox_q_gain": gain(ks[8], (DEPTH, FOX_HEAD_DIM)),
        "fox_k_gain": gain(ks[9], (DEPTH, FOX_HEAD_DIM)),
        "hgrn_lb": nrm(ks[10], (DEPTH, HGRN_FORGET_DIM), 0.1),
        "hgrn_o_gain": gain(ks[11], (DEPTH, HGRN_WIDTH)),
        "s5_lambda_re": -0.5 + nrm(ks[12], (DEPTH, S5_GROUPS, S5_STATE), 0.01),
        "s5_lambda_im": lam_im_base + nrm(ks[13], (DEPTH, S5_GROUPS, S5_STATE), 0.01),
        "s5_log_step": log_lo + (log_hi - log_lo) * jax.random.uniform(ks[14], (DEPTH, S5_GROUPS), f32),
        "s5_B_re": nrm(ks[15], (DEPTH, S5_GROUPS, S5_STATE, S5_GROUP), (2 * S5_GROUP) ** -0.5),
        "s5_B_im": nrm(ks[16], (DEPTH, S5_GROUPS, S5_STATE, S5_GROUP), (2 * S5_GROUP) ** -0.5),
        "s5_C_re": nrm(ks[17], (DEPTH, S5_GROUPS, S5_GROUP, S5_STATE), S5_STATE ** -0.5),
        "s5_C_im": nrm(ks[18], (DEPTH, S5_GROUPS, S5_GROUP, S5_STATE), S5_STATE ** -0.5),
        "s5_D": nrm(ks[19], (DEPTH, S5_WIDTH), 1.0),
        "s5_glu_w": nrm(ks[20], (DEPTH, S5_WIDTH, S5_WIDTH), S5_WIDTH ** -0.5),
        "s5_glu_b": nrm(ks[21], (DEPTH, S5_WIDTH), 0.02),
        "w_out": nrm(ks[22], (DEPTH, MIX_WIDTH, D_MODEL), MIX_WIDTH ** -0.5),
        "ffn2_norm": gain(ks[23], (DEPTH, D_MODEL)),
        "ffn2_w_gate": nrm(ks[24], (DEPTH, D_MODEL, D_FF), D_MODEL ** -0.5),
        "ffn2_w_up": nrm(ks[25], (DEPTH, D_MODEL, D_FF), D_MODEL ** -0.5),
        "ffn2_w_down": nrm(ks[26], (DEPTH, D_FF, D_MODEL), D_FF ** -0.5),
    }

def reference(x, ffn1_norm, ffn1_w_gate, ffn1_w_up, ffn1_w_down, mix_norm, w_in,
              fox_f_bias, fox_q_gain, fox_k_gain, hgrn_lb, hgrn_o_gain,
              s5_lambda_re, s5_lambda_im, s5_log_step, s5_B_re, s5_B_im, s5_C_re, s5_C_im,
              s5_D, s5_glu_w, s5_glu_b, w_out,
              ffn2_norm, ffn2_w_gate, ffn2_w_up, ffn2_w_down):
    bsz, L, _ = x.shape
    lb_all = jnp.cumsum(jax.nn.softmax(hgrn_lb.astype(jnp.float32), axis=0), axis=0)
    lb_all = lb_all - lb_all[0:1]
    for l in range(DEPTH):
        h = rms_norm(x, ffn1_norm[l])
        x = x + 0.5 * swiglu(h, ffn1_w_gate[l], ffn1_w_up[l], ffn1_w_down[l])

        h = rms_norm(x, mix_norm[l])
        p = h @ w_in[l]
        a_q, a_k, a_v, a_f, b_q, b_f, b_i, b_g, c_u = jnp.split(p, IN_SPLITS, axis=-1)

        q = rms_norm(a_q.reshape(bsz, L, FOX_HEADS, FOX_HEAD_DIM), fox_q_gain[l])
        k = rms_norm(a_k.reshape(bsz, L, FOX_HEADS, FOX_HEAD_DIM), fox_k_gain[l])
        v = a_v.reshape(bsz, L, FOX_HEADS, FOX_HEAD_DIM)
        o_a = fox_attention(q, k, v, a_f + fox_f_bias[l]).reshape(bsz, L, FOX_WIDTH)

        lb = lb_all[l].reshape(HGRN_HEADS, HGRN_KEY_DIM)
        o_b = hgrn2(b_q.reshape(bsz, L, HGRN_HEADS, HGRN_KEY_DIM),
                    b_f.reshape(bsz, L, HGRN_HEADS, HGRN_KEY_DIM),
                    b_i.reshape(bsz, L, HGRN_HEADS, HGRN_VAL_DIM), lb)
        o_b = rms_norm(o_b, hgrn_o_gain[l].reshape(HGRN_HEADS, HGRN_VAL_DIM))
        o_b = (o_b * jax.nn.silu(b_g.astype(jnp.float32).reshape(bsz, L, HGRN_HEADS, HGRN_VAL_DIM))
               ).reshape(bsz, L, HGRN_WIDTH)

        o_c = s5_block(c_u, s5_lambda_re[l], s5_lambda_im[l], s5_log_step[l],
                       s5_B_re[l], s5_B_im[l], s5_C_re[l], s5_C_im[l],
                       s5_D[l], s5_glu_w[l], s5_glu_b[l])

        mix = jnp.concatenate([o_a.astype(x.dtype), o_b.astype(x.dtype), o_c.astype(x.dtype)], axis=-1)
        x = x + mix @ w_out[l]

        h = rms_norm(x, ffn2_norm[l])
        x = x + 0.5 * swiglu(h, ffn2_w_gate[l], ffn2_w_up[l], ffn2_w_down[l])
    return x


_drawn_inputs = setup_inputs


def setup_inputs(seed=0):
    import zlib

    import numpy as np

    out = dict(_drawn_inputs(seed))
    spreads = {}
    factors = {'ffn1_norm': 3.585,
     'fox_f_bias': 14.045,
     'fox_q_gain': 25.366,
     'fox_k_gain': 25.837,
     'hgrn_o_gain': 17.868,
     's5_lambda_re': 64.0,
     's5_lambda_im': 25.456,
     's5_log_step': 26.344,
     's5_B_re': 35.752,
     's5_B_im': 36.152,
     's5_C_re': 36.248,
     's5_C_im': 36.792,
     's5_glu_b': 181.639,
     'ffn2_norm': 5.437,
     'hgrn_lb': 2.671,
     's5_glu_w': 5.123}
    for name, (base, spread) in spreads.items():
        noise = np.random.default_rng([zlib.crc32(name.encode()), seed]).standard_normal(out[name].shape)
        drawn = base * np.exp(spread * noise) if base else spread * noise
        out[name] = __import__('jax').numpy.asarray(drawn.astype(out[name].dtype))
    for name, factor in factors.items():
        out[name] = (out[name] * factor).astype(out[name].dtype)
    return out
```

```python
from contextlib import ExitStack

import numpy as np

import concourse.bass as bass
from concourse import mybir

F32 = mybir.dt.float32
F32R = mybir.dt.float32r
U8 = mybir.dt.uint8
ALU = mybir.AluOpType
ACT = mybir.ActivationFunctionType
AX = mybir.AxisListType

P = 128
DEPTH = 2
T = 256
D = 1024
KT = D // P
FF = 2816
ITERS = FF // 256
FOX_HEADS, FOX_DIM = 4, 64
HEADS = 4
GROUPS, GROUP, STATE = 16, 16, 64
S5_TILES = GROUPS * STATE // P
CHUNK = 64
EPS = 1e-6

FFN_UNITS = 3 * ITERS
IN_UNITS = 12
OUT_UNITS = 4
UNITS = 2 * FFN_UNITS + IN_UNITS + OUT_UNITS
SPLIT_UNITS = 2 * FFN_UNITS
DIRECT_UNITS = IN_UNITS + OUT_UNITS
RING = 3
VISITS = UNITS // RING

COLS = {}
_at = 0
for _name, _n in [("gain_mix", KT), ("gain_ffn2", KT), ("gain_next", KT), ("lam_re", S5_TILES),
                  ("lam_im", S5_TILES), ("log_step", S5_TILES), ("lb_logit", 2 * HEADS), ("later_layer", 1),
                  ("o_gain", HEADS), ("skip", 2), ("glu_b", 2), ("q_gain", 1), ("k_gain", 1), ("f_bias", 1),
                  ("w_forget", KT * FOX_HEADS), ("b_re", 2 * P), ("b_im", 2 * P),
                  ("c_re", S5_TILES * 32), ("c_im", S5_TILES * 32), ("glu_w", 512)]:
    COLS[_name] = (_at, _n)
    _at += _n
NPAR = _at

LEVELS = [64, 32, 16, 8, 4, 2, 1]
NLEV = len(LEVELS) + 1
NSTEP = NLEV + 1

TWO_PI = 2.0 * np.pi
PI_A = 6.28125
PI_B = float(np.float32(np.round((TWO_PI - PI_A) * 2.0 ** 22) / 2.0 ** 22))
PI_C = float(np.float32(TWO_PI - PI_A - PI_B))
ROUND = 1.5 * 2.0 ** 23


class Steps:

    def __init__(self, engine, sem, layer, per_layer):
        self.engine, self.sem, self.base, self.per_layer, self.n = engine, sem, layer * per_layer, per_layer, 0

    def mark(self, instruction):
        self.n += 1
        return instruction.then_inc(self.sem, 1)

    def wait(self):
        if self.n:
            self.engine.wait_ge(self.sem, self.base + self.n)

    def close(self):
        assert self.n == self.per_layer, f"{self.n} steps in a layer, not {self.per_layer}"


DVE_STEPS = 55
POOL_STEPS = 61


def build(nc, xT, stream, params, gain0, consts, select, masks, out):
    ctx = ExitStack()
    with ctx:
        def sb(name, shape, dt=F32, where=ctx):
            return where.enter_context(nc.sbuf_tensor(name, shape, dt))

        def sem(name):
            return ctx.enter_context(nc.semaphore(name))

        raw = [sb(f"raw{s}", [P, 2048]) for s in range(4)]
        x = sb("x", [P, KT, T])
        h = sb("h", [P, KT, T])
        sq = sb("sq", [P, 4, T])
        sumsq = sb("sumsq", [P, T])
        ln_ms = sb("ln_ms", [P, T])
        rstd = sb("rstd", [P, T])
        rstd_tok = sb("rstd_tok", [P, 4])
        par = sb("par", [P, NPAR])
        g0 = sb("g0", [P, KT])
        con = sb("con", [P, 3 * P + 384 + HEADS * T])
        sel = sb("sel", [4, 4 * T])
        mask = sb("mask", [P, NLEV * P], U8)
        eps = sb("eps", [P, 1])
        cos = sb("cos", [P, S5_TILES, T])
        sin = sb("sin", [P, S5_TILES, T])
        trig_tmp = sb("trig_tmp", [P, S5_TILES, P])
        rot = sb("rot", [P, 2, 2, S5_TILES])
        mag = sb("mag", [P, S5_TILES])
        coef = sb("coef", [P, 3, S5_TILES])
        s5s = sb("s5s", [P, 12, S5_TILES])
        c_out = sb("c_out", [P, 2, S5_TILES * 32])
        lbs = sb("lbs", [P, 8, HEADS])
        tick = sb("tick", [P, 1])
        zero = sb("zero", [P, 512], F32R)

        ffn_mem = ExitStack()
        hi = [sb(f"hi{s}", [P, 2048], F32R, ffn_mem) for s in range(RING)]
        lo = [sb(f"lo{s}", [P, 2048], F32R, ffn_mem) for s in range(RING)]
        xg_hi = sb("xg_hi", [P, KT, T], F32R, ffn_mem)
        xg_lo = sb("xg_lo", [P, KT, T], F32R, ffn_mem)
        gate = sb("gate", [P, 2, T], F32, ffn_mem)
        up = sb("up", [P, 2, T], F32, ffn_mem)
        silu = sb("silu", [P, 2, T], F32, ffn_mem)
        act = sb("act", [P, 2, T], F32, ffn_mem)
        act_hi = sb("act_hi", [P, 2, T], F32R, ffn_mem)
        act_lo = sb("act_lo", [P, 2, T], F32R, ffn_mem)
        ffn_mem.close()

        bf = sb("bf", [P, HEADS, T])
        key = sb("key", [P, HEADS, T])
        bq = sb("bq", [P, HEADS, T])
        bc = sb("bc", [P, HEADS, T])
        bsum = sb("bsum", [P, HEADS])
        dec = sb("dec", [P, 2, HEADS, T])
        qk = sb("qk", [P, 2, HEADS, T])
        attn = sb("attn", [P, 2 * HEADS, P])
        attn_x = sb("attn_x", [P, HEADS, P])
        v_b = sb("v_b", [P, 2, 512])
        bg = sb("bg", [P, HEADS, T])
        osq = dec[:, 0, :, :].rearrange("p h t -> p (h t)")
        orn = dec[:, 1, :, :].rearrange("p h t -> p (h t)")
        u = sb("u", [P, 2, T])
        ra = sb("ra", [P, 2, 2, T])
        rb = sb("rb", [P, 2, 2, T])
        xin = sb("xin", [P, 2, 2, T])
        xt = sb("xt", [P, 2, 2, T])
        ua = sb("ua", [P, 2, 2, T])
        ub = sb("ub", [P, 2, 2, T])
        xs = sb("xs", [P, S5_TILES, 2, T])
        y = trig_tmp[:, 0:4, :].rearrange("p (a b) t -> p a (b t)", a=2)
        z = trig_tmp[:, 4:8, :].rearrange("p (a b) t -> p a (b t)", a=2)
        fqk = sb("fqk", [P, 2, 2, T])
        fsq = sb("fsq", [P, 2, 2 * T])
        fv = sb("fv", [P, 2, 256])
        fl = sb("fl", [4, 4, T])
        sc = sb("sc", [P, FOX_HEADS, 384])
        pT = xs[:, 0:3, :, :].rearrange("p j a t -> p (j a t)")
        fst = sb("fst", [P, 4, 8])

        ps = ctx.enter_context(nc.psum_tensor("ps", [P, 8 * 512], F32))

        def bank(b, n=1):
            return ps[:, b * 512:(b + n) * 512]

        ident = con[:, 0:P]
        ones = con[:, P:2 * P]
        halves = con[:, 2 * P:3 * P]
        cmask = con[:, 3 * P:3 * P + 384]
        carry = con[:, 3 * P + 384:]

        def prm(name, a=0, n=None):
            at, size = COLS[name]
            return par[:, at + a:at + (size if n is None else a + n)]

        raw_loaded = [sem(f"raw_loaded{s}") for s in range(4)]
        consts_loaded = sem("consts_loaded")
        x_loaded = sem("x_loaded")
        par_loaded = sem("par_loaded")
        hi_written = sem("hi_written")
        lo_written = sem("lo_written")
        units_done = sem("units_done")
        direct_done = sem("direct_done")
        xg_hi_ready = sem("xg_hi_ready")
        xg_lo_ready = sem("xg_lo_ready")
        h_ready = sem("h_ready")
        sq_ready = sem("sq_ready")
        sumsq_added = sem("sumsq_added")
        sums_done = sem("sums_done")
        rstd_ready = sem("rstd_ready")
        rstd_steps = sem("rstd_steps")
        x_ready = sem("x_ready")
        acc_done = sem("acc_done")
        gate_scaled = sem("gate_scaled")
        gu_read = sem("gu_read")
        silu_done = sem("silu_done")
        act_ready = sem("act_ready")
        act_hi_ready = sem("act_hi_ready")
        act_lo_ready = sem("act_lo_ready")
        out_stored = sem("out_stored")
        mask_ready = sem("mask_ready")
        zeros_set = sem("zeros_set")
        once = sem("once")
        s5_dt = sem("s5_dt")
        s5_args = sem("s5_args")
        s5_funs = sem("s5_funs")
        s5_coef = sem("s5_coef")
        pool_step = sem("pool_step")
        tables_ready = sem("tables_ready")
        dve_step = sem("dve_step")
        proj_dve = sem("proj_dve")
        proj_act = sem("proj_act")
        bf_sig = sem("bf_sig")
        bf_f = sem("bf_f")
        bf_log = sem("bf_log")
        dec_arg = sem("dec_arg")
        dec_exp = sem("dec_exp")
        qk_ready = sem("qk_ready")
        lev_done = sem("lev_done")
        lev_read = sem("lev_read")
        attn_clear = sem("attn_clear")
        bu_done = sem("bu_done")
        bu_read = sem("bu_read")
        xin_ready = sem("xin_ready")
        scan_done = sem("scan_done")
        un_ready = sem("un_ready")
        xs_ready = sem("xs_ready")
        y_done = sem("y_done")
        y_ready = sem("y_ready")
        z_ready = sem("z_ready")
        glu_done = sem("glu_done")
        sg_ready = sem("sg_ready")
        mix_s5 = sem("mix_s5")
        fsq_ready = sem("fsq_ready")
        fsum_done = sem("fsum_done")
        frn_ready = sem("frn_ready")
        fln = sem("fln")
        fqk_ready = sem("fqk_ready")
        af_done = sem("af_done")
        af_abs = sem("af_abs")
        af_exp = sem("af_exp")
        af_ln = sem("af_ln")
        cum_ready = sem("cum_ready")
        sc_done = sem("sc_done")
        sc_read = sem("sc_read")
        max_ready = sem("max_ready")
        exp_done = sem("exp_done")
        p_ready = sem("p_ready")
        pt_done = sem("pt_done")
        pt_act = sem("pt_act")
        pt_dve = sem("pt_dve")
        fo_done = sem("fo_done")
        mix_fox = sem("mix_fox")
        o_done = sem("o_done")
        osq_ready = sem("osq_ready")
        osum_done = sem("osum_done")
        oln = sem("oln")
        orn_ready = sem("orn_ready")
        bg_ready = sem("bg_ready")
        mix_hgrn = sem("mix_hgrn")

        block = ctx.enter_context(nc.Block())

        @block.sync
        def _(sp):
            sp.dma_start(g0[:, :], gain0).then_inc(x_loaded, 16)
            sp.dma_start(x[:, :, :], xT).then_inc(x_loaded, 16)

            def load(n, slot):
                sp.dma_start(raw[slot][:, :], stream[bass.ds(n, 1), :, :].rearrange("o p c -> p (o c)")
                             ).then_inc(raw_loaded[slot], 16)

            def load_split(n, at, slot):
                sp.wait_ge(hi_written, n + 1)
                sp.wait_ge(lo_written, n + 1)
                load(at, slot)

            with sp.Fori(0, DEPTH) as l:
                for p in range(RING):
                    load_split(l * SPLIT_UNITS + p, l * UNITS + p, p)
                with sp.Fori(1, ITERS) as i:
                    for p in range(RING):
                        load_split(l * SPLIT_UNITS + i * 3 + p, l * UNITS + i * 3 + p, p)
                for w in range(IN_UNITS):
                    if w < RING:
                        sp.wait_ge(hi_written, l * SPLIT_UNITS + FFN_UNITS + w + 1)
                        sp.wait_ge(lo_written, l * SPLIT_UNITS + FFN_UNITS + w + 1)
                    else:
                        sp.wait_ge(direct_done, l * DIRECT_UNITS + w - 2)
                    load(l * UNITS + FFN_UNITS + w, w % RING)
                for w in range(OUT_UNITS):
                    if w < RING:
                        sp.wait_ge(direct_done, l * DIRECT_UNITS + IN_UNITS - RING + w + 1)
                    load(l * UNITS + FFN_UNITS + IN_UNITS + w, w)
                for p in range(RING):
                    sp.wait_ge(direct_done, l * DIRECT_UNITS + IN_UNITS + p + 1)
                    load(l * UNITS + FFN_UNITS + DIRECT_UNITS + p, p)
                with sp.Fori(1, ITERS) as i:
                    for p in range(RING):
                        load_split(l * SPLIT_UNITS + FFN_UNITS + i * 3 + p,
                                   l * UNITS + FFN_UNITS + DIRECT_UNITS + i * 3 + p, p)
            for m in range(KT):
                sp.wait_ge(x_ready, 24 * (DEPTH - 1) + 16 + m + 1)
                sp.dma_start(out[:, m, :], x[:, m, :]).then_inc(out_stored, 16)
            sp.wait_ge(out_stored, 16 * KT)

        @block.gpsimd
        def _(pool):
            pool.dma_start(con[:, :], consts).then_inc(consts_loaded, 16)
            pool.dma_start(sel[:, :], select).then_inc(consts_loaded, 16)
            pool.dma_start(trig_tmp[:, :, :], masks).then_inc(consts_loaded, 16)
            pool.memset(eps[:, :], EPS).then_inc(once, 1)
            pool.memset(tick[:, :], 0.0).then_inc(gu_read, 1)
            pool.memset(cos[:, :, 0:1], 1.0).then_inc(hi_written, RING)
            pool.memset(sin[:, :, 0:1], 0.0).then_inc(lo_written, RING)
            pool.memset(lbs[:, 7, :], 0.0).then_inc(units_done, RING)

            def sum_squares(norm, first=False):
                for m in range(1, KT):
                    pool.wait_ge(sq_ready, norm * KT + m + 1)
                    if m == 1:
                        if not first:
                            pool.wait_ge(sums_done, norm)
                        a = sq[:, 0, :]
                    else:
                        pool.wait_ge(sumsq_added, norm * 7 + m - 1)
                        a = sumsq[:, :]
                    pool.tensor_tensor(sumsq[:, :], a, sq[:, m % 4, :], ALU.add).then_inc(sumsq_added, 1)

            sum_squares(0, first=True)
            with pool.Fori(0, DEPTH) as l:
                steps = Steps(pool, pool_step, l, POOL_STEPS)
                pool.wait_ge(s5_coef, l + 1)
                n, r = 1, 0
                while n < T:
                    pc, psn = rot[:, r, 0, :], rot[:, r, 1, :]
                    wide_c = pc.unsqueeze(2).broadcast_to([P, S5_TILES, n])
                    wide_s = psn.unsqueeze(2).broadcast_to([P, S5_TILES, n])
                    tmp = trig_tmp[:, :, 0:n]
                    steps.wait()
                    pool.tensor_tensor(cos[:, :, n:2 * n], cos[:, :, 0:n], wide_c, ALU.mult)
                    pool.tensor_tensor(tmp, sin[:, :, 0:n], wide_s, ALU.mult)
                    steps.mark(pool.tensor_tensor(sin[:, :, n:2 * n], sin[:, :, 0:n], wide_c, ALU.mult))
                    steps.wait()
                    steps.mark(pool.tensor_tensor(cos[:, :, n:2 * n], cos[:, :, n:2 * n], tmp, ALU.subtract))
                    steps.wait()
                    steps.mark(pool.tensor_tensor(tmp, cos[:, :, 0:n], wide_s, ALU.mult))
                    steps.wait()
                    steps.mark(pool.tensor_tensor(sin[:, :, n:2 * n], sin[:, :, n:2 * n], tmp, ALU.add))
                    if 2 * n == T:
                        break
                    qc, qs = rot[:, 1 - r, 0, :], rot[:, 1 - r, 1, :]
                    t1 = s5s[:, 11, :]
                    steps.mark(pool.tensor_tensor(qc, pc, pc, ALU.mult))
                    pool.tensor_tensor(t1, psn, psn, ALU.mult)
                    steps.mark(pool.tensor_tensor(qs, pc, psn, ALU.mult))
                    steps.wait()
                    steps.mark(pool.tensor_tensor(qc, qc, t1, ALU.subtract))
                    steps.mark(pool.tensor_tensor(qs, qs, qs, ALU.add))
                    n, r = 2 * n, 1 - r
                cr = prm("c_re").rearrange("p (j c) -> p j c", c=32)
                ci = prm("c_im").rearrange("p (j c) -> p j c", c=32)
                kr = coef[:, 0, :].unsqueeze(2).broadcast_to([P, S5_TILES, 32])
                ki = coef[:, 1, :].unsqueeze(2).broadcast_to([P, S5_TILES, 32])
                minus_ki = coef[:, 2, :].unsqueeze(2).broadcast_to([P, S5_TILES, 32])
                o_re = c_out[:, 0, :].rearrange("p (j c) -> p j c", c=32)
                o_im = c_out[:, 1, :].rearrange("p (j c) -> p j c", c=32)
                tmp = trig_tmp[:, :, 0:32]
                tmp2 = trig_tmp[:, :, 32:64]
                steps.wait()
                pool.tensor_tensor(o_re, cr, kr, ALU.mult)
                pool.tensor_tensor(tmp, ci, ki, ALU.mult)
                pool.tensor_tensor(o_im, cr, minus_ki, ALU.mult)
                steps.mark(pool.tensor_tensor(tmp2, ci, kr, ALU.mult))
                steps.wait()
                pool.tensor_tensor(o_re, o_re, tmp, ALU.subtract)
                pool.tensor_tensor(o_im, o_im, tmp2, ALU.subtract).then_inc(tables_ready, 1)
                steps.close()

                sum_squares(l * 3 + 1)
                pool.wait_ge(sums_done, l * 3 + 2)
                none = cmask[:, P:2 * P].unsqueeze(1).broadcast_to([P, 2 * HEADS, P])
                pool.tensor_tensor(attn[:, :, :], none, none, ALU.add).then_inc(attn_clear, 1)

                def rotated(j):
                    pool.wait_ge(bu_read, l * 8 + j + 1)
                    if j >= 2:
                        pool.wait_ge(scan_done, l * 8 + j - 1)
                    pool.tensor_tensor(xin[:, j % 2, 0, :], ra[:, j % 2, 0, :], rb[:, j % 2, 1, :], ALU.add)
                    pool.tensor_tensor(xin[:, j % 2, 1, :], ra[:, j % 2, 1, :], rb[:, j % 2, 0, :], ALU.subtract
                                       ).then_inc(xin_ready, 1)

                def rotated_back(j):
                    pool.wait_ge(un_ready, l * 8 + j + 1)
                    pool.tensor_tensor(xs[:, j, 0, :], ua[:, j % 2, 0, :], ub[:, j % 2, 1, :], ALU.subtract)
                    pool.tensor_tensor(xs[:, j, 1, :], ub[:, j % 2, 0, :], ua[:, j % 2, 1, :], ALU.add
                                       ).then_inc(xs_ready, 1)

                for j in range(S5_TILES):
                    rotated(j)
                    if j >= 2:
                        rotated_back(j - 2)
                rotated_back(S5_TILES - 2)
                rotated_back(S5_TILES - 1)

                sum_squares(l * 3 + 2)
                sum_squares(l * 3 + 3)

        @block.scalar
        def _(e):
            def boundary(norm, hi_at, wait_x, gain, first=False):
                def square(m):
                    if not first or m >= 4:
                        e.wait_ge(sumsq_added, norm * 7 + (m - 4 if m > 5 else 1 if m >= 4 else 0))
                    e.activation(sq[:, m % 4, :], x[:, m, :], ACT.Square).then_inc(sq_ready, 1)

                for m in range(KT):
                    wait_x(m)
                    if hi_at is None:
                        e.activation(h[:, m, :], x[:, m, :], ACT.Copy, scale=gain[:, m:m + 1]).then_inc(h_ready, 1)
                    else:
                        e.activation(xg_hi[:, m, :], x[:, m, :], ACT.Copy, scale=gain[:, m:m + 1]
                                     ).then_inc(xg_hi_ready, 1)
                    square(m)

            def split_hi(n, visit, slot):
                e.wait_ge(raw_loaded[slot], (visit + 1) * 16)
                e.wait_ge(units_done, n + 1)
                e.activation(hi[slot][:, :], raw[slot][:, :], ACT.Copy).then_inc(hi_written, 1)

            def ffn(l, f, n0, v0, split_first, norm, rstd_step):
                if not split_first:
                    split_hi(n0, v0, 0)
                    split_hi(n0 + 1, v0, 1)
                e.wait_ge(sums_done, norm + 1)
                e.activation(ln_ms[:, :], bank(7)[:, 0:T], ACT.Ln, scale=1.0 / D, bias=eps[:, :]
                             ).then_inc(rstd_steps, 1)
                e.wait_ge(rstd_steps, rstd_step)
                e.activation(rstd[:, :], ln_ms[:, :], ACT.Exp, scale=-0.5).then_inc(rstd_ready, 1)
                split_hi(n0 + 2, v0, 2)

            def ffn_steps(f, n0, v0):
                with e.Fori(0, (ITERS - 1)) as i:
                    e.wait_ge(gate_scaled, f * ITERS + i + 1)
                    e.activation(silu[:, :, :], gate[:, :, :], ACT.Silu).then_inc(silu_done, 1)
                    split_hi(n0 + i * 3 + 3, v0 + i + 1, 0)
                    e.wait_ge(act_ready, f * ITERS + i + 1)
                    e.wait_ge(units_done, n0 + i * 3 + 2 + RING)
                    e.activation(act_hi[:, :, :], act[:, :, :], ACT.Copy).then_inc(act_hi_ready, 1)
                    split_hi(n0 + i * 3 + 4, v0 + i + 1, 1)
                    split_hi(n0 + i * 3 + 5, v0 + i + 1, 2)
                last = ITERS - 1
                e.wait_ge(gate_scaled, f * ITERS + last + 1)
                e.activation(silu[:, :, :], gate[:, :, :], ACT.Silu).then_inc(silu_done, 1)
                e.wait_ge(act_ready, f * ITERS + last + 1)
                e.wait_ge(units_done, n0 + FFN_UNITS - 1 + RING)
                e.activation(act_hi[:, :, :], act[:, :, :], ACT.Copy).then_inc(act_hi_ready, 1)

            e.wait_ge(once, 1)
            e.wait_ge(consts_loaded, 48)
            e.wait_ge(x_loaded, 32)
            boundary(0, 0, lambda m: None, g0, first=True)
            with e.Fori(0, DEPTH) as l:
                e.wait_ge(xg_lo_ready, l * 16 + 8)
                e.dma_start(par[:, :], params[bass.ds(l, 1), :, :].rearrange("o p c -> p (o c)")
                            ).then_inc(par_loaded, 16)
                ffn(l, l * 2, l * SPLIT_UNITS, l * VISITS, False, l * 3, l * 4 + 1)
                e.wait_ge(par_loaded, l * 16 + 16)
                e.activation(s5s[:, 0, :], prm("log_step"), ACT.Exp).then_inc(s5_dt, 1)
                e.wait_ge(s5_args, l * 2 + 1)
                e.activation(mag[:, :], s5s[:, 1, :], ACT.Exp).then_inc(s5_funs, 1)
                e.activation(lbs[:, 2:4, :], lbs[:, 0:2, :], ACT.Exp).then_inc(s5_funs, 1)
                e.wait_ge(s5_args, l * 2 + 2)
                e.activation(s5s[:, 4, :], s5s[:, 3, :], ACT.Sin).then_inc(s5_funs, 1)
                e.activation(s5s[:, 5, :], s5s[:, 3, :], ACT.Sin, scale=0.5).then_inc(s5_funs, 1)
                ffn_steps(l * 2, l * SPLIT_UNITS, l * VISITS)

                def wait_x1(m):
                    e.wait_ge(x_ready, l * 24 + m + 1)
                boundary(l * 3 + 1, None, wait_x1, prm("gain_mix"))
                e.wait_ge(sums_done, l * 3 + 2)
                e.activation(ln_ms[:, :], bank(7)[:, 0:T], ACT.Ln, scale=1.0 / D, bias=eps[:, :]).then_inc(rstd_steps, 1)
                e.activation(rstd_tok[:, 2:4], bank(7)[:, T:T + 2], ACT.Ln, scale=1.0 / D, bias=eps[:, :]
                             ).then_inc(rstd_steps, 1)
                e.wait_ge(rstd_steps, l * 4 + 3)
                e.activation(rstd_tok[:, 0:2], rstd_tok[:, 2:4], ACT.Exp, scale=-0.5)
                e.activation(rstd[:, :], ln_ms[:, :], ACT.Exp, scale=-0.5).then_inc(rstd_ready, 1)
                e.wait_ge(proj_dve, l * 9 + 3)
                e.activation(key[:, :, :], bf[:, :, :], ACT.Sigmoid).then_inc(bf_sig, 1)
                e.wait_ge(bf_f, l + 1)
                e.activation(bf[:, :, :], bf[:, :, :], ACT.Ln).then_inc(bf_log, 1)

                def decays(n):
                    e.wait_ge(dec_arg, l * (NSTEP - 1) + n + 1)
                    d = dec[:, n % 2, :, :]
                    ch = lambda t, c: t.rearrange("p h (c k) -> p h c k", k=CHUNK)[:, :, c, :]
                    if n == 0:
                        e.activation(d.rearrange("p h (n s k) -> p h n s k", s=2, k=CHUNK)[:, :, :, 0, :],
                                     d.rearrange("p h (n s k) -> p h n s k", s=2, k=CHUNK)[:, :, :, 0, :], ACT.Exp)
                        e.activation(d.rearrange("p h (n s k) -> p h n s k", s=2, k=CHUNK)[:, :, :, 1, :],
                                     bc[:, :, :].rearrange("p h (n s k) -> p h n s k", s=2, k=CHUNK)[:, :, :, 1, :],
                                     ACT.Exp).then_inc(dec_exp, 1)
                    elif n == NSTEP - 2:
                        e.activation(d[:, :, 0:T // 2], d[:, :, 0:T // 2], ACT.Exp)
                        e.activation(ch(d, 2), ch(bc[:, :, :], 2), ACT.Exp)
                        e.activation(ch(d, 3), ch(d, 3), ACT.Exp).then_inc(dec_exp, 1)
                    else:
                        e.activation(d, d, ACT.Exp).then_inc(dec_exp, 1)

                def values(n, dst):
                    e.wait_ge(rstd_ready, l * 3 + 2)
                    e.wait_ge(direct_done, l * DIRECT_UNITS + n + 1)
                    for t in range(2):
                        e.activation(dst(t), bank(4 + n % 2)[:, t * 256:(t + 1) * 256], ACT.Copy,
                                     scale=rstd_tok[:, t:t + 1]).then_inc(proj_act, 1)

                def fox_norm(w):
                    e.wait_ge(proj_dve, l * 9 + 6 + w)
                    e.activation(fsq[:, w, :], fqk[:, w, :, :].rearrange("p a t -> p (a t)"), ACT.Square
                                 ).then_inc(fsq_ready, 1)

                def fox_rms(w):
                    e.wait_ge(fsum_done, l * 2 + w + 1)
                    e.activation(fsq[:, w, :], bank(6 + w), ACT.Ln, scale=1.0 / FOX_DIM, bias=eps[:, :]
                                 ).then_inc(fln, 1)
                    e.wait_ge(fln, l * 2 + w + 1)
                    e.activation(fsq[:, w, :], fsq[:, w, :], ACT.Exp, scale=-0.5).then_inc(frn_ready, 1)

                decays(0)
                decays(1)
                fox_norm(0)
                decays(2)
                fox_norm(1)
                e.wait_ge(af_abs, l + 1)
                e.activation(fl[:, 1, :], fl[:, 1, :], ACT.Exp, scale=-1.0).then_inc(af_exp, 1)
                e.wait_ge(af_exp, l + 1)
                e.activation(fl[:, 1, :], fl[:, 1, :], ACT.Ln, bias=ones[0:4, 0:1]).then_inc(af_ln, 1)
                decays(3)
                values(7, lambda t: v_b[:, t, 0:256])
                fox_rms(0)
                fox_rms(1)
                decays(4)
                values(8, lambda t: v_b[:, t, 256:512])
                decays(5)
                values(9, lambda t: fv[:, t, :])
                decays(6)
                decays(7)
                e.wait_ge(max_ready, l + 1)
                for hd in range(FOX_HEADS):
                    for t in range(2):
                        part = sc[:, hd, 0:P] if t == 0 else sc[:, hd, P:384]
                        e.activation(part, part, ACT.Exp, bias=fst[:, 1, t * 4 + hd:t * 4 + hd + 1],
                                     accum_out=fst[:, 2, t * 4 + hd:t * 4 + hd + 1]).then_inc(exp_done, 1)
                e.wait_ge(o_done, l + 1)
                e.activation(osq[:, :], bank(0, 2), ACT.Square).then_inc(osq_ready, 1)
                e.wait_ge(osum_done, l + 1)
                e.activation(orn[:, :], bank(2, 2), ACT.Ln, scale=1.0 / P, bias=eps[:, :]).then_inc(oln, 1)
                e.wait_ge(oln, l + 1)
                e.activation(osq[:, :], orn[:, :], ACT.Exp, scale=-0.5).then_inc(orn_ready, 1)
                e.wait_ge(pt_done, l + 1)
                for b in range(2):
                    e.activation(pT[:, b * 512:(b + 1) * 512], bank(5 + b), ACT.Copy).then_inc(pt_act, 1)
                e.wait_ge(y_ready, l + 1)
                e.activation(z, y, ACT.Gelu_apprx_tanh).then_inc(z_ready, 1)
                e.wait_ge(proj_dve, l * 9 + 9)
                e.activation(bg[:, :, :], bg[:, :, :], ACT.Silu).then_inc(bg_ready, 1)
                e.wait_ge(fo_done, l + 1)
                e.activation(h[:, 0:2, :].rearrange("p a t -> p (a t)"), bank(4), ACT.Copy).then_inc(mix_fox, 1)
                e.wait_ge(glu_done, l + 1)
                for m in range(2):
                    last = e.activation(y[:, m, :], bank(7)[:, m * T:(m + 1) * T], ACT.Sigmoid,
                                        bias=prm("glu_b", m, 1))
                last.then_inc(sg_ready, 1)

                split_hi(l * SPLIT_UNITS + FFN_UNITS, l * VISITS + 16, 0)
                split_hi(l * SPLIT_UNITS + FFN_UNITS + 1, l * VISITS + 16, 1)

                def wait_x2(m):
                    e.wait_ge(x_ready, l * 24 + 8 + m + 1)
                boundary(l * 3 + 2, l * 2 + 1, wait_x2, prm("gain_ffn2"))
                ffn(l, l * 2 + 1, l * SPLIT_UNITS + FFN_UNITS, l * VISITS + 16, True, l * 3 + 2, l * 4 + 4)
                ffn_steps(l * 2 + 1, l * SPLIT_UNITS + FFN_UNITS, l * VISITS + 16)

                def wait_x3(m):
                    e.wait_ge(x_ready, l * 24 + 16 + m + 1)
                boundary(l * 3 + 3, l * 2 + 2, wait_x3, prm("gain_next"))

        @block.tensor
        def _(pe):
            def three(acc, w_hi, w_lo, a_hi, a_lo, start, stop):
                pe.matmul(acc, w_hi, a_hi, start=start, stop=False, skip_group_check=True)
                pe.matmul(acc, w_hi, a_lo, start=False, stop=False, skip_group_check=True)
                return pe.matmul(acc, w_lo, a_hi, start=False, stop=stop, skip_group_check=True)

            def down_acc(m):
                return bank(m // 2)[:, (m % 2) * T:(m % 2 + 1) * T]

            def row_sums(norm, tokens):
                pe.wait_ge(sumsq_added, norm * 7 + 7)
                last = pe.matmul(bank(7)[:, 0:T], ones, sumsq[:, :], start=True, stop=True)
                if tokens:
                    for t in range(2):
                        last = pe.matmul(bank(7)[:, T + t:T + t + 1], sumsq[:, t * P:(t + 1) * P], ones[:, 0:1],
                                         start=True, stop=True, skip_group_check=True)
                last.then_inc(sums_done, 1)

            def ffn(f, n0, norm):
                for k in range(KT):
                    pe.wait_ge(xg_lo_ready, f * KT + k + 1)
                    if k == 0:
                        pe.wait_ge(lo_written, n0 + 1 + RING)
                        pe.wait_ge(lo_written, n0 + 2 + RING)
                    for m in range(2):
                        for s in range(2):
                            w = k * 256 + m * P
                            last = three(bank(4 + m)[:, s * T:(s + 1) * T], hi[s][:, w:w + P], lo[s][:, w:w + P],
                                         xg_hi[:, k, :], xg_lo[:, k, :], k == 0 and s == 0, k == KT - 1)
                last.then_inc(units_done, 2)
                for b in range(4):
                    pe.matmul(bank(b), zero[:, 0:P], zero[:, :], start=True, stop=False, skip_group_check=True)
                row_sums(norm, False)

                def gate_up(half, n, slot, b, first):
                    pe.wait_ge(lo_written, n + 1 + RING)
                    for m in range(2):
                        for k in range(KT):
                            w = k * 256 + m * P
                            last = three(bank(b + m)[:, half * T:(half + 1) * T], hi[slot][:, w:w + P],
                                         lo[slot][:, w:w + P], xg_hi[:, k, :], xg_lo[:, k, :],
                                         k == 0, k == KT - 1)
                    last.then_inc(units_done, 1)

                def step(i, g, first):
                    n = n0 + i * 3 + 2
                    if first:
                        pe.wait_ge(rstd_ready, norm + 1)
                    pe.wait_ge(gu_read, f * ITERS + i + 1)
                    gate_up(0, n, 2, 4 + 2 * g, first)
                    gate_up(1, n + 1, 0, 4 + 2 * g, first)
                    pe.wait_ge(lo_written, n + 3 + RING)
                    pe.wait_ge(act_lo_ready, f * ITERS + i + 1)
                    for m in range(KT):
                        for k in range(2):
                            w = k * D + m * P
                            last = three(down_acc(m), hi[1][:, w:w + P], lo[1][:, w:w + P],
                                         act_hi[:, k, :], act_lo[:, k, :], False, False)
                    last.then_inc(units_done, 1)

                with pe.Fori(0, (ITERS - 1) // 2) as ii:
                    step(ii * 2, 1, True)
                    step(ii * 2 + 1, 0, False)
                pe.wait_ge(lo_written, n0 + FFN_UNITS + RING)
                pe.wait_ge(act_lo_ready, f * ITERS + ITERS)
                for m in range(KT):
                    for k in range(2):
                        w = k * D + m * P
                        last = three(down_acc(m), hi[2][:, w:w + P], lo[2][:, w:w + P],
                                     act_hi[:, k, :], act_lo[:, k, :], False, k == 1)
                    if m % 2 == 1 and m < KT - 1:
                        last.then_inc(acc_done, 1)
                last.then_inc(units_done, 1)

            pe.wait_ge(consts_loaded, 48)
            pe.wait_ge(zeros_set, 1)
            with pe.Fori(0, DEPTH) as l:
                ffn(l * 2, l * SPLIT_UNITS, l * 3)

                dve_units = [0, 1, 2, 3, 4, 5, 6, 10, 11]

                def unit_ready(n):
                    pe.wait_ge(raw_loaded[n % RING], (l * VISITS + ITERS + n // RING + 1) * 16)
                    if n - 2 in dve_units:
                        pe.wait_ge(proj_dve, l * 9 + dve_units.index(n - 2) + 1)
                    elif n >= 2:
                        pe.wait_ge(proj_act, l * 6 + (n - 2 - 7) * 2 + 2)

                def project(n):
                    unit_ready(n)
                    b, w = bank(4 + n % 2), raw[n % RING]
                    for k in range(KT):
                        if n == 0:
                            pe.wait_ge(h_ready, l * KT + k + 1)
                        for m in range(2):
                            last = pe.matmul(b[:, m * T:(m + 1) * T], w[:, k * 256 + m * P:k * 256 + m * P + P],
                                             h[:, k, :], start=k == 0 and m == 0, stop=k == KT - 1,
                                             skip_group_check=True)
                    last.then_inc(direct_done, 1)

                def project_tokens(n):
                    unit_ready(n)
                    b, w = bank(4 + n % 2), raw[n % RING]
                    for t in range(2):
                        for k in range(KT):
                            last = pe.matmul(b[:, t * 256:(t + 1) * 256], h[:, k, t * P:(t + 1) * P],
                                             w[:, k * 256:(k + 1) * 256], start=k == 0, stop=k == KT - 1,
                                             skip_group_check=True)
                    last.then_inc(direct_done, 1)

                def input_matrix(j):
                    if j == 0:
                        pe.wait_ge(proj_dve, l * 9 + 1)
                    if j == 1:
                        pe.wait_ge(rstd_ready, l * 3 + 2)
                    if j >= 2:
                        pe.wait_ge(bu_read, l * 8 + j - 1)
                    r = 32 * (j % 4)
                    for part, name in enumerate(("b_re", "b_im")):
                        last = pe.matmul(bank(6 + j % 2)[:, part * T:(part + 1) * T],
                                         prm(name)[r:r + 32, (j // 4) * P:(j // 4 + 1) * P],
                                         u[r:r + 32, j // 4, :], start=True, stop=True, skip_group_check=True)
                    last.then_inc(bu_done, 1)

                def level(n):
                    b = bank(2 * (n % 2), 2)
                    if n < NLEV - 1 or n == NSTEP - 1:
                        pe.wait_ge(qk_ready, l * (NSTEP - 1) + (n if n < NLEV - 1 else n - 1) + 1)
                    if n >= 2:
                        pe.wait_ge(lev_read, l * NSTEP + n - 1)
                    if n == NSTEP - 1:
                        q = qk[:, (n - 1) % 2, :, :]
                        for hd in range(HEADS):
                            last = pe.matmul(b[:, hd * P:(hd + 1) * P], q[:, hd, 0:P], q[:, hd, P:T],
                                             start=True, stop=True, skip_group_check=True)
                    else:
                        for hd in range(HEADS):
                            for t in range(2):
                                i = hd * 2 + t
                                tok = slice(t * P, (t + 1) * P)
                                if n == NLEV - 1:
                                    a, c = key[:, hd, tok], bq[:, hd, tok]
                                else:
                                    a = c = qk[:, n % 2, hd, tok]
                                last = pe.matmul(b[:, i * P:(i + 1) * P], a, c, start=True, stop=True,
                                                 skip_group_check=True)
                    last.then_inc(lev_done, 1)

                def fox_sums(w):
                    pe.wait_ge(fsq_ready, l * 2 + w + 1)
                    if w == 0:
                        pe.wait_ge(bu_read, l * 8 + 7)
                    else:
                        pe.wait_ge(af_abs, l + 1)
                    pe.matmul(bank(6 + w), halves, fsq[:, w, :], start=True, stop=True).then_inc(fsum_done, 1)

                project(0)
                row_sums(l * 3 + 1, True)
                project(1)
                input_matrix(0)
                input_matrix(1)
                project(2)
                input_matrix(2)
                input_matrix(3)
                project(3)
                input_matrix(4)
                input_matrix(5)
                project(4)
                input_matrix(6)
                input_matrix(7)
                project(5)
                level(0)
                project(6)
                pe.wait_ge(bu_read, l * 8 + 8)
                for k in range(KT):
                    last = pe.matmul(bank(7)[0:4, 0:T], prm("w_forget", k * 4, 4), h[:, k, :],
                                     start=k == 0, stop=k == KT - 1)
                last.then_inc(af_done, 1)
                level(1)
                project_tokens(7)
                fox_sums(0)
                fox_sums(1)
                level(2)
                project_tokens(8)
                level(3)
                project_tokens(9)
                level(4)
                project(10)
                level(5)
                project(11)
                level(6)
                level(7)
                level(8)

                pe.wait_ge(xs_ready, l * 8 + 8)
                pe.wait_ge(tables_ready, l + 1)
                pe.wait_ge(proj_dve, l * 9 + 9)
                for j in range(S5_TILES):
                    r, c = 32 * (j % 4), j // 4
                    for part in range(2):
                        last = pe.matmul(bank(5)[r:r + 32, c * T:(c + 1) * T], c_out[:, part, j * 32:(j + 1) * 32],
                                         xs[:, j, part, :], start=part == 0, stop=part == 1, skip_group_check=True)
                last.then_inc(y_done, 1)

                pe.wait_ge(y_ready, l + 1)
                pe.wait_ge(fqk_ready, l * 2 + 2)
                pe.wait_ge(cum_ready, l + 1)
                pe.wait_ge(frn_ready, l * 2 + 2)
                for t in range(2):
                    for hd in range(FOX_HEADS):
                        n = (t + 1) * P
                        b = bank((6 if t == 0 else 4) + hd % 2)
                        at = (hd // 2) * n
                        r, tile, tok = 64 * (hd % 2), hd // 2, slice(t * P, (t + 1) * P)
                        dst = b[:, at:at + n]
                        pe.matmul(dst, fqk[r:r + 64, 0, tile, tok], fqk[r:r + 64, 1, tile, 0:n],
                                  start=True, stop=False, skip_group_check=True)
                        pe.matmul(dst, fl[:, 2, tok], sel[:, hd * T:hd * T + n], start=False, stop=False,
                                  skip_group_check=True)
                        last = pe.matmul(dst, sel[:, hd * T:hd * T + P], fl[:, 3, 0:n], start=False, stop=True,
                                         skip_group_check=True)
                last.then_inc(sc_done, 1)

                pe.wait_ge(lev_read, l * NSTEP + NSTEP)
                pe.wait_ge(proj_act, l * 6 + 4)
                for hd in range(HEADS):
                    at = hd * T
                    w = slice(hd * P, (hd + 1) * P)
                    o = bank(0, 2)
                    pe.matmul(o[:, at:at + P], v_b[:, 0, w], attn[:, hd * 2, :], start=True, stop=True,
                              skip_group_check=True)
                    pe.matmul(o[:, at + P:at + T], v_b[:, 0, w], attn_x[:, hd, :], start=True, stop=False,
                              skip_group_check=True)
                    last = pe.matmul(o[:, at + P:at + T], v_b[:, 1, w], attn[:, hd * 2 + 1, :], start=False,
                                     stop=True, skip_group_check=True)
                last.then_inc(o_done, 1)
                pe.wait_ge(osq_ready, l + 1)
                for b in range(2):
                    last = pe.matmul(bank(2 + b), ones, osq[:, b * 512:(b + 1) * 512], start=True, stop=True)
                last.then_inc(osum_done, 1)

                pe.wait_ge(p_ready, l + 1)
                for i in range(12):
                    last = pe.transpose(ps[:, 5 * 512 + i * P:5 * 512 + (i + 1) * P],
                                        sc[:, i // 3, (i % 3) * P:(i % 3 + 1) * P], ident)
                last.then_inc(pt_done, 1)
                pe.wait_ge(pt_act, l * 2 + 2)
                pe.wait_ge(pt_dve, l + 1)
                pe.wait_ge(proj_act, l * 6 + 6)
                for hd in range(FOX_HEADS):
                    r, c = 64 * (hd % 2), (hd // 2) * T
                    w = slice(hd * FOX_DIM, (hd + 1) * FOX_DIM)
                    part = lambda i: pT[:, hd * 384 + i * P:hd * 384 + (i + 1) * P]
                    pe.matmul(bank(4)[r:r + 64, c:c + P], fv[:, 0, w], part(0), start=True, stop=True,
                              skip_group_check=True)
                    pe.matmul(bank(4)[r:r + 64, c + P:c + T], fv[:, 0, w], part(1), start=True, stop=False,
                              skip_group_check=True)
                    last = pe.matmul(bank(4)[r:r + 64, c + P:c + T], fv[:, 1, w], part(2), start=False, stop=True,
                                     skip_group_check=True)
                last.then_inc(fo_done, 1)

                pe.wait_ge(z_ready, l + 1)
                for m in range(2):
                    for k in range(2):
                        last = pe.matmul(bank(7)[:, m * T:(m + 1) * T], prm("glu_w", k * T + m * P, P), z[:, k, :],
                                         start=k == 0, stop=k == 1, skip_group_check=True)
                last.then_inc(glu_done, 1)

                pe.wait_ge(mix_hgrn, l + 1)
                pe.wait_ge(mix_fox, l + 1)
                pe.wait_ge(mix_s5, l + 1)
                for n in range(OUT_UNITS):
                    if n < RING:
                        pe.wait_ge(raw_loaded[n], (l * VISITS + ITERS + 4 + 1) * 16)
                    else:
                        pe.wait_ge(raw_loaded[3], (l + 1) * 16)
                    for k in range(KT):
                        for m in range(2):
                            last = pe.matmul(bank(n)[:, m * T:(m + 1) * T],
                                             raw[n][:, k * 256 + m * P:k * 256 + m * P + P], h[:, k, :],
                                             start=k == 0 and m == 0, stop=k == KT - 1, skip_group_check=True)
                    last.then_inc(direct_done, 1)

                ffn(l * 2 + 1, l * SPLIT_UNITS + FFN_UNITS, l * 3 + 2)

        @block.vector
        def _(v):
            def acc(m):
                return bank(m // 2)[:, (m % 2) * T:(m % 2 + 1) * T]

            def split_lo(n, slot):
                v.wait_ge(hi_written, n + 1 + RING)
                v.tensor_tensor(lo[slot][:, :], raw[slot][:, :], hi[slot][:, :].bitcast(F32), ALU.subtract
                                ).then_inc(lo_written, 1)

            def rest_of_x(f, m, gain):
                v.wait_ge(xg_hi_ready, f * KT + m + 1)
                v.scalar_tensor_tensor(xg_lo[:, m, :], x[:, m, :], gain[:, m:m + 1], xg_hi[:, m, :].bitcast(F32),
                                       ALU.mult, ALU.subtract).then_inc(xg_lo_ready, 1)

            def boundary(wait_acc, scale, f, gain):
                for m in range(KT):
                    wait_acc(m)
                    v.scalar_tensor_tensor(x[:, m, :], acc(m), scale, x[:, m, :], ALU.mult, ALU.add
                                           ).then_inc(x_ready, 1)
                    if f is not None and m >= 1:
                        rest_of_x(f, m - 1, gain)
                if f is not None:
                    rest_of_x(f, KT - 1, gain)

            def gated(f, i, g, n_up, before_act, after_act):
                both = bank(4 + 2 * g, 2).rearrange("p (m s t) -> p m s t", m=2, s=2)
                wide = rstd[:, :].unsqueeze(1).broadcast_to([P, 2, T])
                v.wait_ge(units_done, n_up + 1 + RING)
                v.tensor_tensor(gate[:, :, :], both[:, :, 0, :], wide, ALU.mult).then_inc(gate_scaled, 1)
                v.tensor_tensor(up[:, :, :], both[:, :, 1, :], wide, ALU.mult).then_inc(gu_read, 1)
                before_act()
                v.wait_ge(silu_done, f * ITERS + i + 1)
                v.wait_ge(gu_read, f * ITERS + i + 2)
                v.tensor_tensor(act[:, :, :], silu[:, :, :], up[:, :, :], ALU.mult).then_inc(act_ready, 1)
                after_act()
                v.wait_ge(act_hi_ready, f * ITERS + i + 1)
                v.tensor_tensor(act_lo[:, :, :], act[:, :, :], act_hi[:, :, :].bitcast(F32), ALU.subtract
                                ).then_inc(act_lo_ready, 1)

            def ffn_steps(f, n0):
                with v.Fori(0, (ITERS - 1) // 2) as ii:
                    for g in range(2):
                        i = ii * 2 + g
                        n = n0 + i * 3
                        gated(f, i, g, n, lambda: split_lo(n + 3, 0), lambda: split_lo(n + 4, 1))
                        split_lo(n + 5, 2)
                gated(f, ITERS - 1, 0, n0 + FFN_UNITS - 3, lambda: None, lambda: None)

            v.memset(zero[:, :].bitcast(F32), 0.0).then_inc(zeros_set, 1)
            v.wait_ge(consts_loaded, 48)
            v.tensor_copy(mask[:, :], trig_tmp[:, :, :].rearrange("p j t -> p (j t)")).then_inc(mask_ready, 1)
            v.wait_ge(mask_ready, 1)
            v.wait_ge(x_loaded, 32)
            for m in range(KT):
                rest_of_x(0, m, g0)
            with v.Fori(0, DEPTH) as l:
                split_lo(l * SPLIT_UNITS, 0)
                split_lo(l * SPLIT_UNITS + 1, 1)
                split_lo(l * SPLIT_UNITS + 2, 2)
                st = Steps(v, dve_step, l, DVE_STEPS)

                lr, li = prm("lam_re"), prm("lam_im")
                tiny = lambda i: s5s[:, i, :]
                v.wait_ge(par_loaded, l * 16 + 16)
                lg = prm("lb_logit").rearrange("p (d h) -> p d h", d=2)
                st.mark(v.tensor_tensor(lbs[:, 4, :], lg[:, 0, :], lg[:, 1, :], ALU.max))
                st.wait()
                st.mark(v.tensor_tensor(lbs[:, 0:2, :], lg, lbs[:, 4:5, :].broadcast_to([P, 2, HEADS]), ALU.subtract))
                v.wait_ge(s5_dt, l + 1)
                v.tensor_tensor(tiny(2), li, tiny(0), ALU.mult)
                st.wait()
                v.tensor_tensor(tiny(1), lr, tiny(0), ALU.mult).then_inc(s5_args, 1)
                v.wait_ge(s5_args, l * 2 + 1)
                st.mark(v.tensor_scalar(tiny(6), tiny(2), 1.0 / TWO_PI, ROUND, ALU.mult, ALU.add))
                st.wait()
                st.mark(v.tensor_scalar(tiny(6), tiny(6), ROUND, None, ALU.subtract))
                for c in (PI_A, PI_B, PI_C):
                    st.wait()
                    st.mark(v.scalar_tensor_tensor(tiny(2), tiny(6), -c, tiny(2), ALU.mult, ALU.add))
                st.wait()
                v.tensor_scalar(tiny(3), tiny(2), 3.1415925, -3.1415925, ALU.min, ALU.max).then_inc(s5_args, 1)
                v.wait_ge(s5_funs, l * 4 + 2)
                st.mark(v.tensor_tensor(lbs[:, 4, :], lbs[:, 2, :], lbs[:, 3, :], ALU.add))
                st.wait()
                st.mark(v.reciprocal(lbs[:, 4, :], lbs[:, 4, :]))
                st.wait()
                st.mark(v.tensor_tensor(lbs[:, 2, :], lbs[:, 2, :], lbs[:, 4, :], ALU.mult))
                st.mark(v.tensor_tensor(lbs[:, 3, :], lbs[:, 3, :], lbs[:, 4, :], ALU.mult))
                st.wait()
                st.mark(v.tensor_tensor(lbs[:, 5, :], lbs[:, 2, :], lbs[:, 3, :], ALU.add))
                st.wait()
                st.mark(v.tensor_tensor(lbs[:, 5, :], lbs[:, 5, :], lbs[:, 2, :], ALU.subtract))
                st.wait()
                st.mark(v.tensor_scalar(lbs[:, 5, :], lbs[:, 5, :], prm("later_layer"), None, ALU.mult))
                st.wait()
                st.mark(v.tensor_scalar(lbs[:, 6, :], lbs[:, 5, :], -1.0, 1.0, ALU.mult, ALU.add))
                v.wait_ge(s5_funs, l * 4 + 4)
                st.mark(v.tensor_tensor(tiny(6), tiny(5), tiny(5), ALU.mult))
                v.wait_ge(rstd_ready, l * 3 + 1)
                st.mark(v.tensor_copy(rot[:, 0, 1, :], tiny(4)))
                st.wait()
                st.mark(v.tensor_scalar(rot[:, 0, 0, :], tiny(6), -2.0, 1.0, ALU.mult, ALU.add))
                st.wait()
                st.mark(v.tensor_tensor(tiny(7), mag[:, :], rot[:, 0, 0, :], ALU.mult))
                st.mark(v.tensor_tensor(tiny(8), mag[:, :], tiny(4), ALU.mult))
                st.mark(v.tensor_tensor(tiny(9), lr, lr, ALU.mult))
                st.mark(v.tensor_tensor(tiny(10), li, li, ALU.mult))
                st.wait()
                st.mark(v.tensor_scalar(tiny(7), tiny(7), -1.0, None, ALU.add))
                st.mark(v.tensor_tensor(tiny(9), tiny(9), tiny(10), ALU.add))
                st.wait()
                st.mark(v.reciprocal(tiny(9), tiny(9)))
                st.mark(v.tensor_tensor(tiny(0), tiny(7), lr, ALU.mult))
                st.mark(v.tensor_tensor(tiny(1), tiny(8), li, ALU.mult))
                st.mark(v.tensor_tensor(tiny(10), tiny(8), lr, ALU.mult))
                st.mark(v.tensor_tensor(tiny(6), tiny(7), li, ALU.mult))
                st.wait()
                st.mark(v.tensor_tensor(tiny(0), tiny(0), tiny(1), ALU.add))
                st.mark(v.tensor_tensor(tiny(10), tiny(10), tiny(6), ALU.subtract))
                st.wait()
                st.mark(v.tensor_tensor(coef[:, 0, :], tiny(0), tiny(9), ALU.mult))
                st.mark(v.tensor_tensor(coef[:, 1, :], tiny(10), tiny(9), ALU.mult))
                st.wait()
                v.tensor_scalar(coef[:, 2, :], coef[:, 1, :], -1.0, None, ALU.mult).then_inc(s5_coef, 1)

                ffn_steps(l * 2, l * SPLIT_UNITS)

                def wait_ffn1(m):
                    if m < KT - 2:
                        v.wait_ge(acc_done, l * 6 + m // 2 + 1)
                    else:
                        v.wait_ge(units_done, l * SPLIT_UNITS + FFN_UNITS + RING)
                boundary(wait_ffn1, 0.5, None, None)

                wide = rstd[:, :].unsqueeze(1).broadcast_to([P, 2, T])

                def take(n, dst):
                    v.wait_ge(direct_done, l * DIRECT_UNITS + n + 1)
                    v.tensor_tensor(dst, bank(4 + n % 2).rearrange("p (m t) -> p m t", m=2), wide, ALU.mult
                                    ).then_inc(proj_dve, 1)

                def rotate(j):
                    v.wait_ge(bu_done, l * 8 + j + 1)
                    if j == 0:
                        v.wait_ge(tables_ready, l + 1)
                    if j >= 2:
                        v.wait_ge(xin_ready, l * 8 + j - 1)
                    b = bank(6 + j % 2).rearrange("p (a t) -> p a t", a=2)
                    c = cos[:, j:j + 1, :].broadcast_to([P, 2, T])
                    s = sin[:, j:j + 1, :].broadcast_to([P, 2, T])
                    v.tensor_tensor(ra[:, j % 2, :, :], b, c, ALU.mult)
                    v.tensor_tensor(rb[:, j % 2, :, :], b, s, ALU.mult).then_inc(bu_read, 1)

                def scan(j):
                    v.wait_ge(xin_ready, l * 8 + j + 1)
                    decay = mag[:, j:j + 1].broadcast_to([P, T])
                    v.tensor_tensor_scan(xt[:, j % 2, 0, :], decay, xin[:, j % 2, 0, :], 0.0, ALU.mult, ALU.add)
                    v.tensor_tensor_scan(xt[:, j % 2, 1, :], decay, xin[:, j % 2, 1, :], 0.0, ALU.mult, ALU.add
                                         ).then_inc(scan_done, 1)
                    v.wait_ge(scan_done, l * 8 + j + 1)
                    if j >= 2:
                        v.wait_ge(xs_ready, l * 8 + j - 1)
                    c = cos[:, j:j + 1, :].broadcast_to([P, 2, T])
                    s = sin[:, j:j + 1, :].broadcast_to([P, 2, T])
                    v.tensor_tensor(ua[:, j % 2, :, :], xt[:, j % 2, :, :], c, ALU.mult)
                    v.tensor_tensor(ub[:, j % 2, :, :], xt[:, j % 2, :, :], s, ALU.mult).then_inc(un_ready, 1)

                def split2(t, size):
                    return t.rearrange("p h (n s k) -> p (h n) s k", s=2, k=size)

                def exponents(n):
                    if n >= 2:
                        v.wait_ge(qk_ready, l * (NSTEP - 1) + n - 1)
                    d = dec[:, n % 2, :, :]
                    b = bc[:, :, :]
                    if n == NSTEP - 2:
                        chunk = lambda t, c: t[:, :, c * CHUNK:(c + 1) * CHUNK]
                        end = lambda c: b[:, :, (c + 1) * CHUNK - 1:(c + 1) * CHUNK].broadcast_to([P, HEADS, CHUNK])
                        v.tensor_tensor(chunk(d, 0), bsum[:, :].unsqueeze(2).broadcast_to([P, HEADS, CHUNK]),
                                        chunk(b, 0), ALU.subtract)
                        v.tensor_tensor(chunk(d, 1), end(1), chunk(b, 1), ALU.subtract)
                        v.tensor_tensor(chunk(d, 3), chunk(b, 3), end(2), ALU.add).then_inc(dec_arg, 1)
                        return
                    size = LEVELS[n]
                    dv, bv = split2(d, size), split2(b, size)
                    ref = bv[:, :, 0, size - 1:size].broadcast_to([P, HEADS * T // (2 * size), size])
                    first = v.tensor_tensor(dv[:, :, 0, :], ref, bv[:, :, 0, :], ALU.subtract)
                    if size < CHUNK:
                        first = v.tensor_tensor(dv[:, :, 1, :], bv[:, :, 1, :], ref, ALU.subtract)
                    first.then_inc(dec_arg, 1)

                def operands(n):
                    v.wait_ge(dec_exp, l * (NSTEP - 1) + n + 1)
                    if n >= 2:
                        v.wait_ge(lev_done, l * NSTEP + n - 1)
                    d, o = dec[:, n % 2, :, :], qk[:, n % 2, :, :]
                    size = P if n == NSTEP - 2 else LEVELS[n]
                    v.tensor_tensor(split2(o, size)[:, :, 0, :], split2(key[:, :, :], size)[:, :, 0, :],
                                    split2(d, size)[:, :, 0, :], ALU.mult)
                    v.tensor_tensor(split2(o, size)[:, :, 1, :], split2(bq[:, :, :], size)[:, :, 1, :],
                                    split2(d, size)[:, :, 1, :], ALU.mult).then_inc(qk_ready, 1)

                def scores(n):
                    v.wait_ge(lev_done, l * NSTEP + n + 1)
                    if n == 0:
                        v.wait_ge(attn_clear, l + 1)
                    if n == NSTEP - 1:
                        v.tensor_copy(attn_x[:, :, :].rearrange("p h t -> p (h t)"), bank(2 * (n % 2))
                                      ).then_inc(lev_read, 1)
                        return
                    if n >= 1:
                        v.wait_ge(lev_read, l * NSTEP + n)
                    v.memset(tick[:, :], 0.0)
                    m = mask[:, n * P:(n + 1) * P].unsqueeze(1).broadcast_to([P, 2 * HEADS, P])
                    v.copy_predicated(attn[:, :, :], m, bank(2 * (n % 2), 2).rearrange("p (i t) -> p i t", t=P)
                                      ).then_inc(lev_read, 1)

                v.wait_ge(rstd_ready, l * 3 + 2)
                take(0, u[:, :, :])
                take(1, bf[:, 0:2, :])
                rotate(0)
                rotate(1)
                take(2, bf[:, 2:4, :])
                rotate(2)
                rotate(3)
                scan(0)
                v.wait_ge(bf_sig, l + 1)
                for hd in range(HEADS):
                    st.mark(v.tensor_scalar(bf[:, hd, :], key[:, hd, :], lbs[:, 6, hd:hd + 1], lbs[:, 5, hd:hd + 1],
                                            ALU.mult, ALU.add))
                st.wait()
                st.mark(v.tensor_scalar(key[:, :, :], bf[:, :, :], -1.0, 1.0, ALU.mult, ALU.add))
                st.wait()
                v.tensor_scalar(bf[:, :, :], bf[:, :, :], 2.0 ** -63, None, ALU.max).then_inc(bf_f, 1)
                scan(1)
                take(3, bq[:, 0:2, :])
                rotate(4)
                v.wait_ge(bf_log, l + 1)
                st.mark(v.tensor_tensor_scan(bc[:, :, :].rearrange("p h t -> p (h t)"), carry,
                                             bf[:, :, :].rearrange("p h t -> p (h t)"), 0.0, ALU.mult, ALU.add))
                rotate(5)
                st.wait()
                st.mark(v.tensor_tensor(bsum[:, :].unsqueeze(2), bc[:, :, CHUNK - 1:CHUNK],
                                        bc[:, :, 2 * CHUNK - 1:2 * CHUNK], ALU.add))
                scan(2)
                take(4, bq[:, 2:4, :])
                st.wait()
                exponents(0)
                exponents(1)
                rotate(6)
                scan(3)
                rotate(7)
                v.wait_ge(bf_f, l + 1)
                v.wait_ge(proj_dve, l * 9 + 5)
                operands(0)
                take(5, fqk[:, 0, :, :])
                operands(1)
                exponents(2)
                scores(0)
                scan(4)
                take(6, fqk[:, 1, :, :])
                v.wait_ge(af_done, l + 1)
                st.mark(v.tensor_tensor(fl[:, 0, :], bank(7)[0:4, 0:T], rstd[0:4, :], ALU.mult))
                st.wait()
                st.mark(v.tensor_scalar(fl[:, 0, :], fl[:, 0, :], prm("f_bias")[0:4, :], None, ALU.add))
                st.wait()
                st.mark(v.tensor_scalar(fl[:, 1, :], fl[:, 0, :], -1.0, None, ALU.mult))
                st.wait()
                v.tensor_tensor(fl[:, 1, :], fl[:, 1, :], fl[:, 0, :], ALU.max).then_inc(af_abs, 1)
                operands(2)
                exponents(3)
                scores(1)
                scan(5)
                v.wait_ge(af_ln, l + 1)
                st.mark(v.tensor_scalar(fl[:, 0, :], fl[:, 0, :], 0.0, None, ALU.min))
                st.wait()
                st.mark(v.tensor_tensor(fl[:, 0, :], fl[:, 0, :], fl[:, 1, :], ALU.subtract))
                st.wait()
                st.mark(v.tensor_tensor_scan(fl[:, 2, :], ones[0:4, 0:1].broadcast_to([4, T]), fl[:, 0, :], 0.0, ALU.mult, ALU.add))
                st.wait()
                v.tensor_scalar(fl[:, 3, :], fl[:, 2, :], -1.0, None, ALU.mult).then_inc(cum_ready, 1)
                operands(3)
                exponents(4)
                scores(2)
                scan(6)
                st.mark(v.tensor_scalar(fst[:, 0, 0:1], prm("q_gain"), FOX_DIM ** -0.5, None, ALU.mult))
                st.wait()
                for w in range(2):
                    v.wait_ge(frn_ready, l * 2 + w + 1)
                    t = fqk[:, w, :, :].rearrange("p a t -> p (a t)")
                    v.scalar_tensor_tensor(t, t, fst[:, 0, 0:1] if w == 0 else prm("k_gain"), fsq[:, w, :],
                                           ALU.mult, ALU.mult).then_inc(fqk_ready, 1)
                operands(4)
                exponents(5)
                scores(3)
                scan(7)
                operands(5)
                exponents(6)
                scores(4)
                take(10, bg[:, 0:2, :])
                operands(6)
                exponents(7)
                scores(5)
                take(11, bg[:, 2:4, :])
                scores(6)
                operands(7)
                scores(7)
                scores(8)
                v.wait_ge(y_done, l + 1)
                for m in range(2):
                    last = v.scalar_tensor_tensor(y[:, m, :], u[:, m, :], prm("skip", m, 1),
                                                  bank(5)[:, m * T:(m + 1) * T], ALU.mult, ALU.add)
                last.then_inc(y_ready, 1)
                v.wait_ge(sc_done, l + 1)
                for odd in range(2):
                    for n, at, b in ((P, 0, 6), (T, P, 4)):
                        st.mark(v.tensor_tensor(sc[:, odd:4:2, at:at + n],
                                                bank(b + odd)[:, 0:2 * n].rearrange("p (h s) -> p h s", h=2),
                                                cmask[:, at:at + n].unsqueeze(1).broadcast_to([P, 2, n]), ALU.add))
                st.wait()
                st.mark(v.tensor_reduce(fst[:, 0, 0:4], sc[:, :, 0:P], AX.X, ALU.max))
                st.mark(v.tensor_reduce(fst[:, 0, 4:8], sc[:, :, P:384], AX.X, ALU.max))
                st.wait()
                v.tensor_scalar(fst[:, 1, :], fst[:, 0, :], -1.0, None, ALU.mult).then_inc(max_ready, 1)
                v.wait_ge(exp_done, l * 8 + 8)
                st.mark(v.reciprocal(fst[:, 3, :], fst[:, 2, :]))
                st.wait()
                v.tensor_tensor(sc[:, :, 0:P], sc[:, :, 0:P],
                                fst[:, 3, 0:4].unsqueeze(2).broadcast_to([P, 4, P]), ALU.mult)
                v.tensor_tensor(sc[:, :, P:384], sc[:, :, P:384],
                                fst[:, 3, 4:8].unsqueeze(2).broadcast_to([P, 4, T]), ALU.mult).then_inc(p_ready, 1)
                v.wait_ge(pt_done, l + 1)
                v.tensor_copy(pT[:, 1024:1536], bank(7)).then_inc(pt_dve, 1)
                v.wait_ge(orn_ready, l + 1)
                st.mark(v.tensor_tensor(orn[:, :], bank(0, 2), osq[:, :], ALU.mult))
                v.wait_ge(bg_ready, l + 1)
                st.wait()
                for hd in range(HEADS):
                    last = v.scalar_tensor_tensor(h[:, 2 + hd, :], orn[:, hd * T:(hd + 1) * T], prm("o_gain", hd, 1),
                                                  bg[:, hd, :], ALU.mult, ALU.mult)
                last.then_inc(mix_hgrn, 1)
                v.wait_ge(sg_ready, l + 1)
                v.tensor_tensor(h[:, 6:8, :], z, y, ALU.mult).then_inc(mix_s5, 1)
                st.close()

                split_lo(l * SPLIT_UNITS + FFN_UNITS, 0)
                split_lo(l * SPLIT_UNITS + FFN_UNITS + 1, 1)

                def wait_out(m):
                    if m % 2 == 0:
                        v.wait_ge(direct_done, l * DIRECT_UNITS + IN_UNITS + m // 2 + 1)
                boundary(wait_out, 1.0, l * 2 + 1, prm("gain_ffn2"))
                v.wait_ge(rstd_ready, l * 3 + 3)
                split_lo(l * SPLIT_UNITS + FFN_UNITS + 2, 2)
                ffn_steps(l * 2 + 1, l * SPLIT_UNITS + FFN_UNITS)

                def wait_ffn2(m):
                    if m < KT - 2:
                        v.wait_ge(acc_done, l * 6 + 3 + m // 2 + 1)
                    else:
                        v.wait_ge(units_done, l * SPLIT_UNITS + 2 * FFN_UNITS + RING)
                boundary(wait_ffn2, 0.5, l * 2 + 2, prm("gain_next"))


def _tiles(w, cols):
    k = w.shape[0] // P
    return w.reshape(k, P, cols // 256, 256).transpose(2, 1, 0, 3).reshape(cols // 256, P, k * 256)


def _unit_stream(inputs, l):
    def ffn(name):
        g = _tiles(inputs[name + "_w_gate"][l], FF)
        u = _tiles(inputs[name + "_w_up"][l], FF)
        d = inputs[name + "_w_down"][l].reshape(ITERS, 2, P, D).transpose(0, 2, 1, 3).reshape(ITERS, P, 2 * D)
        order = [g[0], u[0]]
        for i in range(1, ITERS):
            order += [g[i], u[i], d[i - 1]]
        return order + [d[ITERS - 1]]

    w = inputs["w_in"][l]
    a = FOX_HEADS * FOX_DIM
    b = 3 * a + FOX_HEADS
    parts = {"q": w[:, 0:a], "k": w[:, a:2 * a], "v": w[:, 2 * a:3 * a], "bq": w[:, b:b + 512],
             "bf": w[:, b + 512:b + 1024], "bi": w[:, b + 1024:b + 1536], "bg": w[:, b + 1536:b + 2048],
             "u": w[:, b + 2048:b + 2304]}
    cols = np.concatenate([parts[n] for n in ("u", "bf", "bq", "q", "k", "bi", "v", "bg")], axis=1)
    w_in = list(_tiles(cols, IN_UNITS * 256))
    w_out = list(_tiles(inputs["w_out"][l], D))
    return ffn("ffn1") + w_in + w_out + ffn("ffn2")


def _params(inputs, l):
    par = np.zeros((P, NPAR), np.float32)

    def put(name, a):
        at, n = COLS[name]
        par[:a.shape[0], at:at + n] = a

    def cols(v):
        return v.reshape(-1, P).T

    put("gain_mix", cols(inputs["mix_norm"][l]))
    put("gain_ffn2", cols(inputs["ffn2_norm"][l]))
    put("gain_next", cols(inputs["ffn1_norm"][(l + 1) % DEPTH]))
    put("lam_re", cols(inputs["s5_lambda_re"][l].reshape(-1)))
    put("lam_im", cols(inputs["s5_lambda_im"][l].reshape(-1)))
    put("log_step", cols(np.repeat(inputs["s5_log_step"][l], STATE)))
    put("lb_logit", np.concatenate([cols(inputs["hgrn_lb"][d]) for d in range(DEPTH)], axis=1))
    put("later_layer", np.full((P, 1), 1.0 if l else 0.0, np.float32))
    put("o_gain", cols(inputs["hgrn_o_gain"][l]))
    put("skip", cols(inputs["s5_D"][l]))
    put("glu_b", cols(inputs["s5_glu_b"][l]))
    put("q_gain", np.tile(inputs["fox_q_gain"][l], 2)[:, None])
    put("k_gain", np.tile(inputs["fox_k_gain"][l], 2)[:, None])
    put("f_bias", inputs["fox_f_bias"][l][:, None])
    forget = inputs["w_in"][l][:, 3 * 256:3 * 256 + FOX_HEADS]
    put("w_forget", forget.reshape(KT, P, FOX_HEADS).transpose(1, 0, 2).reshape(P, -1))
    put("glu_w", inputs["s5_glu_w"][l].reshape(2, P, 256).transpose(1, 0, 2).reshape(P, -1))
    for name, src in (("b_re", "s5_B_re"), ("b_im", "s5_B_im")):
        w = inputs[src][l]
        a = np.zeros((P, 2, P), np.float32)
        for g in range(GROUPS):
            r, c = (g * GROUP) % P, (g % 2) * STATE
            a[r:r + GROUP, g // 8, c:c + STATE] = w[g].T
        put(name, a.reshape(P, -1))
    for name, src in (("c_re", "s5_C_re"), ("c_im", "s5_C_im")):
        w = inputs[src][l]
        a = np.zeros((P, S5_TILES, 32), np.float32)
        for g in range(GROUPS):
            r, c = (g % 2) * STATE, (g % 2) * GROUP
            a[r:r + STATE, g // 2, c:c + GROUP] = w[g].T
        put(name, a.reshape(P, -1))
    return par


def _constants():
    i = np.arange(P)
    causal = np.where(i[:, None] >= i[None, :], 0.0, -1e30)
    carry = np.tile((np.arange(HEADS * T) % CHUNK != 0).astype(np.float32), (P, 1))
    con = np.concatenate([np.eye(P), np.ones((P, P)), (i[:, None] // 64 == i[None, :] // 64),
                          causal, np.zeros((P, P)), causal, carry], axis=1).astype(np.float32)
    select = np.repeat(np.eye(4, dtype=np.float32), T, axis=1)
    masks = []
    for size in LEVELS:
        masks.append((i[:, None] // (2 * size) == i[None, :] // (2 * size))
                     & (i[:, None] % (2 * size) < size) & (i[None, :] % (2 * size) >= size))
    masks.append(i[:, None] == i[None, :])
    return con, select, np.stack(masks, axis=1).astype(np.float32)


def kernel(**inputs):
    import concourse.bacc as bacc
    from concourse.bass_utils import run_bass_kernel_spmd

    inputs = {k: np.asarray(v) for k, v in inputs.items()}
    con, select, masks = _constants()
    arrays = {
        "xT": np.ascontiguousarray(inputs["x"][0].T.reshape(KT, P, T).transpose(1, 0, 2)),
        "stream": np.stack([u for l in range(DEPTH) for u in _unit_stream(inputs, l)]),
        "params": np.stack([_params(inputs, l) for l in range(DEPTH)]),
        "gain0": np.ascontiguousarray(inputs["ffn1_norm"][0].reshape(-1, P).T),
        "consts": con, "select": select, "masks": masks,
    }
    nc = bacc.Bacc("TRN2", target_bir_lowering=False, num_devices=1)
    args = {n: nc.dram_tensor(n, a.shape, mybir.dt.from_np(a.dtype), kind="ExternalInput").ap()
            for n, a in arrays.items()}
    out = nc.dram_tensor("out", (P, KT, T), F32, kind="ExternalOutput").ap()
    build(nc, out=out, **args)
    got = run_bass_kernel_spmd(nc, [arrays], core_ids=[0]).results[0]["out"]
    return np.ascontiguousarray(got.transpose(1, 0, 2).reshape(D, T).T)[None]
```

```python
from contextlib import ExitStack

import numpy as np

import concourse.bass as bass
from concourse import mybir

F32 = mybir.dt.float32
F32R = mybir.dt.float32r
U8 = mybir.dt.uint8
ALU = mybir.AluOpType
ACT = mybir.ActivationFunctionType
AX = mybir.AxisListType

P = 128
DEPTH = 2
T = 256
D = 1024
KT = D // P
FF = 2816
ITERS = FF // 256
FOX_HEADS, FOX_DIM = 4, 64
HEADS = 4
GROUPS, GROUP, STATE = 16, 16, 64
S5_TILES = GROUPS * STATE // P
CHUNK = 64
EPS = 1e-6

FFN_UNITS = 3 * ITERS
IN_UNITS = 12
OUT_UNITS = 4
UNITS = 2 * FFN_UNITS + IN_UNITS + OUT_UNITS
SPLIT_UNITS = 2 * FFN_UNITS
DIRECT_UNITS = IN_UNITS + OUT_UNITS
RING = 3
AHEAD = 2
VISITS = UNITS // RING

COLS = {}
_at = 0
for _name, _n in [("gain_mix", KT), ("gain_ffn2", KT), ("gain_next", KT), ("lam_re", S5_TILES),
                  ("lam_im", S5_TILES), ("log_step", S5_TILES), ("lb_logit", 2 * HEADS), ("later_layer", 1),
                  ("o_gain", HEADS), ("skip", 2), ("glu_b", 2), ("q_gain", 1), ("k_gain", 1), ("f_bias", 1),
                  ("w_forget", KT * FOX_HEADS), ("b_re", 2 * P), ("b_im", 2 * P),
                  ("c_re", S5_TILES * 32), ("c_im", S5_TILES * 32), ("glu_w", 512)]:
    COLS[_name] = (_at, _n)
    _at += _n
NPAR = _at

LEVELS = [64, 32, 16, 8, 4, 2, 1]
NLEV = len(LEVELS) + 1
NSTEP = NLEV + 1

TWO_PI = 2.0 * np.pi
PI_A = 6.28125
PI_B = float(np.float32(np.round((TWO_PI - PI_A) * 2.0 ** 22) / 2.0 ** 22))
PI_C = float(np.float32(TWO_PI - PI_A - PI_B))
ROUND = 1.5 * 2.0 ** 23


class Steps:

    def __init__(self, engine, sem, layer, per_layer):
        self.engine, self.sem, self.base, self.per_layer, self.n = engine, sem, layer * per_layer, per_layer, 0

    def mark(self, instruction):
        self.n += 1
        return instruction.then_inc(self.sem, 1)

    def wait(self):
        if self.n:
            self.engine.wait_ge(self.sem, self.base + self.n)

    def close(self):
        assert self.n == self.per_layer, f"{self.n} steps in a layer, not {self.per_layer}"


DVE_STEPS = 52
POOL_STEPS = 61


def build(nc, xT, stream, params, gain0, consts, select, masks, out):
    ctx = ExitStack()
    with ctx:
        def sb(name, shape, dt=F32, where=ctx):
            return where.enter_context(nc.sbuf_tensor(name, shape, dt))

        def sem(name):
            return ctx.enter_context(nc.semaphore(name))

        raw = [sb(f"raw{s}", [P, 2048]) for s in range(4)]
        x = sb("x", [P, KT, T])
        h = sb("h", [P, KT, T])
        sq = sb("sq", [P, 4, T])
        sumsq = sb("sumsq", [P, T])
        ln_ms = sb("ln_ms", [P, T])
        rstd = sb("rstd", [P, T])
        rstd_tok = sb("rstd_tok", [P, 4])
        par = sb("par", [P, NPAR])
        g0 = sb("g0", [P, KT])
        con = sb("con", [P, 3 * P + 384 + HEADS * T])
        sel = sb("sel", [4, 4 * T])
        mask = sb("mask", [P, NLEV * P], U8)
        eps = sb("eps", [P, 1])
        cos = sb("cos", [P, S5_TILES, T])
        sin = sb("sin", [P, S5_TILES, T])
        trig_tmp = sb("trig_tmp", [P, S5_TILES, P])
        rot = sb("rot", [P, 2, 2, S5_TILES])
        mag = sb("mag", [P, S5_TILES])
        coef = sb("coef", [P, 3, S5_TILES])
        s5s = sb("s5s", [P, 12, S5_TILES])
        c_out = sb("c_out", [P, 2, S5_TILES * 32])
        lbs = sb("lbs", [P, 8, HEADS])
        tick = sb("tick", [P, 1])
        zero = sb("zero", [P, 512], F32R)

        ffn_mem = ExitStack()
        hi = [sb(f"hi{s}", [P, 2048], F32R, ffn_mem) for s in range(RING)]
        lo = [sb(f"lo{s}", [P, 2048], F32R, ffn_mem) for s in range(RING)]
        xg_hi = sb("xg_hi", [P, KT, T], F32R, ffn_mem)
        xg_lo = sb("xg_lo", [P, KT, T], F32R, ffn_mem)
        gate = sb("gate", [P, 2, T], F32, ffn_mem)
        up = sb("up", [P, 2, T], F32, ffn_mem)
        silu = sb("silu", [P, 2, T], F32, ffn_mem)
        act = sb("act", [P, 2, T], F32, ffn_mem)
        act_hi = sb("act_hi", [P, 2, T], F32R, ffn_mem)
        act_lo = sb("act_lo", [P, 2, T], F32R, ffn_mem)
        ffn_mem.close()

        bf = sb("bf", [P, HEADS, T])
        key = sb("key", [P, HEADS, T])
        bq = sb("bq", [P, HEADS, T])
        bc = sb("bc", [P, HEADS, T])
        bsum = sb("bsum", [P, HEADS])
        dec = sb("dec", [P, 2, HEADS, T])
        qk = sb("qk", [P, 2, HEADS, T])
        attn = sb("attn", [P, 2 * HEADS, P])
        attn_x = sb("attn_x", [P, HEADS, P])
        v_b = sb("v_b", [P, 2, 512])
        bg = sb("bg", [P, HEADS, T])
        osq = dec[:, 0, :, :].rearrange("p h t -> p (h t)")
        orn = dec[:, 1, :, :].rearrange("p h t -> p (h t)")
        u = sb("u", [P, 2, T])
        ra = sb("ra", [P, 2, 2, T])
        rb = sb("rb", [P, 2, 2, T])
        xin = sb("xin", [P, 2, 2, T])
        xt = sb("xt", [P, 2, 2, T])
        ua = sb("ua", [P, 2, 2, T])
        ub = sb("ub", [P, 2, 2, T])
        xs = sb("xs", [P, S5_TILES, 2, T])
        y = trig_tmp[:, 0:4, :].rearrange("p (a b) t -> p a (b t)", a=2)
        z = trig_tmp[:, 4:8, :].rearrange("p (a b) t -> p a (b t)", a=2)
        fqk = sb("fqk", [P, 2, 2, T])
        fsq = sb("fsq", [P, 2, 2 * T])
        fv = sb("fv", [P, 2, 256])
        fl = sb("fl", [4, 4, T])
        fox_out = fsq[:, 0, :].rearrange("p (a t) -> p a t", a=2)
        s5_out = y
        sc = sb("sc", [P, FOX_HEADS, 384])
        pT = xs[:, 0:3, :, :].rearrange("p j a t -> p (j a t)")
        fst = sb("fst", [P, 4, 8])

        ps = ctx.enter_context(nc.psum_tensor("ps", [P, 8 * 512], F32))

        def bank(b, n=1):
            return ps[:, b * 512:(b + n) * 512]

        def out_bank(n):
            return bank((n + 2) % 4)

        ident = con[:, 0:P]
        ones = con[:, P:2 * P]
        halves = con[:, 2 * P:3 * P]
        cmask = con[:, 3 * P:3 * P + 384]
        carry = con[:, 3 * P + 384:]

        def prm(name, a=0, n=None):
            at, size = COLS[name]
            return par[:, at + a:at + (size if n is None else a + n)]

        raw_loaded = [sem(f"raw_loaded{s}") for s in range(4)]
        consts_loaded = sem("consts_loaded")
        x_loaded = [sem("x_loaded0"), sem("x_loaded1")]
        par_loaded = sem("par_loaded")
        hi_written = sem("hi_written")
        lo_written = sem("lo_written")
        units_done = sem("units_done")
        direct_done = sem("direct_done")
        xg_hi_ready = sem("xg_hi_ready")
        xg_lo_ready = sem("xg_lo_ready")
        h_ready = sem("h_ready")
        sq_ready = sem("sq_ready")
        sumsq_added = sem("sumsq_added")
        sums_done = sem("sums_done")
        rstd_ready = sem("rstd_ready")
        rstd_steps = sem("rstd_steps")
        x_ready = sem("x_ready")
        acc_done = sem("acc_done")
        gate_scaled = sem("gate_scaled")
        gu_read = sem("gu_read")
        silu_done = sem("silu_done")
        act_ready = sem("act_ready")
        act_hi_ready = sem("act_hi_ready")
        act_lo_ready = sem("act_lo_ready")
        out_stored = sem("out_stored")
        mask_ready = sem("mask_ready")
        zeros_set = sem("zeros_set")
        once = sem("once")
        s5_dt = sem("s5_dt")
        s5_args = sem("s5_args")
        s5_funs = sem("s5_funs")
        s5_coef = sem("s5_coef")
        pool_step = sem("pool_step")
        tables_ready = sem("tables_ready")
        dve_step = sem("dve_step")
        proj_dve = sem("proj_dve")
        proj_act = sem("proj_act")
        bf_sig = sem("bf_sig")
        bf_f = sem("bf_f")
        bf_log = sem("bf_log")
        dec_arg = sem("dec_arg")
        dec_exp = sem("dec_exp")
        qk_ready = sem("qk_ready")
        lev_done = sem("lev_done")
        lev_read = sem("lev_read")
        attn_clear = sem("attn_clear")
        bu_done = sem("bu_done")
        bu_read = sem("bu_read")
        xin_ready = sem("xin_ready")
        scan_done = sem("scan_done")
        un_ready = sem("un_ready")
        xs_ready = sem("xs_ready")
        y_done = sem("y_done")
        y_ready = sem("y_ready")
        z_ready = sem("z_ready")
        glu_done = sem("glu_done")
        sg_ready = sem("sg_ready")
        mix_s5 = sem("mix_s5")
        fsq_ready = sem("fsq_ready")
        fsum_done = sem("fsum_done")
        frn_ready = sem("frn_ready")
        fln = sem("fln")
        fqk_ready = sem("fqk_ready")
        af_done = sem("af_done")
        af_abs = sem("af_abs")
        af_exp = sem("af_exp")
        af_ln = sem("af_ln")
        cum_ready = sem("cum_ready")
        sc_done = sem("sc_done")
        sc_read = sem("sc_read")
        max_ready = sem("max_ready")
        exp_done = sem("exp_done")
        p_ready = sem("p_ready")
        pt_done = sem("pt_done")
        pt_act = sem("pt_act")
        pt_dve = sem("pt_dve")
        fo_done = sem("fo_done")
        mix_fox = sem("mix_fox")
        o_done = sem("o_done")
        osq_ready = sem("osq_ready")
        osum_done = sem("osum_done")
        oln = sem("oln")
        orn_ready = sem("orn_ready")
        bg_ready = sem("bg_ready")
        mix_hgrn = sem("mix_hgrn")

        block = ctx.enter_context(nc.Block())

        @block.sync
        def _(sp):
            sp.dma_start(g0[:, :], gain0).then_inc(x_loaded[0], 16)
            sp.dma_start(x[:, 0:KT // 2, :], xT[:, 0:KT // 2, :]).then_inc(x_loaded[0], 16)
            sp.dma_start(x[:, KT // 2:, :], xT[:, KT // 2:, :]).then_inc(x_loaded[1], 16)

            def load(n, slot):
                sp.dma_start(raw[slot][:, :], stream[bass.ds(n, 1), :, :].rearrange("o p c -> p (o c)")
                             ).then_inc(raw_loaded[slot], 16)

            def load_split(n, at, slot):
                sp.wait_ge(hi_written, n + 1)
                sp.wait_ge(lo_written, n + 1)
                load(at, slot)

            for p in range(AHEAD):
                load(p, p)
            with sp.Fori(0, DEPTH) as l:
                load_split(l * SPLIT_UNITS + 2, l * UNITS + 2, 2)
                with sp.Fori(1, ITERS) as i:
                    for p in range(RING):
                        load_split(l * SPLIT_UNITS + i * 3 + p, l * UNITS + i * 3 + p, p)
                for w in range(IN_UNITS):
                    if w < RING:
                        sp.wait_ge(hi_written, l * SPLIT_UNITS + FFN_UNITS + w + 1)
                        sp.wait_ge(lo_written, l * SPLIT_UNITS + FFN_UNITS + w + 1)
                    else:
                        sp.wait_ge(direct_done, l * DIRECT_UNITS + w - 2)
                    load(l * UNITS + FFN_UNITS + w, w % RING)
                for w in range(OUT_UNITS):
                    if w < RING:
                        sp.wait_ge(direct_done, l * DIRECT_UNITS + IN_UNITS - RING + w + 1)
                    load(l * UNITS + FFN_UNITS + IN_UNITS + w, w)
                for p in range(RING):
                    sp.wait_ge(direct_done, l * DIRECT_UNITS + IN_UNITS + p + 1)
                    load(l * UNITS + FFN_UNITS + DIRECT_UNITS + p, p)
                with sp.Fori(1, ITERS) as i:
                    for p in range(RING):
                        load_split(l * SPLIT_UNITS + FFN_UNITS + i * 3 + p,
                                   l * UNITS + FFN_UNITS + DIRECT_UNITS + i * 3 + p, p)
                for p in range(AHEAD):
                    load_split((l + 1) * SPLIT_UNITS + p, (l + 1) * UNITS + p, p)
            for m in range(KT):
                sp.wait_ge(x_ready, 24 * (DEPTH - 1) + 16 + m + 1)
                sp.dma_start(out[:, m, :], x[:, m, :]).then_inc(out_stored, 16)
            sp.wait_ge(out_stored, 16 * KT)

        @block.gpsimd
        def _(pool):
            pool.memset(eps[:, :], EPS).then_inc(once, 1)
            pool.memset(tick[:, :], 0.0).then_inc(gu_read, 1)
            pool.memset(cos[:, :, 0:1], 1.0).then_inc(hi_written, RING)
            pool.memset(sin[:, :, 0:1], 0.0).then_inc(lo_written, RING)
            pool.memset(lbs[:, 7, :], 0.0).then_inc(units_done, RING)
            pool.wait_ge(x_loaded[0], 32)
            pool.dma_start(con[:, :], consts).then_inc(consts_loaded, 16)
            pool.dma_start(sel[:, :], select).then_inc(consts_loaded, 16)
            pool.dma_start(trig_tmp[:, :, :], masks).then_inc(consts_loaded, 16)

            def sum_squares(norm, first=False):
                for m in range(1, KT):
                    pool.wait_ge(sq_ready, norm * KT + m + 1)
                    if m == 1:
                        if not first:
                            pool.wait_ge(sums_done, norm)
                        a = sq[:, 0, :]
                    else:
                        pool.wait_ge(sumsq_added, norm * 7 + m - 1)
                        a = sumsq[:, :]
                    pool.tensor_tensor(sumsq[:, :], a, sq[:, m % 4, :], ALU.add).then_inc(sumsq_added, 1)

            sum_squares(0, first=True)
            with pool.Fori(0, DEPTH) as l:
                steps = Steps(pool, pool_step, l, POOL_STEPS)
                pool.wait_ge(s5_coef, l + 1)
                n, r = 1, 0
                while n < T:
                    pc, psn = rot[:, r, 0, :], rot[:, r, 1, :]
                    wide_c = pc.unsqueeze(2).broadcast_to([P, S5_TILES, n])
                    wide_s = psn.unsqueeze(2).broadcast_to([P, S5_TILES, n])
                    tmp = trig_tmp[:, :, 0:n]
                    steps.wait()
                    pool.tensor_tensor(cos[:, :, n:2 * n], cos[:, :, 0:n], wide_c, ALU.mult)
                    pool.tensor_tensor(tmp, sin[:, :, 0:n], wide_s, ALU.mult)
                    steps.mark(pool.tensor_tensor(sin[:, :, n:2 * n], sin[:, :, 0:n], wide_c, ALU.mult))
                    steps.wait()
                    steps.mark(pool.tensor_tensor(cos[:, :, n:2 * n], cos[:, :, n:2 * n], tmp, ALU.subtract))
                    steps.wait()
                    steps.mark(pool.tensor_tensor(tmp, cos[:, :, 0:n], wide_s, ALU.mult))
                    steps.wait()
                    steps.mark(pool.tensor_tensor(sin[:, :, n:2 * n], sin[:, :, n:2 * n], tmp, ALU.add))
                    if 2 * n == T:
                        break
                    qc, qs = rot[:, 1 - r, 0, :], rot[:, 1 - r, 1, :]
                    t1 = s5s[:, 11, :]
                    steps.mark(pool.tensor_tensor(qc, pc, pc, ALU.mult))
                    pool.tensor_tensor(t1, psn, psn, ALU.mult)
                    steps.mark(pool.tensor_tensor(qs, pc, psn, ALU.mult))
                    steps.wait()
                    steps.mark(pool.tensor_tensor(qc, qc, t1, ALU.subtract))
                    steps.mark(pool.tensor_tensor(qs, qs, qs, ALU.add))
                    n, r = 2 * n, 1 - r
                cr = prm("c_re").rearrange("p (j c) -> p j c", c=32)
                ci = prm("c_im").rearrange("p (j c) -> p j c", c=32)
                kr = coef[:, 0, :].unsqueeze(2).broadcast_to([P, S5_TILES, 32])
                ki = coef[:, 1, :].unsqueeze(2).broadcast_to([P, S5_TILES, 32])
                minus_ki = coef[:, 2, :].unsqueeze(2).broadcast_to([P, S5_TILES, 32])
                o_re = c_out[:, 0, :].rearrange("p (j c) -> p j c", c=32)
                o_im = c_out[:, 1, :].rearrange("p (j c) -> p j c", c=32)
                tmp = trig_tmp[:, :, 0:32]
                tmp2 = trig_tmp[:, :, 32:64]
                steps.wait()
                pool.tensor_tensor(o_re, cr, kr, ALU.mult)
                pool.tensor_tensor(tmp, ci, ki, ALU.mult)
                pool.tensor_tensor(o_im, cr, minus_ki, ALU.mult)
                steps.mark(pool.tensor_tensor(tmp2, ci, kr, ALU.mult))
                steps.wait()
                pool.tensor_tensor(o_re, o_re, tmp, ALU.subtract)
                pool.tensor_tensor(o_im, o_im, tmp2, ALU.subtract).then_inc(tables_ready, 1)
                steps.close()

                sum_squares(l * 3 + 1)
                pool.wait_ge(sums_done, l * 3 + 2)
                none = cmask[:, P:2 * P].unsqueeze(1).broadcast_to([P, 2 * HEADS, P])
                pool.tensor_tensor(attn[:, :, :], none, none, ALU.add).then_inc(attn_clear, 1)

                def rotated(j):
                    pool.wait_ge(bu_read, l * 8 + j + 1)
                    if j >= 2:
                        pool.wait_ge(scan_done, l * 8 + j - 1)
                    pool.tensor_tensor(xin[:, j % 2, 0, :], ra[:, j % 2, 0, :], rb[:, j % 2, 1, :], ALU.add)
                    pool.tensor_tensor(xin[:, j % 2, 1, :], ra[:, j % 2, 1, :], rb[:, j % 2, 0, :], ALU.subtract
                                       ).then_inc(xin_ready, 1)

                def rotated_back(j):
                    pool.wait_ge(un_ready, l * 8 + j + 1)
                    pool.tensor_tensor(xs[:, j, 0, :], ua[:, j % 2, 0, :], ub[:, j % 2, 1, :], ALU.subtract)
                    pool.tensor_tensor(xs[:, j, 1, :], ub[:, j % 2, 0, :], ua[:, j % 2, 1, :], ALU.add
                                       ).then_inc(xs_ready, 1)

                for j in range(S5_TILES):
                    rotated(j)
                    if j >= 2:
                        rotated_back(j - 2)
                rotated_back(S5_TILES - 2)
                rotated_back(S5_TILES - 1)

                sum_squares(l * 3 + 2)
                sum_squares(l * 3 + 3)

        @block.scalar
        def _(e):
            def square(norm, m, first=False):
                if not first or m >= 4:
                    e.wait_ge(sumsq_added, norm * 7 + (m - 4 if m > 5 else 1 if m >= 4 else 0))
                e.activation(sq[:, m % 4, :], x[:, m, :], ACT.Square).then_inc(sq_ready, 1)

            def boundary(norm, hi_at, wait_x, gain):
                for m in range(KT):
                    wait_x(m)
                    if hi_at is None:
                        e.activation(h[:, m, :], x[:, m, :], ACT.Copy, scale=gain[:, m:m + 1]).then_inc(h_ready, 1)
                    else:
                        e.activation(xg_hi[:, m, :], x[:, m, :], ACT.Copy, scale=gain[:, m:m + 1]
                                     ).then_inc(xg_hi_ready, 1)
                    square(norm, m)

            def split_hi(n, visit, slot):
                e.wait_ge(raw_loaded[slot], (visit + 1) * 16)
                e.wait_ge(units_done, n + 1)
                e.activation(hi[slot][:, :], raw[slot][:, :], ACT.Copy).then_inc(hi_written, 1)

            def ffn_start(n0, v0, norm, rstd_step):
                split_hi(n0 + 2, v0, 2)
                e.wait_ge(sums_done, norm + 1)
                e.activation(ln_ms[:, :], bank(7)[:, 0:T], ACT.Ln, scale=1.0 / D, bias=eps[:, :]
                             ).then_inc(rstd_steps, 1)
                e.wait_ge(rstd_steps, rstd_step)
                e.activation(rstd[:, :], ln_ms[:, :], ACT.Exp, scale=-0.5).then_inc(rstd_ready, 1)
                split_hi(n0 + 3, v0 + 1, 0)

            def ffn_steps(f, n0, v0, ahead, between=lambda: None):
                def gated(i, after_silu=lambda: None):
                    e.wait_ge(gate_scaled, f * ITERS + i + 1)
                    e.activation(silu[:, :, :], gate[:, :, :], ACT.Silu).then_inc(silu_done, 1)
                    after_silu()
                    e.wait_ge(act_ready, f * ITERS + i + 1)
                    e.wait_ge(units_done, n0 + i * 3 + 2 + RING)
                    e.activation(act_hi[:, :, :], act[:, :, :], ACT.Copy).then_inc(act_hi_ready, 1)

                def split_three(i):
                    split_hi(n0 + i * 3 + 5, v0 + i + 1, 2)
                    split_hi(n0 + i * 3 + 6, v0 + i + 2, 0)
                    split_hi(n0 + i * 3 + 7, v0 + i + 2, 1)

                gated(0)
                split_hi(n0 + 4, v0 + 1, 1)
                between()
                split_three(0)
                with e.Fori(1, ITERS - 2) as i:
                    gated(i)
                    split_three(i)
                gated(ITERS - 2)
                split_hi(n0 + FFN_UNITS - 1, v0 + ITERS - 1, 2)
                gated(ITERS - 1, lambda: split_hi(n0 + FFN_UNITS, v0 + ITERS, 0) if ahead else None)
                if ahead:
                    split_hi(n0 + FFN_UNITS + 1, v0 + ITERS, 1)

            e.wait_ge(once, 1)
            for m in range(KT):
                e.wait_ge(x_loaded[2 * m // KT], 32 if m < KT // 2 else 16)
                e.activation(xg_hi[:, m, :], x[:, m, :], ACT.Copy, scale=g0[:, m:m + 1]).then_inc(xg_hi_ready, 1)
            split_hi(0, 0, 0)
            split_hi(1, 0, 1)
            for m in range(KT):
                square(0, m, first=True)
            e.wait_ge(consts_loaded, 48)
            with e.Fori(0, DEPTH) as l:
                e.wait_ge(xg_lo_ready, l * 16 + 8)
                e.dma_start(par[:, :], params[bass.ds(l, 1), :, :].rearrange("o p c -> p (o c)")
                            ).then_inc(par_loaded, 16)
                ffn_start(l * SPLIT_UNITS, l * VISITS, l * 3, l * 4 + 1)
                def parameters():
                    e.wait_ge(par_loaded, l * 16 + 16)
                    e.activation(s5s[:, 0, :], prm("log_step"), ACT.Exp).then_inc(s5_dt, 1)
                    e.wait_ge(s5_args, l * 2 + 1)
                    e.activation(mag[:, :], s5s[:, 1, :], ACT.Exp).then_inc(s5_funs, 1)
                    e.activation(lbs[:, 2:4, :], lbs[:, 0:2, :], ACT.Exp).then_inc(s5_funs, 1)
                    e.wait_ge(s5_args, l * 2 + 2)
                    e.activation(s5s[:, 4, :], s5s[:, 3, :], ACT.Sin).then_inc(s5_funs, 1)
                    e.activation(s5s[:, 5, :], s5s[:, 3, :], ACT.Sin, scale=0.5).then_inc(s5_funs, 1)

                ffn_steps(l * 2, l * SPLIT_UNITS, l * VISITS, False, parameters)

                def wait_x1(m):
                    e.wait_ge(x_ready, l * 24 + m + 1)
                boundary(l * 3 + 1, None, wait_x1, prm("gain_mix"))
                e.wait_ge(sums_done, l * 3 + 2)
                e.activation(ln_ms[:, :], bank(7)[:, 0:T], ACT.Ln, scale=1.0 / D, bias=eps[:, :]).then_inc(rstd_steps, 1)
                e.activation(rstd_tok[:, 2:4], bank(7)[:, T:T + 2], ACT.Ln, scale=1.0 / D, bias=eps[:, :]
                             ).then_inc(rstd_steps, 1)
                e.wait_ge(rstd_steps, l * 4 + 3)
                e.activation(rstd_tok[:, 0:2], rstd_tok[:, 2:4], ACT.Exp, scale=-0.5)
                e.activation(rstd[:, :], ln_ms[:, :], ACT.Exp, scale=-0.5).then_inc(rstd_ready, 1)
                e.wait_ge(proj_dve, l * 9 + 3)
                e.activation(key[:, :, :], bf[:, :, :], ACT.Sigmoid).then_inc(bf_sig, 1)
                e.wait_ge(bf_f, l + 1)
                e.activation(bf[:, :, :], bf[:, :, :], ACT.Ln).then_inc(bf_log, 1)

                def decays(n):
                    e.wait_ge(dec_arg, l * (NSTEP - 1) + n + 1)
                    d = dec[:, n % 2, :, :]
                    ch = lambda t, c: t.rearrange("p h (c k) -> p h c k", k=CHUNK)[:, :, c, :]
                    if n == 0:
                        e.activation(d.rearrange("p h (n s k) -> p h n s k", s=2, k=CHUNK)[:, :, :, 0, :],
                                     d.rearrange("p h (n s k) -> p h n s k", s=2, k=CHUNK)[:, :, :, 0, :], ACT.Exp)
                        e.activation(d.rearrange("p h (n s k) -> p h n s k", s=2, k=CHUNK)[:, :, :, 1, :],
                                     bc[:, :, :].rearrange("p h (n s k) -> p h n s k", s=2, k=CHUNK)[:, :, :, 1, :],
                                     ACT.Exp).then_inc(dec_exp, 1)
                    elif n == NSTEP - 2:
                        e.activation(d[:, :, 0:T // 2], d[:, :, 0:T // 2], ACT.Exp)
                        e.activation(ch(d, 2), ch(bc[:, :, :], 2), ACT.Exp)
                        e.activation(ch(d, 3), ch(d, 3), ACT.Exp).then_inc(dec_exp, 1)
                    else:
                        e.activation(d, d, ACT.Exp).then_inc(dec_exp, 1)

                def values(n, dst):
                    e.wait_ge(rstd_ready, l * 3 + 2)
                    e.wait_ge(direct_done, l * DIRECT_UNITS + n + 1)
                    for t in range(2):
                        e.activation(dst(t), bank(4 + n % 2)[:, t * 256:(t + 1) * 256], ACT.Copy,
                                     scale=rstd_tok[:, t:t + 1]).then_inc(proj_act, 1)

                def fox_norm(w):
                    e.wait_ge(proj_dve, l * 9 + 6 + w)
                    e.activation(fsq[:, w, :], fqk[:, w, :, :].rearrange("p a t -> p (a t)"), ACT.Square
                                 ).then_inc(fsq_ready, 1)

                def fox_rms(w):
                    e.wait_ge(fsum_done, l * 2 + w + 1)
                    e.activation(fsq[:, w, :], bank(6 + w), ACT.Ln, scale=1.0 / FOX_DIM, bias=eps[:, :]
                                 ).then_inc(fln, 1)
                    e.wait_ge(fln, l * 2 + w + 1)
                    e.activation(fsq[:, w, :], fsq[:, w, :], ACT.Exp, scale=-0.5).then_inc(frn_ready, 1)

                decays(0)
                decays(1)
                fox_norm(0)
                decays(2)
                fox_norm(1)
                e.wait_ge(af_abs, l + 1)
                e.activation(fl[:, 1, :], fl[:, 1, :], ACT.Exp, scale=-1.0).then_inc(af_exp, 1)
                e.wait_ge(af_exp, l + 1)
                e.activation(fl[:, 1, :], fl[:, 1, :], ACT.Ln, bias=ones[0:4, 0:1]).then_inc(af_ln, 1)
                decays(3)
                values(7, lambda t: v_b[:, t, 0:256])
                fox_rms(0)
                fox_rms(1)
                def fox_exp(t):
                    e.wait_ge(max_ready, l * 2 + 2 - t)
                    for hd in range(FOX_HEADS):
                        part = sc[:, hd, 0:P] if t == 0 else sc[:, hd, P:384]
                        e.activation(part, part, ACT.Exp, bias=fst[:, 1, t * 4 + hd:t * 4 + hd + 1],
                                     accum_out=fst[:, 2, t * 4 + hd:t * 4 + hd + 1]).then_inc(exp_done, 1)

                pT_heads = pT.rearrange("p (h c) -> p h c", c=384)
                decays(4)
                values(8, lambda t: v_b[:, t, 256:512])
                decays(5)
                fox_exp(1)
                decays(6)
                values(9, lambda t: fv[:, t, :])
                decays(7)
                e.wait_ge(y_ready, l + 1)
                e.activation(z, y, ACT.Gelu_apprx_tanh).then_inc(z_ready, 1)
                fox_exp(0)
                e.wait_ge(pt_done, l * 2 + 1)
                e.activation(pT_heads[:, 0:2, P:384], bank(6).rearrange("p (h c) -> p h c", c=T), ACT.Copy
                             ).then_inc(pt_act, 1)
                e.wait_ge(glu_done, l + 1)
                for m in range(2):
                    last = e.activation(y[:, m, :], bank(5)[:, m * T:(m + 1) * T], ACT.Sigmoid,
                                        bias=prm("glu_b", m, 1))
                last.then_inc(sg_ready, 1)
                e.wait_ge(pt_done, l * 2 + 2)
                e.activation(pT_heads[:, :, 0:P], bank(6).rearrange("p (h c) -> p h c", c=P), ACT.Copy
                             ).then_inc(pt_act, 1)
                e.wait_ge(o_done, l + 1)
                e.activation(osq[:, :], bank(0, 2), ACT.Square).then_inc(osq_ready, 1)
                e.wait_ge(osum_done, l + 1)
                e.activation(orn[:, :], bank(2, 2), ACT.Ln, scale=1.0 / P, bias=eps[:, :]).then_inc(oln, 1)
                e.wait_ge(oln, l + 1)
                e.activation(osq[:, :], orn[:, :], ACT.Exp, scale=-0.5).then_inc(orn_ready, 1)
                e.wait_ge(fo_done, l + 1)
                e.activation(fsq[:, 0, :], bank(4), ACT.Copy).then_inc(mix_fox, 1)
                e.wait_ge(proj_dve, l * 9 + 9)
                e.activation(bg[:, :, :], bg[:, :, :], ACT.Silu).then_inc(bg_ready, 1)

                split_hi(l * SPLIT_UNITS + FFN_UNITS, l * VISITS + 16, 0)
                split_hi(l * SPLIT_UNITS + FFN_UNITS + 1, l * VISITS + 16, 1)

                def wait_x2(m):
                    e.wait_ge(x_ready, l * 24 + 8 + m + 1)
                boundary(l * 3 + 2, l * 2 + 1, wait_x2, prm("gain_ffn2"))
                ffn_start(l * SPLIT_UNITS + FFN_UNITS, l * VISITS + 16, l * 3 + 2, l * 4 + 4)
                ffn_steps(l * 2 + 1, l * SPLIT_UNITS + FFN_UNITS, l * VISITS + 16, True)

                def wait_x3(m):
                    e.wait_ge(x_ready, l * 24 + 16 + m + 1)
                boundary(l * 3 + 3, l * 2 + 2, wait_x3, prm("gain_next"))

        @block.tensor
        def _(pe):
            def three(acc, w_hi, w_lo, a_hi, a_lo, start, stop):
                pe.matmul(acc, w_hi, a_hi, start=start, stop=False, skip_group_check=True)
                pe.matmul(acc, w_hi, a_lo, start=False, stop=False, skip_group_check=True)
                return pe.matmul(acc, w_lo, a_hi, start=False, stop=stop, skip_group_check=True)

            def down_acc(m):
                return bank(m // 2)[:, (m % 2) * T:(m % 2 + 1) * T]

            def row_sums(norm, tokens):
                pe.wait_ge(consts_loaded, 48)
                pe.wait_ge(sumsq_added, norm * 7 + 7)
                last = pe.matmul(bank(7)[:, 0:T], ones, sumsq[:, :], start=True, stop=True)
                if tokens:
                    for t in range(2):
                        last = pe.matmul(bank(7)[:, T + t:T + t + 1], sumsq[:, t * P:(t + 1) * P], ones[:, 0:1],
                                         start=True, stop=True, skip_group_check=True)
                last.then_inc(sums_done, 1)

            def ffn(f, n0, norm):
                for k in range(KT):
                    pe.wait_ge(xg_lo_ready, f * KT + k + 1)
                    if k == 0:
                        pe.wait_ge(lo_written, n0 + 1 + RING)
                        pe.wait_ge(lo_written, n0 + 2 + RING)
                    if k == 5:
                        row_sums(norm, False)
                    for m in range(2):
                        for s in range(2):
                            w = k * 256 + m * P
                            last = three(bank(4 + m)[:, s * T:(s + 1) * T], hi[s][:, w:w + P], lo[s][:, w:w + P],
                                         xg_hi[:, k, :], xg_lo[:, k, :], k == 0 and s == 0, k == KT - 1)
                last.then_inc(units_done, 2)
                for b in range(4):
                    pe.matmul(bank(b), zero[:, 0:P], zero[:, :], start=True, stop=False, skip_group_check=True)

                def gate_up(half, n, slot, b, first):
                    pe.wait_ge(lo_written, n + 1 + RING)
                    for m in range(2):
                        for k in range(KT):
                            w = k * 256 + m * P
                            last = three(bank(b + m)[:, half * T:(half + 1) * T], hi[slot][:, w:w + P],
                                         lo[slot][:, w:w + P], xg_hi[:, k, :], xg_lo[:, k, :],
                                         k == 0, k == KT - 1)
                    last.then_inc(units_done, 1)

                def step(i, g, first):
                    n = n0 + i * 3 + 2
                    if first:
                        pe.wait_ge(rstd_ready, norm + 1)
                    pe.wait_ge(gu_read, f * ITERS + i + 1)
                    gate_up(0, n, 2, 4 + 2 * g, first)
                    gate_up(1, n + 1, 0, 4 + 2 * g, first)
                    pe.wait_ge(lo_written, n + 3 + RING)
                    pe.wait_ge(act_lo_ready, f * ITERS + i + 1)
                    for m in range(KT):
                        for k in range(2):
                            w = k * D + m * P
                            last = three(down_acc(m), hi[1][:, w:w + P], lo[1][:, w:w + P],
                                         act_hi[:, k, :], act_lo[:, k, :], False, False)
                    last.then_inc(units_done, 1)

                with pe.Fori(0, (ITERS - 1) // 2) as ii:
                    step(ii * 2, 1, True)
                    step(ii * 2 + 1, 0, False)
                pe.wait_ge(lo_written, n0 + FFN_UNITS + RING)
                pe.wait_ge(act_lo_ready, f * ITERS + ITERS)
                for m in range(KT):
                    for k in range(2):
                        w = k * D + m * P
                        last = three(down_acc(m), hi[2][:, w:w + P], lo[2][:, w:w + P],
                                     act_hi[:, k, :], act_lo[:, k, :], False, k == 1)
                    if m % 2 == 1 and m < KT - 1:
                        last.then_inc(acc_done, 1)
                last.then_inc(units_done, 1)

            pe.wait_ge(zeros_set, 1)
            with pe.Fori(0, DEPTH) as l:
                ffn(l * 2, l * SPLIT_UNITS, l * 3)

                dve_units = [0, 1, 2, 3, 4, 5, 6, 10, 11]

                def unit_ready(n):
                    pe.wait_ge(raw_loaded[n % RING], (l * VISITS + ITERS + n // RING + 1) * 16)
                    if n - 2 in dve_units:
                        pe.wait_ge(proj_dve, l * 9 + dve_units.index(n - 2) + 1)
                    elif n >= 2:
                        pe.wait_ge(proj_act, l * 6 + (n - 2 - 7) * 2 + 2)

                def project(n, at_tile={}):
                    unit_ready(n)
                    b, w = bank(4 + n % 2), raw[n % RING]
                    for k in range(KT):
                        if k in at_tile:
                            at_tile[k]()
                        if n == 0:
                            pe.wait_ge(h_ready, l * KT + k + 1)
                        for m in range(2):
                            last = pe.matmul(b[:, m * T:(m + 1) * T], w[:, k * 256 + m * P:k * 256 + m * P + P],
                                             h[:, k, :], start=k == 0 and m == 0, stop=k == KT - 1,
                                             skip_group_check=True)
                    last.then_inc(direct_done, 1)

                def project_tokens(n):
                    unit_ready(n)
                    b, w = bank(4 + n % 2), raw[n % RING]
                    for t in range(2):
                        for k in range(KT):
                            last = pe.matmul(b[:, t * 256:(t + 1) * 256], h[:, k, t * P:(t + 1) * P],
                                             w[:, k * 256:(k + 1) * 256], start=k == 0, stop=k == KT - 1,
                                             skip_group_check=True)
                    last.then_inc(direct_done, 1)

                def input_matrix(j):
                    if j == 0:
                        pe.wait_ge(proj_dve, l * 9 + 1)
                    if j == 1:
                        pe.wait_ge(rstd_ready, l * 3 + 2)
                    if j >= 2:
                        pe.wait_ge(bu_read, l * 8 + j - 1)
                    r = 32 * (j % 4)
                    for part, name in enumerate(("b_re", "b_im")):
                        last = pe.matmul(bank(6 + j % 2)[:, part * T:(part + 1) * T],
                                         prm(name)[r:r + 32, (j // 4) * P:(j // 4 + 1) * P],
                                         u[r:r + 32, j // 4, :], start=True, stop=True, skip_group_check=True)
                    last.then_inc(bu_done, 1)

                def level(n):
                    b = bank(2 * (n % 2), 2)
                    if n < NLEV - 1 or n == NSTEP - 1:
                        pe.wait_ge(qk_ready, l * (NSTEP - 1) + (n if n < NLEV - 1 else n - 1) + 1)
                    if n >= 2:
                        pe.wait_ge(lev_read, l * NSTEP + n - 1)
                    if n == NSTEP - 1:
                        q = qk[:, (n - 1) % 2, :, :]
                        for hd in range(HEADS):
                            last = pe.matmul(b[:, hd * P:(hd + 1) * P], q[:, hd, 0:P], q[:, hd, P:T],
                                             start=True, stop=True, skip_group_check=True)
                    else:
                        for hd in range(HEADS):
                            for t in range(2):
                                i = hd * 2 + t
                                tok = slice(t * P, (t + 1) * P)
                                if n == NLEV - 1:
                                    a, c = key[:, hd, tok], bq[:, hd, tok]
                                else:
                                    a = c = qk[:, n % 2, hd, tok]
                                last = pe.matmul(b[:, i * P:(i + 1) * P], a, c, start=True, stop=True,
                                                 skip_group_check=True)
                    last.then_inc(lev_done, 1)

                def fox_sums(w):
                    pe.wait_ge(fsq_ready, l * 2 + w + 1)
                    if w == 0:
                        pe.wait_ge(bu_read, l * 8 + 7)
                    else:
                        pe.wait_ge(af_abs, l + 1)
                    pe.matmul(bank(6 + w), halves, fsq[:, w, :], start=True, stop=True).then_inc(fsum_done, 1)

                def s5_output():
                    pe.wait_ge(xs_ready, l * 8 + 8)
                    pe.wait_ge(tables_ready, l + 1)
                    pe.wait_ge(proj_act, l * 6 + 4)
                    for j in range(S5_TILES):
                        r, c = 32 * (j % 4), j // 4
                        for part in range(2):
                            last = pe.matmul(bank(4)[r:r + 32, c * T:(c + 1) * T],
                                             c_out[:, part, j * 32:(j + 1) * 32], xs[:, j, part, :],
                                             start=part == 0, stop=part == 1, skip_group_check=True)
                    last.then_inc(y_done, 1)

                def s5_glu():
                    pe.wait_ge(z_ready, l + 1)
                    pe.wait_ge(proj_act, l * 6 + 6)
                    for m in range(2):
                        for k in range(2):
                            last = pe.matmul(bank(5)[:, m * T:(m + 1) * T], prm("glu_w", k * T + m * P, P),
                                             z[:, k, :], start=k == 0, stop=k == 1, skip_group_check=True)
                    last.then_inc(glu_done, 1)

                def fox_scores(t):
                    if t == 1:
                        pe.wait_ge(fqk_ready, l * 2 + 2)
                        pe.wait_ge(cum_ready, l + 1)
                        pe.wait_ge(frn_ready, l * 2 + 2)
                    else:
                        pe.wait_ge(sc_read, l * 2 + 1)
                    n, tok = (t + 1) * P, slice(t * P, (t + 1) * P)
                    for hd in range(FOX_HEADS):
                        r, tile = 64 * (hd % 2), hd // 2
                        dst = bank(6 + hd % 2)[:, tile * n:(tile + 1) * n]
                        pe.matmul(dst, fqk[r:r + 64, 0, tile, tok], fqk[r:r + 64, 1, tile, 0:n],
                                  start=True, stop=False, skip_group_check=True)
                        pe.matmul(dst, fl[:, 2, tok], sel[:, hd * T:hd * T + n], start=False, stop=False,
                                  skip_group_check=True)
                        last = pe.matmul(dst, sel[:, hd * T:hd * T + P], fl[:, 3, 0:n], start=False, stop=True,
                                         skip_group_check=True)
                    last.then_inc(sc_done, 1)

                def fox_transposes(t):
                    if t == 1:
                        pe.wait_ge(p_ready, l * 2 + 1)
                        pe.wait_ge(sc_read, l * 2 + 2)
                    else:
                        pe.wait_ge(p_ready, l * 2 + 2)
                        pe.wait_ge(pt_act, l * 2 + 1)
                    i = 0
                    for hd in range(FOX_HEADS):
                        for part in ((1, 2) if t == 1 else (0,)):
                            last = pe.transpose(ps[:, 6 * 512 + i * P:6 * 512 + (i + 1) * P],
                                                sc[:, hd, part * P:(part + 1) * P], ident)
                            i += 1
                    last.then_inc(pt_done, 1)

                def fox_output():
                    pe.wait_ge(pt_act, l * 2 + 2)
                    pe.wait_ge(pt_dve, l + 1)
                    pe.wait_ge(proj_dve, l * 9 + 8)
                    for hd in range(FOX_HEADS):
                        r, c = 64 * (hd % 2), (hd // 2) * T
                        w = slice(hd * FOX_DIM, (hd + 1) * FOX_DIM)
                        part = lambda i: pT[:, hd * 384 + i * P:hd * 384 + (i + 1) * P]
                        pe.matmul(bank(4)[r:r + 64, c:c + P], fv[:, 0, w], part(0), start=True, stop=True,
                                  skip_group_check=True)
                        pe.matmul(bank(4)[r:r + 64, c + P:c + T], fv[:, 0, w], part(1), start=True, stop=False,
                                  skip_group_check=True)
                        last = pe.matmul(bank(4)[r:r + 64, c + P:c + T], fv[:, 1, w], part(2), start=False,
                                         stop=True, skip_group_check=True)
                    last.then_inc(fo_done, 1)

                def hgrn_output():
                    pe.wait_ge(lev_read, l * NSTEP + NSTEP)
                    pe.wait_ge(proj_act, l * 6 + 4)
                    for hd in range(HEADS):
                        at = hd * T
                        w = slice(hd * P, (hd + 1) * P)
                        o = bank(0, 2)
                        pe.matmul(o[:, at:at + P], v_b[:, 0, w], attn[:, hd * 2, :], start=True, stop=True,
                                  skip_group_check=True)
                        pe.matmul(o[:, at + P:at + T], v_b[:, 0, w], attn_x[:, hd, :], start=True, stop=False,
                                  skip_group_check=True)
                        last = pe.matmul(o[:, at + P:at + T], v_b[:, 1, w], attn[:, hd * 2 + 1, :], start=False,
                                         stop=True, skip_group_check=True)
                    last.then_inc(o_done, 1)

                def hgrn_sums():
                    pe.wait_ge(osq_ready, l + 1)
                    for b in range(2):
                        last = pe.matmul(bank(2 + b), ones, osq[:, b * 512:(b + 1) * 512], start=True, stop=True)
                    last.then_inc(osum_done, 1)

                project(0)
                row_sums(l * 3 + 1, True)
                project(1)
                input_matrix(0)
                input_matrix(1)
                project(2)
                input_matrix(2)
                input_matrix(3)
                project(3)
                input_matrix(4)
                input_matrix(5)
                project(4)
                input_matrix(6)
                input_matrix(7)
                project(5)
                level(0)
                project(6)
                pe.wait_ge(bu_read, l * 8 + 8)
                for k in range(KT):
                    last = pe.matmul(bank(7)[0:4, 0:T], prm("w_forget", k * 4, 4), h[:, k, :],
                                     start=k == 0, stop=k == KT - 1)
                last.then_inc(af_done, 1)
                level(1)
                project_tokens(7)
                fox_sums(0)
                fox_sums(1)
                level(2)
                project_tokens(8)
                level(3)
                fox_scores(1)
                project_tokens(9)
                level(4)
                s5_output()
                fox_scores(0)
                level(5)
                pe.wait_ge(y_ready, l + 1)
                project(10)
                level(6)
                fox_transposes(1)
                level(7)
                s5_glu()
                level(8)
                fox_transposes(0)
                hgrn_output()
                pe.wait_ge(sg_ready, l + 1)
                project(11, {3: hgrn_sums, 5: fox_output})

                def project_out(n, tiles, last_part):
                    for k in tiles:
                        if k < 2:
                            a = fox_out[:, k, :]
                        elif k >= 6:
                            a = s5_out[:, k - 6, :]
                        else:
                            a = h[:, k, :]
                        for m in range(2):
                            last = pe.matmul(out_bank(n)[:, m * T:(m + 1) * T],
                                             raw[n][:, k * 256 + m * P:k * 256 + m * P + P], a,
                                             start=k == 6 and m == 0, stop=last_part and k == tiles[-1],
                                             skip_group_check=True)
                    if last_part:
                        last.then_inc(direct_done, 1)

                pe.wait_ge(oln, l + 1)
                pe.wait_ge(mix_s5, l + 1)
                pe.wait_ge(mix_fox, l + 1)
                for n in range(2):
                    pe.wait_ge(raw_loaded[n], (l * VISITS + ITERS + 4 + 1) * 16)
                    project_out(n, (6, 7, 0, 1), False)
                pe.wait_ge(mix_hgrn, l + 1)
                for n in range(2):
                    project_out(n, (2, 3, 4, 5), True)
                pe.wait_ge(raw_loaded[2], (l * VISITS + ITERS + 4 + 1) * 16)
                project_out(2, (6, 7, 0, 1, 2, 3, 4, 5), True)
                pe.wait_ge(raw_loaded[3], (l + 1) * 16)
                project_out(3, (6, 7, 0, 1, 2, 3, 4, 5), True)

                ffn(l * 2 + 1, l * SPLIT_UNITS + FFN_UNITS, l * 3 + 2)

        @block.vector
        def _(v):
            def acc(m):
                return bank(m // 2)[:, (m % 2) * T:(m % 2 + 1) * T]

            def split_lo(n, slot):
                v.wait_ge(hi_written, n + 1 + RING)
                v.tensor_tensor(lo[slot][:, :], raw[slot][:, :], hi[slot][:, :].bitcast(F32), ALU.subtract
                                ).then_inc(lo_written, 1)

            def rest_of_x(f, m, gain):
                v.wait_ge(xg_hi_ready, f * KT + m + 1)
                v.scalar_tensor_tensor(xg_lo[:, m, :], x[:, m, :], gain[:, m:m + 1], xg_hi[:, m, :].bitcast(F32),
                                       ALU.mult, ALU.subtract).then_inc(xg_lo_ready, 1)

            def boundary(wait_acc, scale, f, gain, acc=acc):
                for m in range(KT):
                    wait_acc(m)
                    v.scalar_tensor_tensor(x[:, m, :], acc(m), scale, x[:, m, :], ALU.mult, ALU.add
                                           ).then_inc(x_ready, 1)
                    if f is not None and m >= 1:
                        rest_of_x(f, m - 1, gain)
                if f is not None:
                    rest_of_x(f, KT - 1, gain)

            def gated(f, i, g, n_up, norm, after_act=lambda: None):
                both = bank(4 + 2 * g, 2).rearrange("p (m s t) -> p m s t", m=2, s=2)
                wide = rstd[:, :].unsqueeze(1).broadcast_to([P, 2, T])
                v.wait_ge(rstd_ready, norm + 1)
                v.wait_ge(units_done, n_up + 1 + RING)
                v.tensor_tensor(gate[:, :, :], both[:, :, 0, :], wide, ALU.mult).then_inc(gate_scaled, 1)
                v.tensor_tensor(up[:, :, :], both[:, :, 1, :], wide, ALU.mult).then_inc(gu_read, 1)
                v.wait_ge(silu_done, f * ITERS + i + 1)
                v.wait_ge(gu_read, f * ITERS + i + 2)
                v.tensor_tensor(act[:, :, :], silu[:, :, :], up[:, :, :], ALU.mult).then_inc(act_ready, 1)
                after_act()
                v.wait_ge(act_hi_ready, f * ITERS + i + 1)
                v.tensor_tensor(act_lo[:, :, :], act[:, :, :], act_hi[:, :, :].bitcast(F32), ALU.subtract
                                ).then_inc(act_lo_ready, 1)

            def ffn_steps(f, n0, norm, ahead, between=lambda: None):
                def split_three(i):
                    split_lo(n0 + i * 3 + 5, 2)
                    split_lo(n0 + i * 3 + 6, 0)
                    split_lo(n0 + i * 3 + 7, 1)

                split_lo(n0 + 2, 2)
                split_lo(n0 + 3, 0)
                gated(f, 0, 0, n0, norm)
                split_lo(n0 + 4, 1)
                between()
                split_three(0)
                with v.Fori(0, (ITERS - 3) // 2) as ii:
                    for g in (1, 0):
                        i = ii * 2 + 2 - g
                        gated(f, i, g, n0 + i * 3, norm)
                        split_three(i)
                gated(f, ITERS - 2, 1, n0 + 3 * (ITERS - 2), norm)
                split_lo(n0 + FFN_UNITS - 1, 2)
                gated(f, ITERS - 1, 0, n0 + 3 * (ITERS - 1), norm,
                      lambda: split_lo(n0 + FFN_UNITS, 0) if ahead else None)
                if ahead:
                    split_lo(n0 + FFN_UNITS + 1, 1)

            v.memset(zero[:, :].bitcast(F32), 0.0).then_inc(zeros_set, 1)
            for m in range(KT):
                rest_of_x(0, m, g0)
            split_lo(0, 0)
            split_lo(1, 1)
            v.wait_ge(consts_loaded, 48)
            v.tensor_copy(mask[:, :], trig_tmp[:, :, :].rearrange("p j t -> p (j t)")).then_inc(mask_ready, 1)
            v.wait_ge(mask_ready, 1)
            with v.Fori(0, DEPTH) as l:
                st = Steps(v, dve_step, l, DVE_STEPS)

                def parameters():
                    lr, li = prm("lam_re"), prm("lam_im")
                    tiny = lambda i: s5s[:, i, :]
                    v.wait_ge(par_loaded, l * 16 + 16)
                    lg = prm("lb_logit").rearrange("p (d h) -> p d h", d=2)
                    st.mark(v.tensor_tensor(lbs[:, 4, :], lg[:, 0, :], lg[:, 1, :], ALU.max))
                    st.wait()
                    st.mark(v.tensor_tensor(lbs[:, 0:2, :], lg, lbs[:, 4:5, :].broadcast_to([P, 2, HEADS]), ALU.subtract))
                    v.wait_ge(s5_dt, l + 1)
                    v.tensor_tensor(tiny(2), li, tiny(0), ALU.mult)
                    st.wait()
                    v.tensor_tensor(tiny(1), lr, tiny(0), ALU.mult).then_inc(s5_args, 1)
                    v.wait_ge(s5_args, l * 2 + 1)
                    st.mark(v.tensor_scalar(tiny(6), tiny(2), 1.0 / TWO_PI, ROUND, ALU.mult, ALU.add))
                    st.wait()
                    st.mark(v.tensor_scalar(tiny(6), tiny(6), ROUND, None, ALU.subtract))
                    for c in (PI_A, PI_B, PI_C):
                        st.wait()
                        st.mark(v.scalar_tensor_tensor(tiny(2), tiny(6), -c, tiny(2), ALU.mult, ALU.add))
                    st.wait()
                    v.tensor_scalar(tiny(3), tiny(2), 3.1415925, -3.1415925, ALU.min, ALU.max).then_inc(s5_args, 1)
                    v.wait_ge(s5_funs, l * 4 + 2)
                    st.mark(v.tensor_tensor(lbs[:, 4, :], lbs[:, 2, :], lbs[:, 3, :], ALU.add))
                    st.wait()
                    st.mark(v.reciprocal(lbs[:, 4, :], lbs[:, 4, :]))
                    st.wait()
                    st.mark(v.tensor_tensor(lbs[:, 2, :], lbs[:, 2, :], lbs[:, 4, :], ALU.mult))
                    st.mark(v.tensor_tensor(lbs[:, 3, :], lbs[:, 3, :], lbs[:, 4, :], ALU.mult))
                    st.wait()
                    st.mark(v.tensor_tensor(lbs[:, 5, :], lbs[:, 2, :], lbs[:, 3, :], ALU.add))
                    st.wait()
                    st.mark(v.tensor_tensor(lbs[:, 5, :], lbs[:, 5, :], lbs[:, 2, :], ALU.subtract))
                    st.wait()
                    st.mark(v.tensor_scalar(lbs[:, 5, :], lbs[:, 5, :], prm("later_layer"), None, ALU.mult))
                    st.wait()
                    st.mark(v.tensor_scalar(lbs[:, 6, :], lbs[:, 5, :], -1.0, 1.0, ALU.mult, ALU.add))
                    v.wait_ge(s5_funs, l * 4 + 4)
                    st.mark(v.tensor_tensor(tiny(6), tiny(5), tiny(5), ALU.mult))
                    st.mark(v.tensor_copy(rot[:, 0, 1, :], tiny(4)))
                    st.wait()
                    st.mark(v.tensor_scalar(rot[:, 0, 0, :], tiny(6), -2.0, 1.0, ALU.mult, ALU.add))
                    st.wait()
                    st.mark(v.tensor_tensor(tiny(7), mag[:, :], rot[:, 0, 0, :], ALU.mult))
                    st.mark(v.tensor_tensor(tiny(8), mag[:, :], tiny(4), ALU.mult))
                    st.mark(v.tensor_tensor(tiny(9), lr, lr, ALU.mult))
                    st.mark(v.tensor_tensor(tiny(10), li, li, ALU.mult))
                    st.wait()
                    st.mark(v.tensor_scalar(tiny(7), tiny(7), -1.0, None, ALU.add))
                    st.mark(v.tensor_tensor(tiny(9), tiny(9), tiny(10), ALU.add))
                    st.wait()
                    st.mark(v.reciprocal(tiny(9), tiny(9)))
                    st.mark(v.tensor_tensor(tiny(0), tiny(7), lr, ALU.mult))
                    st.mark(v.tensor_tensor(tiny(1), tiny(8), li, ALU.mult))
                    st.mark(v.tensor_tensor(tiny(10), tiny(8), lr, ALU.mult))
                    st.mark(v.tensor_tensor(tiny(6), tiny(7), li, ALU.mult))
                    st.wait()
                    st.mark(v.tensor_tensor(tiny(0), tiny(0), tiny(1), ALU.add))
                    st.mark(v.tensor_tensor(tiny(10), tiny(10), tiny(6), ALU.subtract))
                    st.wait()
                    st.mark(v.tensor_tensor(coef[:, 0, :], tiny(0), tiny(9), ALU.mult))
                    st.mark(v.tensor_tensor(coef[:, 1, :], tiny(10), tiny(9), ALU.mult))
                    st.wait()
                    v.tensor_scalar(coef[:, 2, :], coef[:, 1, :], -1.0, None, ALU.mult).then_inc(s5_coef, 1)

                ffn_steps(l * 2, l * SPLIT_UNITS, l * 3, False, parameters)

                def wait_ffn1(m):
                    if m < KT - 2:
                        v.wait_ge(acc_done, l * 6 + m // 2 + 1)
                    else:
                        v.wait_ge(units_done, l * SPLIT_UNITS + FFN_UNITS + RING)
                boundary(wait_ffn1, 0.5, None, None)

                wide = rstd[:, :].unsqueeze(1).broadcast_to([P, 2, T])

                def take(n, dst):
                    v.wait_ge(direct_done, l * DIRECT_UNITS + n + 1)
                    v.tensor_tensor(dst, bank(4 + n % 2).rearrange("p (m t) -> p m t", m=2), wide, ALU.mult
                                    ).then_inc(proj_dve, 1)

                def rotate(j):
                    v.wait_ge(bu_done, l * 8 + j + 1)
                    if j == 0:
                        v.wait_ge(tables_ready, l + 1)
                    if j >= 2:
                        v.wait_ge(xin_ready, l * 8 + j - 1)
                    b = bank(6 + j % 2).rearrange("p (a t) -> p a t", a=2)
                    c = cos[:, j:j + 1, :].broadcast_to([P, 2, T])
                    s = sin[:, j:j + 1, :].broadcast_to([P, 2, T])
                    v.tensor_tensor(ra[:, j % 2, :, :], b, c, ALU.mult)
                    v.tensor_tensor(rb[:, j % 2, :, :], b, s, ALU.mult).then_inc(bu_read, 1)

                def scan(j):
                    v.wait_ge(xin_ready, l * 8 + j + 1)
                    decay = mag[:, j:j + 1].broadcast_to([P, T])
                    v.tensor_tensor_scan(xt[:, j % 2, 0, :], decay, xin[:, j % 2, 0, :], 0.0, ALU.mult, ALU.add)
                    v.tensor_tensor_scan(xt[:, j % 2, 1, :], decay, xin[:, j % 2, 1, :], 0.0, ALU.mult, ALU.add
                                         ).then_inc(scan_done, 1)
                    v.wait_ge(scan_done, l * 8 + j + 1)
                    if j >= 2:
                        v.wait_ge(xs_ready, l * 8 + j - 1)
                    c = cos[:, j:j + 1, :].broadcast_to([P, 2, T])
                    s = sin[:, j:j + 1, :].broadcast_to([P, 2, T])
                    v.tensor_tensor(ua[:, j % 2, :, :], xt[:, j % 2, :, :], c, ALU.mult)
                    v.tensor_tensor(ub[:, j % 2, :, :], xt[:, j % 2, :, :], s, ALU.mult).then_inc(un_ready, 1)

                def split2(t, size):
                    return t.rearrange("p h (n s k) -> p (h n) s k", s=2, k=size)

                def exponents(n):
                    if n >= 2:
                        v.wait_ge(qk_ready, l * (NSTEP - 1) + n - 1)
                    d = dec[:, n % 2, :, :]
                    b = bc[:, :, :]
                    if n == NSTEP - 2:
                        chunk = lambda t, c: t[:, :, c * CHUNK:(c + 1) * CHUNK]
                        end = lambda c: b[:, :, (c + 1) * CHUNK - 1:(c + 1) * CHUNK].broadcast_to([P, HEADS, CHUNK])
                        v.tensor_tensor(chunk(d, 0), bsum[:, :].unsqueeze(2).broadcast_to([P, HEADS, CHUNK]),
                                        chunk(b, 0), ALU.subtract)
                        v.tensor_tensor(chunk(d, 1), end(1), chunk(b, 1), ALU.subtract)
                        v.tensor_tensor(chunk(d, 3), chunk(b, 3), end(2), ALU.add).then_inc(dec_arg, 1)
                        return
                    size = LEVELS[n]
                    dv, bv = split2(d, size), split2(b, size)
                    ref = bv[:, :, 0, size - 1:size].broadcast_to([P, HEADS * T // (2 * size), size])
                    first = v.tensor_tensor(dv[:, :, 0, :], ref, bv[:, :, 0, :], ALU.subtract)
                    if size < CHUNK:
                        first = v.tensor_tensor(dv[:, :, 1, :], bv[:, :, 1, :], ref, ALU.subtract)
                    first.then_inc(dec_arg, 1)

                def operands(n):
                    v.wait_ge(dec_exp, l * (NSTEP - 1) + n + 1)
                    if n >= 2:
                        v.wait_ge(lev_done, l * NSTEP + n - 1)
                    d, o = dec[:, n % 2, :, :], qk[:, n % 2, :, :]
                    size = P if n == NSTEP - 2 else LEVELS[n]
                    v.tensor_tensor(split2(o, size)[:, :, 0, :], split2(key[:, :, :], size)[:, :, 0, :],
                                    split2(d, size)[:, :, 0, :], ALU.mult)
                    v.tensor_tensor(split2(o, size)[:, :, 1, :], split2(bq[:, :, :], size)[:, :, 1, :],
                                    split2(d, size)[:, :, 1, :], ALU.mult).then_inc(qk_ready, 1)

                def scores(n):
                    v.wait_ge(lev_done, l * NSTEP + n + 1)
                    if n == 0:
                        v.wait_ge(attn_clear, l + 1)
                    if n == NSTEP - 1:
                        v.tensor_copy(attn_x[:, :, :].rearrange("p h t -> p (h t)"), bank(2 * (n % 2))
                                      ).then_inc(lev_read, 1)
                        return
                    if n >= 1:
                        v.wait_ge(lev_read, l * NSTEP + n)
                    v.memset(tick[:, :], 0.0)
                    m = mask[:, n * P:(n + 1) * P].unsqueeze(1).broadcast_to([P, 2 * HEADS, P])
                    v.copy_predicated(attn[:, :, :], m, bank(2 * (n % 2), 2).rearrange("p (i t) -> p i t", t=P)
                                      ).then_inc(lev_read, 1)

                v.wait_ge(rstd_ready, l * 3 + 2)
                take(0, u[:, :, :])
                take(1, bf[:, 0:2, :])
                rotate(0)
                rotate(1)
                take(2, bf[:, 2:4, :])
                rotate(2)
                rotate(3)
                scan(0)
                v.wait_ge(bf_sig, l + 1)
                for hd in range(HEADS):
                    st.mark(v.tensor_scalar(bf[:, hd, :], key[:, hd, :], lbs[:, 6, hd:hd + 1], lbs[:, 5, hd:hd + 1],
                                            ALU.mult, ALU.add))
                st.wait()
                st.mark(v.tensor_scalar(key[:, :, :], bf[:, :, :], -1.0, 1.0, ALU.mult, ALU.add))
                st.wait()
                v.tensor_scalar(bf[:, :, :], bf[:, :, :], 2.0 ** -63, None, ALU.max).then_inc(bf_f, 1)
                scan(1)
                take(3, bq[:, 0:2, :])
                rotate(4)
                v.wait_ge(bf_log, l + 1)
                st.mark(v.tensor_tensor_scan(bc[:, :, :].rearrange("p h t -> p (h t)"), carry,
                                             bf[:, :, :].rearrange("p h t -> p (h t)"), 0.0, ALU.mult, ALU.add))
                rotate(5)
                st.wait()
                st.mark(v.tensor_tensor(bsum[:, :].unsqueeze(2), bc[:, :, CHUNK - 1:CHUNK],
                                        bc[:, :, 2 * CHUNK - 1:2 * CHUNK], ALU.add))
                scan(2)
                take(4, bq[:, 2:4, :])
                st.wait()
                exponents(0)
                exponents(1)
                rotate(6)
                scan(3)
                rotate(7)
                v.wait_ge(bf_f, l + 1)
                v.wait_ge(proj_dve, l * 9 + 5)
                operands(0)
                take(5, fqk[:, 0, :, :])
                operands(1)
                exponents(2)
                scores(0)
                scan(4)
                take(6, fqk[:, 1, :, :])
                v.wait_ge(af_done, l + 1)
                st.mark(v.tensor_tensor(fl[:, 0, :], bank(7)[0:4, 0:T], rstd[0:4, :], ALU.mult))
                st.wait()
                st.mark(v.tensor_scalar(fl[:, 0, :], fl[:, 0, :], prm("f_bias")[0:4, :], None, ALU.add))
                st.wait()
                st.mark(v.tensor_scalar(fl[:, 1, :], fl[:, 0, :], -1.0, None, ALU.mult))
                st.wait()
                v.tensor_tensor(fl[:, 1, :], fl[:, 1, :], fl[:, 0, :], ALU.max).then_inc(af_abs, 1)
                operands(2)
                exponents(3)
                scores(1)
                scan(5)
                v.wait_ge(af_ln, l + 1)
                st.mark(v.tensor_scalar(fl[:, 0, :], fl[:, 0, :], 0.0, None, ALU.min))
                st.wait()
                st.mark(v.tensor_tensor(fl[:, 0, :], fl[:, 0, :], fl[:, 1, :], ALU.subtract))
                st.wait()
                st.mark(v.tensor_tensor_scan(fl[:, 2, :], ones[0:4, 0:1].broadcast_to([4, T]), fl[:, 0, :], 0.0, ALU.mult, ALU.add))
                st.wait()
                v.tensor_scalar(fl[:, 3, :], fl[:, 2, :], -1.0, None, ALU.mult).then_inc(cum_ready, 1)
                operands(3)
                exponents(4)
                scores(2)
                scan(6)
                st.mark(v.tensor_scalar(fst[:, 0, 0:1], prm("q_gain"), FOX_DIM ** -0.5, None, ALU.mult))
                st.wait()
                for w in range(2):
                    v.wait_ge(frn_ready, l * 2 + w + 1)
                    t = fqk[:, w, :, :].rearrange("p a t -> p (a t)")
                    v.scalar_tensor_tensor(t, t, fst[:, 0, 0:1] if w == 0 else prm("k_gain"), fsq[:, w, :],
                                           ALU.mult, ALU.mult).then_inc(fqk_ready, 1)
                def fox_mask(t):
                    v.wait_ge(sc_done, l * 2 + 2 - t)
                    at, n = t * P, (t + 1) * P
                    for odd in range(2):
                        last = v.tensor_tensor(sc[:, odd:4:2, at:at + n],
                                               bank(6 + odd)[:, 0:2 * n].rearrange("p (h s) -> p h s", h=2),
                                               cmask[:, at:at + n].unsqueeze(1).broadcast_to([P, 2, n]), ALU.add)
                    last.then_inc(sc_read, 1)
                    v.wait_ge(sc_read, l * 2 + 2 - t)
                    st.mark(v.tensor_reduce(fst[:, 0, t * 4:t * 4 + 4], sc[:, :, at:at + n], AX.X, ALU.max))
                    st.wait()
                    v.tensor_scalar(fst[:, 1, t * 4:t * 4 + 4], fst[:, 0, t * 4:t * 4 + 4], -1.0, None, ALU.mult
                                    ).then_inc(max_ready, 1)

                def fox_probabilities(t):
                    v.wait_ge(exp_done, l * 8 + 8 - 4 * t)
                    at, n = t * P, (t + 1) * P
                    st.mark(v.reciprocal(fst[:, 3, t * 4:t * 4 + 4], fst[:, 2, t * 4:t * 4 + 4]))
                    st.wait()
                    v.tensor_tensor(sc[:, :, at:at + n], sc[:, :, at:at + n],
                                    fst[:, 3, t * 4:t * 4 + 4].unsqueeze(2).broadcast_to([P, 4, n]), ALU.mult
                                    ).then_inc(p_ready, 1)

                operands(4)
                exponents(5)
                scores(3)
                scan(7)
                operands(5)
                exponents(6)
                fox_mask(1)
                operands(6)
                exponents(7)
                scores(4)
                fox_probabilities(1)
                v.wait_ge(y_done, l + 1)
                for m in range(2):
                    last = v.scalar_tensor_tensor(y[:, m, :], u[:, m, :], prm("skip", m, 1),
                                                  bank(4)[:, m * T:(m + 1) * T], ALU.mult, ALU.add)
                last.then_inc(y_ready, 1)
                scores(5)
                fox_mask(0)
                operands(7)
                fox_probabilities(0)
                take(10, bg[:, 0:2, :])
                scores(6)
                v.wait_ge(pt_done, l * 2 + 1)
                v.tensor_copy(pT.rearrange("p (h c) -> p h c", c=384)[:, 2:4, P:384],
                              bank(7).rearrange("p (h c) -> p h c", c=T)).then_inc(pt_dve, 1)
                scores(7)
                scores(8)
                v.wait_ge(sg_ready, l + 1)
                v.tensor_tensor(s5_out, z, y, ALU.mult).then_inc(mix_s5, 1)
                take(11, bg[:, 2:4, :])
                v.wait_ge(orn_ready, l + 1)
                st.mark(v.tensor_tensor(orn[:, :], bank(0, 2), osq[:, :], ALU.mult))
                v.wait_ge(bg_ready, l + 1)
                st.wait()
                for hd in range(HEADS):
                    last = v.scalar_tensor_tensor(h[:, 2 + hd, :], orn[:, hd * T:(hd + 1) * T], prm("o_gain", hd, 1),
                                                  bg[:, hd, :], ALU.mult, ALU.mult)
                last.then_inc(mix_hgrn, 1)
                st.close()

                split_lo(l * SPLIT_UNITS + FFN_UNITS, 0)
                split_lo(l * SPLIT_UNITS + FFN_UNITS + 1, 1)

                def wait_out(m):
                    if m % 2 == 0:
                        v.wait_ge(direct_done, l * DIRECT_UNITS + IN_UNITS + m // 2 + 1)
                boundary(wait_out, 1.0, l * 2 + 1, prm("gain_ffn2"),
                         lambda m: out_bank(m // 2)[:, (m % 2) * T:(m % 2 + 1) * T])
                ffn_steps(l * 2 + 1, l * SPLIT_UNITS + FFN_UNITS, l * 3 + 2, True)

                def wait_ffn2(m):
                    if m < KT - 2:
                        v.wait_ge(acc_done, l * 6 + 3 + m // 2 + 1)
                    else:
                        v.wait_ge(units_done, l * SPLIT_UNITS + 2 * FFN_UNITS + RING)
                boundary(wait_ffn2, 0.5, l * 2 + 2, prm("gain_next"))


def _tiles(w, cols):
    k = w.shape[0] // P
    return w.reshape(k, P, cols // 256, 256).transpose(2, 1, 0, 3).reshape(cols // 256, P, k * 256)


def _unit_stream(inputs, l):
    def ffn(name):
        g = _tiles(inputs[name + "_w_gate"][l], FF)
        u = _tiles(inputs[name + "_w_up"][l], FF)
        d = inputs[name + "_w_down"][l].reshape(ITERS, 2, P, D).transpose(0, 2, 1, 3).reshape(ITERS, P, 2 * D)
        order = [g[0], u[0]]
        for i in range(1, ITERS):
            order += [g[i], u[i], d[i - 1]]
        return order + [d[ITERS - 1]]

    w = inputs["w_in"][l]
    a = FOX_HEADS * FOX_DIM
    b = 3 * a + FOX_HEADS
    parts = {"q": w[:, 0:a], "k": w[:, a:2 * a], "v": w[:, 2 * a:3 * a], "bq": w[:, b:b + 512],
             "bf": w[:, b + 512:b + 1024], "bi": w[:, b + 1024:b + 1536], "bg": w[:, b + 1536:b + 2048],
             "u": w[:, b + 2048:b + 2304]}
    cols = np.concatenate([parts[n] for n in ("u", "bf", "bq", "q", "k", "bi", "v", "bg")], axis=1)
    w_in = list(_tiles(cols, IN_UNITS * 256))
    w_out = list(_tiles(inputs["w_out"][l], D))
    return ffn("ffn1") + w_in + w_out + ffn("ffn2")


def _params(inputs, l):
    par = np.zeros((P, NPAR), np.float32)

    def put(name, a):
        at, n = COLS[name]
        par[:a.shape[0], at:at + n] = a

    def cols(v):
        return v.reshape(-1, P).T

    put("gain_mix", cols(inputs["mix_norm"][l]))
    put("gain_ffn2", cols(inputs["ffn2_norm"][l]))
    put("gain_next", cols(inputs["ffn1_norm"][(l + 1) % DEPTH]))
    put("lam_re", cols(inputs["s5_lambda_re"][l].reshape(-1)))
    put("lam_im", cols(inputs["s5_lambda_im"][l].reshape(-1)))
    put("log_step", cols(np.repeat(inputs["s5_log_step"][l], STATE)))
    put("lb_logit", np.concatenate([cols(inputs["hgrn_lb"][d]) for d in range(DEPTH)], axis=1))
    put("later_layer", np.full((P, 1), 1.0 if l else 0.0, np.float32))
    put("o_gain", cols(inputs["hgrn_o_gain"][l]))
    put("skip", cols(inputs["s5_D"][l]))
    put("glu_b", cols(inputs["s5_glu_b"][l]))
    put("q_gain", np.tile(inputs["fox_q_gain"][l], 2)[:, None])
    put("k_gain", np.tile(inputs["fox_k_gain"][l], 2)[:, None])
    put("f_bias", inputs["fox_f_bias"][l][:, None])
    forget = inputs["w_in"][l][:, 3 * 256:3 * 256 + FOX_HEADS]
    put("w_forget", forget.reshape(KT, P, FOX_HEADS).transpose(1, 0, 2).reshape(P, -1))
    put("glu_w", inputs["s5_glu_w"][l].reshape(2, P, 256).transpose(1, 0, 2).reshape(P, -1))
    for name, src in (("b_re", "s5_B_re"), ("b_im", "s5_B_im")):
        w = inputs[src][l]
        a = np.zeros((P, 2, P), np.float32)
        for g in range(GROUPS):
            r, c = (g * GROUP) % P, (g % 2) * STATE
            a[r:r + GROUP, g // 8, c:c + STATE] = w[g].T
        put(name, a.reshape(P, -1))
    for name, src in (("c_re", "s5_C_re"), ("c_im", "s5_C_im")):
        w = inputs[src][l]
        a = np.zeros((P, S5_TILES, 32), np.float32)
        for g in range(GROUPS):
            r, c = (g % 2) * STATE, (g % 2) * GROUP
            a[r:r + STATE, g // 2, c:c + GROUP] = w[g].T
        put(name, a.reshape(P, -1))
    return par


def _constants():
    i = np.arange(P)
    causal = np.where(i[:, None] >= i[None, :], 0.0, -1e30)
    carry = np.tile((np.arange(HEADS * T) % CHUNK != 0).astype(np.float32), (P, 1))
    con = np.concatenate([np.eye(P), np.ones((P, P)), (i[:, None] // 64 == i[None, :] // 64),
                          causal, np.zeros((P, P)), causal, carry], axis=1).astype(np.float32)
    select = np.repeat(np.eye(4, dtype=np.float32), T, axis=1)
    masks = []
    for size in LEVELS:
        masks.append((i[:, None] // (2 * size) == i[None, :] // (2 * size))
                     & (i[:, None] % (2 * size) < size) & (i[None, :] % (2 * size) >= size))
    masks.append(i[:, None] == i[None, :])
    return con, select, np.stack(masks, axis=1).astype(np.float32)


def kernel(**inputs):
    import concourse.bacc as bacc
    from concourse.bass_utils import run_bass_kernel_spmd

    inputs = {k: np.asarray(v) for k, v in inputs.items()}
    con, select, masks = _constants()
    arrays = {
        "xT": np.ascontiguousarray(inputs["x"][0].T.reshape(KT, P, T).transpose(1, 0, 2)),
        "stream": np.stack([u for l in range(DEPTH) for u in _unit_stream(inputs, l)]
                           + [np.zeros((P, 2048), np.float32)] * AHEAD),
        "params": np.stack([_params(inputs, l) for l in range(DEPTH)]),
        "gain0": np.ascontiguousarray(inputs["ffn1_norm"][0].reshape(-1, P).T),
        "consts": con, "select": select, "masks": masks,
    }
    nc = bacc.Bacc("TRN2", target_bir_lowering=False, num_devices=1)
    args = {n: nc.dram_tensor(n, a.shape, mybir.dt.from_np(a.dtype), kind="ExternalInput").ap()
            for n, a in arrays.items()}
    out = nc.dram_tensor("out", (P, KT, T), F32, kind="ExternalOutput").ap()
    build(nc, out=out, **args)
    got = run_bass_kernel_spmd(nc, [arrays], core_ids=[0]).results[0]["out"]
    return np.ascontiguousarray(got.transpose(1, 0, 2).reshape(D, T).T)[None]
```

```python
from contextlib import ExitStack

import numpy as np

import concourse.bass as bass
from concourse import mybir

F32 = mybir.dt.float32
F32R = mybir.dt.float32r
U8 = mybir.dt.uint8
ALU = mybir.AluOpType
ACT = mybir.ActivationFunctionType
AX = mybir.AxisListType

P = 128
DEPTH = 2
T = 256
D = 1024
KT = D // P
FF = 2816
ITERS = FF // 256
FOX_HEADS, FOX_DIM = 4, 64
HEADS = 4
GROUPS, GROUP, STATE = 16, 16, 64
S5_TILES = GROUPS * STATE // P
CHUNK = 64
EPS = 1e-6

FFN_UNITS = 3 * ITERS
IN_UNITS = 12
OUT_UNITS = 4
UNITS = 2 * FFN_UNITS + IN_UNITS + OUT_UNITS
SPLIT_UNITS = 2 * FFN_UNITS
QUARTERS = 4
IN_QUARTERS = QUARTERS * IN_UNITS
POOL_UNITS = (2, 4, 5, 6, 7, 8, 9, 10, 11)
DVE_UNITS = tuple(n for n in range(IN_UNITS) if n not in POOL_UNITS)
RING = 3
AHEAD = 2
VISITS = UNITS // RING

COLS = {}
_at = 0
for _name, _n in [("gain_mix", KT), ("gain_ffn2", KT), ("gain_next", KT), ("lam_re", S5_TILES),
                  ("lam_im", S5_TILES), ("log_step", S5_TILES), ("lb_logit", 2 * HEADS), ("later_layer", 1),
                  ("o_gain", HEADS), ("skip", 2), ("glu_b", 2), ("q_gain", 1), ("k_gain", 1), ("f_bias", 1),
                  ("w_forget", KT * FOX_HEADS), ("b_re", 2 * P), ("b_im", 2 * P),
                  ("c_re", S5_TILES * 32), ("c_im", S5_TILES * 32), ("glu_w", 512)]:
    COLS[_name] = (_at, _n)
    _at += _n
NPAR = _at

LEVELS = [64, 32, 16, 8, 4, 2, 1]
NLEV = len(LEVELS) + 1
NSTEP = NLEV + 1

TWO_PI = 2.0 * np.pi
PI_A = 6.28125
PI_B = float(np.float32(np.round((TWO_PI - PI_A) * 2.0 ** 22) / 2.0 ** 22))
PI_C = float(np.float32(TWO_PI - PI_A - PI_B))
ROUND = 1.5 * 2.0 ** 23


class Steps:

    def __init__(self, engine, sem, layer, per_layer):
        self.engine, self.sem, self.base, self.per_layer, self.n = engine, sem, layer * per_layer, per_layer, 0

    def mark(self, instruction):
        self.n += 1
        return instruction.then_inc(self.sem, 1)

    def wait(self):
        if self.n:
            self.engine.wait_ge(self.sem, self.base + self.n)

    def close(self):
        assert self.n == self.per_layer, f"{self.n} steps in a layer, not {self.per_layer}"


DVE_STEPS = 49
POOL_STEPS = 61


def build(nc, xT, stream, params, gain0, consts, masks, out):
    ctx = ExitStack()
    with ctx:
        def sb(name, shape, dt=F32, where=ctx):
            return where.enter_context(nc.sbuf_tensor(name, shape, dt))

        def sem(name):
            return ctx.enter_context(nc.semaphore(name))

        raw = [sb(f"raw{s}", [P, 2048]) for s in range(RING)]
        x = sb("x", [P, KT, T])
        h_hi = sb("h_hi", [P, KT, T], F32R)
        h_lo = sb("h_lo", [P, KT, T], F32R)
        in_hi = [sb(f"in_hi{s}", [P, 512], F32R) for s in range(QUARTERS)]
        in_lo = [sb(f"in_lo{s}", [P, 512], F32R) for s in range(QUARTERS)]
        forget_hi = sb("forget_hi", [P, KT * FOX_HEADS], F32R)
        forget_lo = sb("forget_lo", [P, KT * FOX_HEADS], F32R)
        sq = sb("sq", [P, 4, T])
        sumsq = sb("sumsq", [P, T])
        ln_ms = sb("ln_ms", [P, T])
        rstd = sb("rstd", [P, T])
        rstd_tok = sb("rstd_tok", [P, 4])
        par = sb("par", [P, NPAR])
        g0 = sb("g0", [P, KT])
        con = sb("con", [P, 3 * P + 384 + T])
        mask = sb("mask", [P, NLEV * P], U8)
        eps = sb("eps", [P, 1])
        cos = sb("cos", [P, S5_TILES, T])
        sin = sb("sin", [P, S5_TILES, T])
        trig_tmp = sb("trig_tmp", [P, S5_TILES, P])
        rot = sb("rot", [P, 2, 2, S5_TILES])
        mag = sb("mag", [P, S5_TILES])
        coef = sb("coef", [P, 3, S5_TILES])
        s5s = sb("s5s", [P, 12, S5_TILES])
        c_out = sb("c_out", [P, 2, S5_TILES * 32])
        lbs = sb("lbs", [P, 8, HEADS])
        tick = sb("tick", [P, 1])
        zero = sb("zero", [P, 512], F32R)

        ffn_mem = ExitStack()
        hi = [sb(f"hi{s}", [P, 2048], F32R, ffn_mem) for s in range(RING)]
        lo = [sb(f"lo{s}", [P, 2048], F32R, ffn_mem) for s in range(RING)]
        xg_hi = sb("xg_hi", [P, KT, T], F32R, ffn_mem)
        xg_lo = sb("xg_lo", [P, KT, T], F32R, ffn_mem)
        gate = sb("gate", [P, 2, T], F32, ffn_mem)
        up = sb("up", [P, 2, T], F32, ffn_mem)
        silu = sb("silu", [P, 2, T], F32, ffn_mem)
        act = sb("act", [P, 2, T], F32, ffn_mem)
        act_hi = [sb(f"act_hi{s}", [P, 2, T], F32R, ffn_mem) for s in range(2)]
        act_lo = [sb(f"act_lo{s}", [P, 2, T], F32R, ffn_mem) for s in range(2)]
        ffn_mem.close()

        bf = sb("bf", [P, HEADS, T])
        key = sb("key", [P, HEADS, T])
        bq = sb("bq", [P, HEADS, T])
        bc = sb("bc", [P, HEADS, T])
        bsum = sb("bsum", [P, HEADS])
        dec = sb("dec", [P, 2, HEADS, T])
        qk = sb("qk", [P, 2, HEADS, T])
        attn = sb("attn", [P, 2 * HEADS, P])
        attn_x = sb("attn_x", [P, HEADS, P])
        v_b = sb("v_b", [P, 2, 512])
        bg = sb("bg", [P, HEADS, T])
        osq = dec[:, 0, :, :].rearrange("p h t -> p (h t)")
        orn = dec[:, 1, :, :].rearrange("p h t -> p (h t)")
        u = sb("u", [P, 2, T])
        s5b = sb("s5b", [P, 4, 2, T])
        xs = sb("xs", [P, S5_TILES, 2, T])
        y = trig_tmp[:, 0:4, :].rearrange("p (a b) t -> p a (b t)", a=2)
        z = trig_tmp[:, 4:8, :].rearrange("p (a b) t -> p a (b t)", a=2)
        fqk = sb("fqk", [P, 2, 2, T])
        fsq = sb("fsq", [P, 2, 2 * T])
        s5a = sb("s5a", [P, 4, 2, T])
        fv = sb("fv", [P, 2, 256])
        fl = sb("fl", [4, 4, T])
        fox_out = fsq[:, 0, :].rearrange("p (a t) -> p a t", a=2)
        s5_out = y
        sc = sb("sc", [P, FOX_HEADS, 384])
        raw.append(s5a[:, :, :, :].rearrange("p j a t -> p (j a t)"))
        pT = xs[:, 0:3, :, :].rearrange("p j a t -> p (j a t)")
        fst = sb("fst", [P, 4, 8])

        ps = ctx.enter_context(nc.psum_tensor("ps", [P, 8 * 512], F32))

        def bank(b, n=1):
            return ps[:, b * 512:(b + n) * 512]

        def out_bank(n):
            return bank((n + 2) % 4)

        ident = con[:, 0:P]

        def head_row(hd, n):
            return ident[0:4, hd:hd + 1].broadcast_to([4, n])

        ones = con[:, P:2 * P]
        halves = con[:, 2 * P:3 * P]
        cmask = con[:, 3 * P:3 * P + 384]
        carry = con[:, 3 * P + 384:]

        def prm(name, a=0, n=None):
            at, size = COLS[name]
            return par[:, at + a:at + (size if n is None else a + n)]

        hgrn_out = cos[:, 0:HEADS, :]

        def in_split_count(l, n, part):
            units = POOL_UNITS if n in POOL_UNITS else DVE_UNITS
            return (l * len(units) + units.index(n)) * QUARTERS + part + 1

        raw_loaded = [sem(f"raw_loaded{s}") for s in range(4)]
        consts_loaded = sem("consts_loaded")
        x_loaded = [sem("x_loaded0"), sem("x_loaded1")]
        par_loaded = sem("par_loaded")
        hi_written = sem("hi_written")
        lo_written = sem("lo_written")
        units_done = sem("units_done")
        in_hi_written = sem("in_hi_written")
        in_lo_dve = sem("in_lo_dve")
        in_lo_pool = sem("in_lo_pool")
        in_used = sem("in_used")
        out_unit_done = sem("out_unit_done")
        forget_split = sem("forget_split")
        forget_ready = sem("forget_ready")
        xg_hi_ready = sem("xg_hi_ready")
        xg_lo_ready = sem("xg_lo_ready")
        h_hi_ready = sem("h_hi_ready")
        h_lo_ready = sem("h_lo_ready")
        sq_ready = sem("sq_ready")
        sumsq_added = sem("sumsq_added")
        sums_done = sem("sums_done")
        rstd_ready = sem("rstd_ready")
        rstd_steps = sem("rstd_steps")
        x_ready = sem("x_ready")
        acc_done = sem("acc_done")
        gate_scaled = sem("gate_scaled")
        gu_read = sem("gu_read")
        silu_done = sem("silu_done")
        act_ready = sem("act_ready")
        act_hi_ready = sem("act_hi_ready")
        act_lo_ready = sem("act_lo_ready")
        out_stored = sem("out_stored")
        mask_ready = sem("mask_ready")
        zeros_set = sem("zeros_set")
        once = sem("once")
        s5_dt = sem("s5_dt")
        s5_args = sem("s5_args")
        s5_funs = sem("s5_funs")
        s5_coef = sem("s5_coef")
        pool_step = sem("pool_step")
        tables_ready = sem("tables_ready")
        dve_step = sem("dve_step")
        proj_dve = sem("proj_dve")
        proj_act = sem("proj_act")
        bf_sig = sem("bf_sig")
        bf_f = sem("bf_f")
        bf_log = sem("bf_log")
        dec_arg = sem("dec_arg")
        dec_exp = sem("dec_exp")
        qk_ready = sem("qk_ready")
        lev_done = sem("lev_done")
        lev_read = sem("lev_read")
        attn_clear = sem("attn_clear")
        bu_done = sem("bu_done")
        bu_read = sem("bu_read")
        xin_ready = sem("xin_ready")
        scan_done = sem("scan_done")
        un_ready = sem("un_ready")
        xs_ready = sem("xs_ready")
        y_done = sem("y_done")
        y_ready = sem("y_ready")
        z_ready = sem("z_ready")
        glu_done = sem("glu_done")
        sg_ready = sem("sg_ready")
        mix_s5 = sem("mix_s5")
        fsq_ready = sem("fsq_ready")
        fsum_done = sem("fsum_done")
        frn_ready = sem("frn_ready")
        fln = sem("fln")
        fqk_ready = sem("fqk_ready")
        af_done = sem("af_done")
        af_abs = sem("af_abs")
        af_exp = sem("af_exp")
        af_ln = sem("af_ln")
        cum_ready = sem("cum_ready")
        sc_done = sem("sc_done")
        sc_read = sem("sc_read")
        max_ready = sem("max_ready")
        exp_done = sem("exp_done")
        p_ready = sem("p_ready")
        pt_done = sem("pt_done")
        pt_act = sem("pt_act")
        pt_dve = sem("pt_dve")
        fo_done = sem("fo_done")
        mix_fox = sem("mix_fox")
        o_done = sem("o_done")
        osq_ready = sem("osq_ready")
        osum_done = sem("osum_done")
        oln = sem("oln")
        orn_ready = sem("orn_ready")
        bg_ready = sem("bg_ready")
        mix_hgrn = sem("mix_hgrn")

        block = ctx.enter_context(nc.Block())

        @block.sync
        def _(sp):
            sp.dma_start(g0[:, :], gain0).then_inc(x_loaded[0], 16)
            sp.dma_start(x[:, 0:KT // 2, :], xT[:, 0:KT // 2, :]).then_inc(x_loaded[0], 16)
            sp.dma_start(x[:, KT // 2:, :], xT[:, KT // 2:, :]).then_inc(x_loaded[1], 16)

            def load(n, slot):
                sp.dma_start(raw[slot][:, :], stream[bass.ds(n, 1), :, :].rearrange("o p c -> p (o c)")
                             ).then_inc(raw_loaded[slot], 16)

            def load_split(n, at, slot):
                sp.wait_ge(hi_written, n + 1)
                sp.wait_ge(lo_written, n + 1)
                load(at, slot)

            for p in range(AHEAD):
                load(p, p)
            with sp.Fori(0, DEPTH) as l:
                def wait_in_split(n):
                    sp.wait_ge(in_lo_pool if n in POOL_UNITS else in_lo_dve, in_split_count(l, n, QUARTERS - 1))

                load_split(l * SPLIT_UNITS + 2, l * UNITS + 2, 2)
                with sp.Fori(1, ITERS) as i:
                    for p in range(RING):
                        load_split(l * SPLIT_UNITS + i * 3 + p, l * UNITS + i * 3 + p, p)
                for w in range(IN_UNITS):
                    if w < RING:
                        sp.wait_ge(hi_written, l * SPLIT_UNITS + FFN_UNITS + w + 1)
                        sp.wait_ge(lo_written, l * SPLIT_UNITS + FFN_UNITS + w + 1)
                    else:
                        wait_in_split(w - RING)
                    load(l * UNITS + FFN_UNITS + w, w % RING)
                for w in range(OUT_UNITS):
                    if w < RING:
                        wait_in_split(IN_UNITS - RING + w)
                    else:
                        sp.wait_ge(xs_ready, l * 8 + 8)
                    load(l * UNITS + FFN_UNITS + IN_UNITS + w, w)
                for p in range(RING):
                    sp.wait_ge(out_unit_done, l * OUT_UNITS + p + 1)
                    load(l * UNITS + FFN_UNITS + IN_UNITS + OUT_UNITS + p, p)
                with sp.Fori(1, ITERS) as i:
                    for p in range(RING):
                        load_split(l * SPLIT_UNITS + FFN_UNITS + i * 3 + p,
                                   l * UNITS + FFN_UNITS + IN_UNITS + OUT_UNITS + i * 3 + p, p)
                for p in range(AHEAD):
                    load_split((l + 1) * SPLIT_UNITS + p, (l + 1) * UNITS + p, p)
            for m in range(KT):
                sp.wait_ge(x_ready, 24 * (DEPTH - 1) + 16 + m + 1)
                sp.dma_start(out[:, m, :], x[:, m, :]).then_inc(out_stored, 16)
            sp.wait_ge(out_stored, 16 * KT)

        @block.gpsimd
        def _(pool):
            pool.memset(eps[:, :], EPS).then_inc(once, 1)
            pool.memset(tick[:, :], 0.0).then_inc(gu_read, 1)
            pool.memset(cos[:, :, 0:1], 1.0).then_inc(hi_written, RING)
            pool.memset(sin[:, :, 0:1], 0.0).then_inc(lo_written, RING)
            pool.memset(lbs[:, 7, :], 0.0).then_inc(units_done, RING)
            pool.memset(coef[:, 0, :], 0.0).then_inc(in_used, QUARTERS)
            pool.wait_ge(x_loaded[0], 32)
            pool.dma_start(con[:, :], consts).then_inc(consts_loaded, 16)
            pool.dma_start(trig_tmp[:, :, :], masks).then_inc(consts_loaded, 16)

            def sum_squares(norm, first=False):
                for m in range(1, KT):
                    pool.wait_ge(sq_ready, norm * KT + m + 1)
                    if m == 1:
                        if not first:
                            pool.wait_ge(sums_done, norm)
                        a = sq[:, 0, :]
                    else:
                        pool.wait_ge(sumsq_added, norm * 7 + m - 1)
                        a = sumsq[:, :]
                    pool.tensor_tensor(sumsq[:, :], a, sq[:, m % 4, :], ALU.add).then_inc(sumsq_added, 1)

            sum_squares(0, first=True)
            with pool.Fori(0, DEPTH) as l:
                steps = Steps(pool, pool_step, l, POOL_STEPS)
                pool.wait_ge(s5_coef, l + 1)
                n, r = 1, 0
                while n < T:
                    pc, psn = rot[:, r, 0, :], rot[:, r, 1, :]
                    wide_c = pc.unsqueeze(2).broadcast_to([P, S5_TILES, n])
                    wide_s = psn.unsqueeze(2).broadcast_to([P, S5_TILES, n])
                    tmp = trig_tmp[:, :, 0:n]
                    steps.wait()
                    pool.tensor_tensor(cos[:, :, n:2 * n], cos[:, :, 0:n], wide_c, ALU.mult)
                    pool.tensor_tensor(tmp, sin[:, :, 0:n], wide_s, ALU.mult)
                    steps.mark(pool.tensor_tensor(sin[:, :, n:2 * n], sin[:, :, 0:n], wide_c, ALU.mult))
                    steps.wait()
                    steps.mark(pool.tensor_tensor(cos[:, :, n:2 * n], cos[:, :, n:2 * n], tmp, ALU.subtract))
                    steps.wait()
                    steps.mark(pool.tensor_tensor(tmp, cos[:, :, 0:n], wide_s, ALU.mult))
                    steps.wait()
                    steps.mark(pool.tensor_tensor(sin[:, :, n:2 * n], sin[:, :, n:2 * n], tmp, ALU.add))
                    if 2 * n == T:
                        break
                    qc, qs = rot[:, 1 - r, 0, :], rot[:, 1 - r, 1, :]
                    t1 = s5s[:, 11, :]
                    steps.mark(pool.tensor_tensor(qc, pc, pc, ALU.mult))
                    pool.tensor_tensor(t1, psn, psn, ALU.mult)
                    steps.mark(pool.tensor_tensor(qs, pc, psn, ALU.mult))
                    steps.wait()
                    steps.mark(pool.tensor_tensor(qc, qc, t1, ALU.subtract))
                    steps.mark(pool.tensor_tensor(qs, qs, qs, ALU.add))
                    n, r = 2 * n, 1 - r
                cr = prm("c_re").rearrange("p (j c) -> p j c", c=32)
                ci = prm("c_im").rearrange("p (j c) -> p j c", c=32)
                kr = coef[:, 0, :].unsqueeze(2).broadcast_to([P, S5_TILES, 32])
                ki = coef[:, 1, :].unsqueeze(2).broadcast_to([P, S5_TILES, 32])
                minus_ki = coef[:, 2, :].unsqueeze(2).broadcast_to([P, S5_TILES, 32])
                o_re = c_out[:, 0, :].rearrange("p (j c) -> p j c", c=32)
                o_im = c_out[:, 1, :].rearrange("p (j c) -> p j c", c=32)
                tmp = trig_tmp[:, :, 0:32]
                tmp2 = trig_tmp[:, :, 32:64]
                steps.wait()
                pool.tensor_tensor(o_re, cr, kr, ALU.mult)
                pool.tensor_tensor(tmp, ci, ki, ALU.mult)
                pool.tensor_tensor(o_im, cr, minus_ki, ALU.mult)
                steps.mark(pool.tensor_tensor(tmp2, ci, kr, ALU.mult))
                steps.wait()
                pool.tensor_tensor(o_re, o_re, tmp, ALU.subtract)
                pool.tensor_tensor(o_im, o_im, tmp2, ALU.subtract).then_inc(tables_ready, 1)
                steps.close()

                sum_squares(l * 3 + 1)
                def rotated(j):
                    pool.wait_ge(bu_read, l * 8 + j + 1)
                    a, b = s5a[:, j % 4, :, :], s5b[:, j % 4, :, :]
                    pool.tensor_tensor(a[:, 0, :], a[:, 0, :], b[:, 1, :], ALU.add)
                    pool.tensor_tensor(a[:, 1, :], a[:, 1, :], b[:, 0, :], ALU.subtract).then_inc(xin_ready, 1)

                def rotated_back(j):
                    pool.wait_ge(un_ready, l * 8 + j + 1)
                    a, b = s5a[:, j % 4, :, :], s5b[:, j % 4, :, :]
                    pool.tensor_tensor(xs[:, j, 0, :], a[:, 0, :], b[:, 1, :], ALU.subtract)
                    pool.tensor_tensor(xs[:, j, 1, :], b[:, 0, :], a[:, 1, :], ALU.add).then_inc(xs_ready, 1)

                quarter = iter([(n, part) for n in POOL_UNITS for part in range(QUARTERS)])

                def split_in(count):
                    for n, part in (next(quarter) for _ in range(count)):
                        pool.wait_ge(in_hi_written, l * IN_QUARTERS + n * QUARTERS + part + 1)
                        pool.tensor_tensor(in_lo[part][:, :], raw[n % RING][:, part * 512:(part + 1) * 512],
                                           in_hi[part][:, :].bitcast(F32), ALU.subtract).then_inc(in_lo_pool, 1)

                split_in(4)
                pool.wait_ge(sums_done, l * 3 + 2)
                none = cmask[:, P:2 * P].unsqueeze(1).broadcast_to([P, 2 * HEADS, P])
                pool.tensor_tensor(attn[:, :, :], none, none, ALU.add).then_inc(attn_clear, 1)
                rotated(0)
                rotated(1)
                split_in(1)
                rotated(2)
                split_in(2)
                rotated(3)
                split_in(1)
                rotated_back(0)
                split_in(2)
                rotated_back(1)
                split_in(3)
                rotated_back(2)
                split_in(1)
                rotated(4)
                split_in(1)
                rotated(5)
                split_in(2)
                rotated_back(3)
                split_in(4)
                rotated(6)
                split_in(1)
                rotated(7)
                split_in(3)
                rotated_back(4)
                split_in(1)
                rotated_back(5)
                split_in(2)
                rotated_back(6)
                split_in(2)
                rotated_back(7)
                split_in(6)

                sum_squares(l * 3 + 2)
                sum_squares(l * 3 + 3)

        @block.scalar
        def _(e):
            def square(norm, m, first=False):
                if not first or m >= 4:
                    e.wait_ge(sumsq_added, norm * 7 + (m - 4 if m > 5 else 1 if m >= 4 else 0))
                e.activation(sq[:, m % 4, :], x[:, m, :], ACT.Square).then_inc(sq_ready, 1)

            def boundary(norm, hi_at, wait_x, gain):
                for m in range(KT):
                    wait_x(m)
                    if hi_at is None:
                        e.activation(h_hi[:, m, :], x[:, m, :], ACT.Copy, scale=gain[:, m:m + 1]
                                     ).then_inc(h_hi_ready, 1)
                    else:
                        e.activation(xg_hi[:, m, :], x[:, m, :], ACT.Copy, scale=gain[:, m:m + 1]
                                     ).then_inc(xg_hi_ready, 1)
                    square(norm, m)

            def split_hi(n, visit, slot):
                e.wait_ge(raw_loaded[slot], (visit + 1) * 16)
                e.wait_ge(units_done, n + 1)
                e.activation(hi[slot][:, :], raw[slot][:, :], ACT.Copy).then_inc(hi_written, 1)

            def ffn_start(n0, v0, norm, rstd_step):
                split_hi(n0 + 2, v0, 2)
                e.wait_ge(sums_done, norm + 1)
                e.activation(ln_ms[:, :], bank(7)[:, 0:T], ACT.Ln, scale=1.0 / D, bias=eps[:, :]
                             ).then_inc(rstd_steps, 1)
                e.wait_ge(rstd_steps, rstd_step)
                e.activation(rstd[:, :], ln_ms[:, :], ACT.Exp, scale=-0.5).then_inc(rstd_ready, 1)
                split_hi(n0 + 3, v0 + 1, 0)

            def ffn_steps(f, n0, v0, ahead, between=lambda: None):
                def gated(i, odd, after_silu=lambda: None, first=False):
                    e.wait_ge(gate_scaled, f * ITERS + i + 1)
                    e.activation(silu[:, :, :], gate[:, :, :], ACT.Silu).then_inc(silu_done, 1)
                    after_silu()
                    e.wait_ge(act_ready, f * ITERS + i + 1)
                    if not first:
                        e.wait_ge(units_done, n0 + i * 3 - 1 + RING)
                    e.activation(act_hi[odd][:, :, :], act[:, :, :], ACT.Copy).then_inc(act_hi_ready, 1)

                def split_three(i, first=False):
                    if not first:
                        split_hi(n0 + i * 3 + 5, v0 + i + 1, 2)
                    split_hi(n0 + i * 3 + 6, v0 + i + 2, 0)
                    split_hi(n0 + i * 3 + 7, v0 + i + 2, 1)

                gated(0, 0, first=True)
                split_hi(n0 + 4, v0 + 1, 1)
                split_hi(n0 + 5, v0 + 1, 2)
                between()
                split_three(0, first=True)
                gated(1, 1, first=True)
                split_three(1)
                with e.Fori(1, (ITERS - 3) // 2) as ii:
                    for odd in range(2):
                        gated(ii * 2 + odd, odd)
                        split_three(ii * 2 + odd)
                gated(ITERS - 3, 0)
                split_three(ITERS - 3)
                gated(ITERS - 2, 1)
                split_hi(n0 + FFN_UNITS - 1, v0 + ITERS - 1, 2)
                gated(ITERS - 1, 0, lambda: split_hi(n0 + FFN_UNITS, v0 + ITERS, 0) if ahead else None)
                if ahead:
                    split_hi(n0 + FFN_UNITS + 1, v0 + ITERS, 1)

            e.wait_ge(once, 1)
            for m in range(KT):
                e.wait_ge(x_loaded[2 * m // KT], 32 if m < KT // 2 else 16)
                e.activation(xg_hi[:, m, :], x[:, m, :], ACT.Copy, scale=g0[:, m:m + 1]).then_inc(xg_hi_ready, 1)
            split_hi(0, 0, 0)
            split_hi(1, 0, 1)
            for m in range(KT):
                square(0, m, first=True)
            e.wait_ge(consts_loaded, 32)
            with e.Fori(0, DEPTH) as l:
                e.wait_ge(xg_lo_ready, l * 16 + 8)
                e.dma_start(par[:, :], params[bass.ds(l, 1), :, :].rearrange("o p c -> p (o c)")
                            ).then_inc(par_loaded, 16)
                ffn_start(l * SPLIT_UNITS, l * VISITS, l * 3, l * 4 + 1)
                def parameters():
                    e.wait_ge(par_loaded, l * 16 + 16)
                    e.activation(s5s[:, 0, :], prm("log_step"), ACT.Exp).then_inc(s5_dt, 1)
                    e.wait_ge(s5_args, l * 2 + 1)
                    e.activation(mag[:, :], s5s[:, 1, :], ACT.Exp).then_inc(s5_funs, 1)
                    e.activation(lbs[:, 2:4, :], lbs[:, 0:2, :], ACT.Exp).then_inc(s5_funs, 1)
                    e.wait_ge(s5_args, l * 2 + 2)
                    e.activation(s5s[:, 4, :], s5s[:, 3, :], ACT.Sin).then_inc(s5_funs, 1)
                    e.activation(s5s[:, 5, :], s5s[:, 3, :], ACT.Sin, scale=0.5).then_inc(s5_funs, 1)
                    e.activation(forget_hi[:, :], prm("w_forget"), ACT.Copy).then_inc(forget_split, 1)

                ffn_steps(l * 2, l * SPLIT_UNITS, l * VISITS, False, parameters)

                quarter = iter(range(IN_QUARTERS))

                def split_in(count):
                    for c in (next(quarter) for _ in range(count)):
                        n, part = c // QUARTERS, c % QUARTERS
                        if part == 0:
                            e.wait_ge(raw_loaded[n % RING], (l * VISITS + ITERS + n // RING + 1) * 16)
                        e.wait_ge(in_used, l * IN_QUARTERS + c + 1)
                        e.activation(in_hi[part][:, :], raw[n % RING][:, part * 512:(part + 1) * 512], ACT.Copy
                                     ).then_inc(in_hi_written, 1)

                split_in(4)

                def wait_x1(m):
                    e.wait_ge(x_ready, l * 24 + m + 1)
                boundary(l * 3 + 1, None, wait_x1, prm("gain_mix"))
                split_in(4)
                e.wait_ge(sums_done, l * 3 + 2)
                e.activation(ln_ms[:, :], bank(7)[:, 0:T], ACT.Ln, scale=1.0 / D, bias=eps[:, :]).then_inc(rstd_steps, 1)
                e.activation(rstd_tok[:, 2:4], bank(7)[:, T:T + 2], ACT.Ln, scale=1.0 / D, bias=eps[:, :]
                             ).then_inc(rstd_steps, 1)
                e.wait_ge(rstd_steps, l * 4 + 3)
                e.activation(rstd_tok[:, 0:2], rstd_tok[:, 2:4], ACT.Exp, scale=-0.5)
                e.activation(rstd[:, :], ln_ms[:, :], ACT.Exp, scale=-0.5).then_inc(rstd_ready, 1)
                split_in(8)
                e.wait_ge(proj_dve, l * 9 + 3)
                e.activation(key[:, :, :], bf[:, :, :], ACT.Sigmoid).then_inc(bf_sig, 1)
                split_in(4)
                e.wait_ge(bf_f, l + 1)
                e.activation(bf[:, :, :], bf[:, :, :], ACT.Ln).then_inc(bf_log, 1)

                def decays(n):
                    e.wait_ge(dec_arg, l * (NSTEP - 1) + n + 1)
                    d = dec[:, n % 2, :, :]
                    ch = lambda t, c: t.rearrange("p h (c k) -> p h c k", k=CHUNK)[:, :, c, :]
                    if n == 0:
                        e.activation(d.rearrange("p h (n s k) -> p h n s k", s=2, k=CHUNK)[:, :, :, 0, :],
                                     d.rearrange("p h (n s k) -> p h n s k", s=2, k=CHUNK)[:, :, :, 0, :], ACT.Exp)
                        e.activation(d.rearrange("p h (n s k) -> p h n s k", s=2, k=CHUNK)[:, :, :, 1, :],
                                     bc[:, :, :].rearrange("p h (n s k) -> p h n s k", s=2, k=CHUNK)[:, :, :, 1, :],
                                     ACT.Exp).then_inc(dec_exp, 1)
                    elif n == NSTEP - 2:
                        e.activation(d[:, :, 0:T // 2], d[:, :, 0:T // 2], ACT.Exp)
                        e.activation(ch(d, 2), ch(bc[:, :, :], 2), ACT.Exp)
                        e.activation(ch(d, 3), ch(d, 3), ACT.Exp).then_inc(dec_exp, 1)
                    else:
                        e.activation(d, d, ACT.Exp).then_inc(dec_exp, 1)

                def values(n, dst):
                    e.wait_ge(rstd_ready, l * 3 + 2)
                    e.wait_ge(in_used, l * IN_QUARTERS + (n + 1) * QUARTERS + QUARTERS)
                    for t in range(2):
                        e.activation(dst(t), bank(4 + n % 2)[:, t * 256:(t + 1) * 256], ACT.Copy,
                                     scale=rstd_tok[:, t:t + 1]).then_inc(proj_act, 1)

                def fox_norm(w):
                    e.wait_ge(proj_dve, l * 9 + 6 + w)
                    e.activation(fsq[:, w, :], fqk[:, w, :, :].rearrange("p a t -> p (a t)"), ACT.Square
                                 ).then_inc(fsq_ready, 1)

                def fox_rms():
                    for w in range(2):
                        e.wait_ge(fsum_done, l * 2 + w + 1)
                        e.activation(fsq[:, w, :], bank(6 + w), ACT.Ln, scale=1.0 / FOX_DIM, bias=eps[:, :]
                                     ).then_inc(fln, 1)
                    for w in range(2):
                        e.wait_ge(fln, l * 2 + w + 1)
                        e.activation(fsq[:, w, :], fsq[:, w, :], ACT.Exp, scale=-0.5).then_inc(frn_ready, 1)

                def fox_exp(t):
                    e.wait_ge(max_ready, l * 2 + 2 - t)
                    for hd in range(FOX_HEADS):
                        part = sc[:, hd, 0:P] if t == 0 else sc[:, hd, P:384]
                        e.activation(part, part, ACT.Exp, bias=fst[:, 1, t * 4 + hd:t * 4 + hd + 1],
                                     accum_out=fst[:, 2, t * 4 + hd:t * 4 + hd + 1]).then_inc(exp_done, 1)

                pT_heads = pT.rearrange("p (h c) -> p h c", c=384)
                split_in(4)
                decays(0)
                split_in(2)
                decays(1)
                split_in(2)
                fox_norm(0)
                split_in(1)
                decays(2)
                split_in(3)
                fox_norm(1)
                split_in(1)
                e.wait_ge(af_abs, l + 1)
                e.activation(fl[:, 1, :], fl[:, 1, :], ACT.Exp, scale=-1.0).then_inc(af_exp, 1)
                e.wait_ge(af_exp, l + 1)
                e.activation(fl[:, 1, :], fl[:, 1, :], ACT.Ln, bias=ones[0:4, 0:1]).then_inc(af_ln, 1)
                split_in(2)
                decays(3)
                split_in(1)
                values(7, lambda t: v_b[:, t, 0:256])
                fox_rms()
                split_in(2)
                decays(4)
                split_in(2)
                values(8, lambda t: v_b[:, t, 256:512])
                decays(5)
                split_in(1)
                split_in(3)
                fox_exp(1)
                values(9, lambda t: fv[:, t, :])
                decays(6)
                decays(7)
                e.wait_ge(y_ready, l + 1)
                e.activation(z, y, ACT.Gelu_apprx_tanh).then_inc(z_ready, 1)
                split_in(4)
                fox_exp(0)
                e.wait_ge(pt_done, l * 2 + 1)
                e.activation(pT_heads[:, 0:2, P:384], bank(6).rearrange("p (h c) -> p h c", c=T), ACT.Copy
                             ).then_inc(pt_act, 1)
                e.wait_ge(glu_done, l + 1)
                for m in range(2):
                    last = e.activation(y[:, m, :], bank(5)[:, m * T:(m + 1) * T], ACT.Sigmoid,
                                        bias=prm("glu_b", m, 1))
                last.then_inc(sg_ready, 1)
                e.wait_ge(o_done, l + 1)
                e.activation(osq[:, :], bank(0, 2), ACT.Square).then_inc(osq_ready, 1)
                e.wait_ge(pt_done, l * 2 + 2)
                e.activation(pT_heads[:, :, 0:P], bank(6).rearrange("p (h c) -> p h c", c=P), ACT.Copy
                             ).then_inc(pt_act, 1)
                e.wait_ge(osum_done, l + 1)
                e.activation(orn[:, :], bank(2, 2), ACT.Ln, scale=1.0 / P, bias=eps[:, :]).then_inc(oln, 1)
                e.wait_ge(oln, l + 1)
                e.activation(osq[:, :], orn[:, :], ACT.Exp, scale=-0.5).then_inc(orn_ready, 1)
                e.wait_ge(fo_done, l + 1)
                e.activation(fsq[:, 0, :], bank(4), ACT.Copy).then_inc(mix_fox, 1)
                e.wait_ge(proj_dve, l * 9 + 9)
                e.activation(bg[:, :, :], bg[:, :, :], ACT.Silu).then_inc(bg_ready, 1)

                split_hi(l * SPLIT_UNITS + FFN_UNITS, l * VISITS + 16, 0)
                split_hi(l * SPLIT_UNITS + FFN_UNITS + 1, l * VISITS + 16, 1)

                def wait_x2(m):
                    e.wait_ge(x_ready, l * 24 + 8 + m + 1)
                boundary(l * 3 + 2, l * 2 + 1, wait_x2, prm("gain_ffn2"))
                ffn_start(l * SPLIT_UNITS + FFN_UNITS, l * VISITS + 16, l * 3 + 2, l * 4 + 4)
                ffn_steps(l * 2 + 1, l * SPLIT_UNITS + FFN_UNITS, l * VISITS + 16, True)

                def wait_x3(m):
                    e.wait_ge(x_ready, l * 24 + 16 + m + 1)
                boundary(l * 3 + 3, l * 2 + 2, wait_x3, prm("gain_next"))

        @block.tensor
        def _(pe):
            def three(acc, w_hi, w_lo, a_hi, a_lo, start, stop):
                pe.matmul(acc, w_hi, a_hi, start=start, stop=False, skip_group_check=True)
                pe.matmul(acc, w_hi, a_lo, start=False, stop=False, skip_group_check=True)
                return pe.matmul(acc, w_lo, a_hi, start=False, stop=stop, skip_group_check=True)

            def down_acc(m):
                return bank(m // 2)[:, (m % 2) * T:(m % 2 + 1) * T]

            def row_sums(norm, tokens):
                pe.wait_ge(consts_loaded, 32)
                pe.wait_ge(sumsq_added, norm * 7 + 7)
                last = pe.matmul(bank(7)[:, 0:T], ones, sumsq[:, :], start=True, stop=True)
                if tokens:
                    for t in range(2):
                        last = pe.matmul(bank(7)[:, T + t:T + t + 1], sumsq[:, t * P:(t + 1) * P], ones[:, 0:1],
                                         start=True, stop=True, skip_group_check=True)
                last.then_inc(sums_done, 1)

            def ffn(f, n0, norm):
                for k in range(KT):
                    pe.wait_ge(xg_lo_ready, f * KT + k + 1)
                    if k == 0:
                        pe.wait_ge(lo_written, n0 + 1 + RING)
                        pe.wait_ge(lo_written, n0 + 2 + RING)
                    if k == 5:
                        row_sums(norm, False)
                    for m in range(2):
                        for s in range(2):
                            w = k * 256 + m * P
                            last = three(bank(4 + m)[:, s * T:(s + 1) * T], hi[s][:, w:w + P], lo[s][:, w:w + P],
                                         xg_hi[:, k, :], xg_lo[:, k, :], k == 0 and s == 0, k == KT - 1)
                last.then_inc(units_done, 2)
                for b in range(4):
                    pe.matmul(bank(b), zero[:, 0:P], zero[:, :], start=True, stop=False, skip_group_check=True)

                def gate_up(half, n, slot, b, first):
                    pe.wait_ge(lo_written, n + 1 + RING)
                    for m in range(2):
                        for k in range(KT):
                            w = k * 256 + m * P
                            last = three(bank(b + m)[:, half * T:(half + 1) * T], hi[slot][:, w:w + P],
                                         lo[slot][:, w:w + P], xg_hi[:, k, :], xg_lo[:, k, :],
                                         k == 0, k == KT - 1)
                    last.then_inc(units_done, 1)

                def step(i, g, first):
                    n = n0 + i * 3 + 2
                    if first:
                        pe.wait_ge(rstd_ready, norm + 1)
                    pe.wait_ge(gu_read, f * ITERS + i + 1)
                    gate_up(0, n, 2, 4 + 2 * g, first)
                    gate_up(1, n + 1, 0, 4 + 2 * g, first)
                    pe.wait_ge(lo_written, n + 3 + RING)
                    pe.wait_ge(act_lo_ready, f * ITERS + i + 1)
                    for m in range(KT):
                        for k in range(2):
                            w = k * D + m * P
                            last = three(down_acc(m), hi[1][:, w:w + P], lo[1][:, w:w + P],
                                         act_hi[1 - g][:, k, :], act_lo[1 - g][:, k, :], False, False)
                    last.then_inc(units_done, 1)

                with pe.Fori(0, (ITERS - 1) // 2) as ii:
                    step(ii * 2, 1, True)
                    step(ii * 2 + 1, 0, False)
                pe.wait_ge(lo_written, n0 + FFN_UNITS + RING)
                pe.wait_ge(act_lo_ready, f * ITERS + ITERS)
                for m in range(KT):
                    for k in range(2):
                        w = k * D + m * P
                        last = three(down_acc(m), hi[2][:, w:w + P], lo[2][:, w:w + P],
                                     act_hi[0][:, k, :], act_lo[0][:, k, :], False, k == 1)
                    if m % 2 == 1 and m < KT - 1:
                        last.then_inc(acc_done, 1)
                last.then_inc(units_done, 1)

            pe.wait_ge(zeros_set, 1)
            with pe.Fori(0, DEPTH) as l:
                ffn(l * 2, l * SPLIT_UNITS, l * 3)

                dve_units = [0, 1, 2, 3, 4, 5, 6, 10, 11]

                def quarter_ready(n, part):
                    pe.wait_ge(in_lo_pool if n in POOL_UNITS else in_lo_dve, in_split_count(l, n, part))

                def unit_ready(n):
                    if n - 2 in dve_units:
                        pe.wait_ge(proj_dve, l * 9 + dve_units.index(n - 2) + 1)
                    elif n >= 2:
                        pe.wait_ge(proj_act, l * 6 + (n - 2 - 7) * 2 + 2)

                def project(n, at_tile={}):
                    unit_ready(n)
                    b = bank(4 + n % 2)
                    for k in range(KT):
                        part, w = k // 2, k % 2 * 256
                        if k in at_tile:
                            at_tile[k]()
                        if k % 2 == 0:
                            quarter_ready(n, part)
                        if n == 0:
                            pe.wait_ge(h_lo_ready, l * KT + k + 1)
                        for m in range(2):
                            last = three(b[:, m * T:(m + 1) * T], in_hi[part][:, w + m * P:w + m * P + P],
                                         in_lo[part][:, w + m * P:w + m * P + P], h_hi[:, k, :], h_lo[:, k, :],
                                         k == 0 and m == 0, k == KT - 1)
                        if k % 2 == 1:
                            last.then_inc(in_used, 1)

                def project_tokens(n, at_tile={}):
                    unit_ready(n)
                    b = bank(4 + n % 2)
                    for k in range(KT):
                        part, w = k // 2, k % 2 * 256
                        if k in at_tile:
                            at_tile[k]()
                        if k % 2 == 0:
                            quarter_ready(n, part)
                        for t in range(2):
                            tok = slice(t * P, (t + 1) * P)
                            last = three(b[:, t * 256:(t + 1) * 256], h_hi[:, k, tok], h_lo[:, k, tok],
                                         in_hi[part][:, w:w + 256], in_lo[part][:, w:w + 256],
                                         k == 0 and t == 0, k == KT - 1)
                        if k % 2 == 1:
                            last.then_inc(in_used, 1)

                def input_matrix(j0):
                    if j0 == 0:
                        pe.wait_ge(proj_dve, l * 9 + 1)
                        pe.wait_ge(rstd_ready, l * 3 + 2)
                    else:
                        pe.wait_ge(bu_read, l * 8 + j0)
                    for part, name in enumerate(("b_re", "b_im")):
                        for j in (j0, j0 + 1):
                            r = 32 * (j % 4)
                            last = pe.matmul(bank(6 + j % 2)[:, part * T:(part + 1) * T],
                                             prm(name)[r:r + 32, (j // 4) * P:(j // 4 + 1) * P],
                                             u[r:r + 32, j // 4, :], start=True, stop=True, skip_group_check=True)
                            if part == 1:
                                last.then_inc(bu_done, 1)

                def level(n):
                    b = bank(2 * (n % 2), 2)
                    if n < NLEV - 1 or n == NSTEP - 1:
                        pe.wait_ge(qk_ready, l * (NSTEP - 1) + (n if n < NLEV - 1 else n - 1) + 1)
                    if n >= 2:
                        pe.wait_ge(lev_read, l * NSTEP + n - 1)
                    if n == NSTEP - 1:
                        q = qk[:, (n - 1) % 2, :, :]
                        for hd in range(HEADS):
                            last = pe.matmul(b[:, hd * P:(hd + 1) * P], q[:, hd, 0:P], q[:, hd, P:T],
                                             start=True, stop=True, skip_group_check=True)
                    else:
                        for hd in range(HEADS):
                            for t in range(2):
                                i = hd * 2 + t
                                tok = slice(t * P, (t + 1) * P)
                                if n == NLEV - 1:
                                    last = pe.matmul(b[:, i * P:(i + 1) * P], key[:, hd, tok], bq[:, hd, tok],
                                                     start=True, stop=True, skip_group_check=True)
                                else:
                                    a = qk[:, n % 2, hd, tok]
                                    c = a.rearrange("p (n s k) -> p n s k", s=2, k=LEVELS[n])[:, :, 1, :]
                                    last = pe.matmul(b[:, i * P // 2:(i + 1) * P // 2], a, c, start=True, stop=True,
                                                     skip_group_check=True)
                    last.then_inc(lev_done, 1)

                def fox_sums(w):
                    pe.wait_ge(fsq_ready, l * 2 + w + 1)
                    pe.wait_ge(bu_read, l * 8 + 7 + w)
                    pe.matmul(bank(6 + w), halves, fsq[:, w, :], start=True, stop=True).then_inc(fsum_done, 1)

                def s5_output():
                    pe.wait_ge(xs_ready, l * 8 + 8)
                    pe.wait_ge(tables_ready, l + 1)
                    pe.wait_ge(proj_act, l * 6 + 4)
                    for j in range(S5_TILES):
                        r, c = 32 * (j % 4), j // 4
                        for part in range(2):
                            last = pe.matmul(bank(4)[r:r + 32, c * T:(c + 1) * T],
                                             c_out[:, part, j * 32:(j + 1) * 32], xs[:, j, part, :],
                                             start=part == 0, stop=part == 1, skip_group_check=True)
                    last.then_inc(y_done, 1)

                def s5_glu():
                    pe.wait_ge(z_ready, l + 1)
                    pe.wait_ge(proj_act, l * 6 + 6)
                    for m in range(2):
                        for k in range(2):
                            last = pe.matmul(bank(5)[:, m * T:(m + 1) * T], prm("glu_w", k * T + m * P, P),
                                             z[:, k, :], start=k == 0, stop=k == 1, skip_group_check=True)
                    last.then_inc(glu_done, 1)

                def fox_scores(t, first):
                    n, tok = (t + 1) * P, slice(t * P, (t + 1) * P)
                    dst = lambda hd: bank(6 + hd % 2)[:, hd // 2 * n:(hd // 2 + 1) * n]

                    def products(pair):
                        if pair == 0 and t == 1:
                            pe.wait_ge(fqk_ready, l * 2 + 2)
                            pe.wait_ge(cum_ready, l + 1)
                            pe.wait_ge(frn_ready, l * 2 + 2)
                        elif pair == 0:
                            pe.wait_ge(sc_read, l * 2 + 1)
                        for hd in (2 * pair, 2 * pair + 1):
                            r = 64 * (hd % 2)
                            pe.matmul(dst(hd), fqk[r:r + 64, 0, pair, tok], fqk[r:r + 64, 1, pair, 0:n],
                                      start=True, stop=False, skip_group_check=True)

                    def sums(hd):
                        pe.matmul(dst(hd), fl[:, 2, tok], head_row(hd, n), start=False, stop=False,
                                  skip_group_check=True)
                        last = pe.matmul(dst(hd), head_row(hd, P), fl[:, 3, 0:n], start=False, stop=True,
                                         skip_group_check=True)
                        if hd == FOX_HEADS - 1:
                            last.then_inc(sc_done, 1)

                    steps = [lambda: products(0), lambda: sums(0), lambda: sums(1), lambda: products(1),
                             lambda: sums(2), lambda: sums(3)]
                    return {first + i: step for i, step in enumerate(steps)}

                def fox_transposes(t):
                    if t == 1:
                        pe.wait_ge(p_ready, l * 2 + 1)
                        pe.wait_ge(sc_read, l * 2 + 2)
                    else:
                        pe.wait_ge(p_ready, l * 2 + 2)
                        pe.wait_ge(pt_act, l * 2 + 1)
                    i = 0
                    for hd in range(FOX_HEADS):
                        for part in ((1, 2) if t == 1 else (0,)):
                            last = pe.transpose(ps[:, 6 * 512 + i * P:6 * 512 + (i + 1) * P],
                                                sc[:, hd, part * P:(part + 1) * P], ident)
                            i += 1
                    last.then_inc(pt_done, 1)

                def fox_output():
                    pe.wait_ge(pt_act, l * 2 + 2)
                    pe.wait_ge(pt_dve, l + 1)
                    pe.wait_ge(proj_dve, l * 9 + 8)
                    for hd in range(FOX_HEADS):
                        r, c = 64 * (hd % 2), (hd // 2) * T
                        w = slice(hd * FOX_DIM, (hd + 1) * FOX_DIM)
                        part = lambda i: pT[:, hd * 384 + i * P:hd * 384 + (i + 1) * P]
                        pe.matmul(bank(4)[r:r + 64, c:c + P], fv[:, 0, w], part(0), start=True, stop=True,
                                  skip_group_check=True)
                        pe.matmul(bank(4)[r:r + 64, c + P:c + T], fv[:, 0, w], part(1), start=True, stop=False,
                                  skip_group_check=True)
                        last = pe.matmul(bank(4)[r:r + 64, c + P:c + T], fv[:, 1, w], part(2), start=False,
                                         stop=True, skip_group_check=True)
                    last.then_inc(fo_done, 1)

                def hgrn_output():
                    pe.wait_ge(lev_read, l * NSTEP + NSTEP)
                    pe.wait_ge(proj_act, l * 6 + 4)
                    for hd in range(HEADS):
                        at = hd * T
                        w = slice(hd * P, (hd + 1) * P)
                        o = bank(0, 2)
                        pe.matmul(o[:, at:at + P], v_b[:, 0, w], attn[:, hd * 2, :], start=True, stop=True,
                                  skip_group_check=True)
                        pe.matmul(o[:, at + P:at + T], v_b[:, 0, w], attn_x[:, hd, :], start=True, stop=False,
                                  skip_group_check=True)
                        last = pe.matmul(o[:, at + P:at + T], v_b[:, 1, w], attn[:, hd * 2 + 1, :], start=False,
                                         stop=True, skip_group_check=True)
                    last.then_inc(o_done, 1)

                def hgrn_sums():
                    pe.wait_ge(osq_ready, l + 1)
                    for b in range(2):
                        last = pe.matmul(bank(2 + b), ones, osq[:, b * 512:(b + 1) * 512], start=True, stop=True)
                    last.then_inc(osum_done, 1)

                project(0)
                row_sums(l * 3 + 1, True)
                project(1)
                input_matrix(0)
                project(2)
                input_matrix(2)
                project(3)
                project(4)
                input_matrix(4)
                project(5)
                project(6, {1: lambda: level(0)})
                pe.wait_ge(bu_read, l * 8 + 6)
                pe.wait_ge(forget_ready, l + 1)
                for k in range(KT):
                    last = three(bank(7)[0:4, 0:T], forget_hi[:, k * 4:k * 4 + 4], forget_lo[:, k * 4:k * 4 + 4],
                                 h_hi[:, k, :], h_lo[:, k, :], k == 0, k == KT - 1)
                last.then_inc(af_done, 1)
                level(1)
                pe.wait_ge(af_abs, l + 1)
                project_tokens(7, {1: lambda: input_matrix(6)})
                level(2)
                project_tokens(8, {2: lambda: fox_sums(0), 3: lambda: fox_sums(1)})
                level(3)
                project_tokens(9, fox_scores(1, 2))
                level(4)
                s5_output()
                level(5)
                pe.wait_ge(y_ready, l + 1)
                project(10, fox_scores(0, 2))
                level(6)
                fox_transposes(1)
                s5_glu()
                level(7)
                level(8)
                hgrn_output()
                pe.wait_ge(sg_ready, l + 1)
                project(11, {2: lambda: fox_transposes(0), 3: hgrn_sums, 6: fox_output})

                def project_out(n, tiles, last_part):
                    for k in tiles:
                        if k < 2:
                            a = fox_out[:, k, :]
                        elif k >= 6:
                            a = s5_out[:, k - 6, :]
                        else:
                            a = hgrn_out[:, k - 2, :]
                        for m in range(2):
                            last = pe.matmul(out_bank(n)[:, m * T:(m + 1) * T],
                                             raw[n][:, k * 256 + m * P:k * 256 + m * P + P], a,
                                             start=k == 6 and m == 0, stop=last_part and k == tiles[-1],
                                             skip_group_check=True)
                    if last_part:
                        last.then_inc(out_unit_done, 1)

                pe.wait_ge(oln, l + 1)
                pe.wait_ge(mix_s5, l + 1)
                pe.wait_ge(mix_fox, l + 1)
                for n in range(2):
                    pe.wait_ge(raw_loaded[n], (l * VISITS + ITERS + 4 + 1) * 16)
                    project_out(n, (6, 7, 0, 1), False)
                pe.wait_ge(mix_hgrn, l + 1)
                for n in range(2):
                    project_out(n, (2, 3, 4, 5), True)
                pe.wait_ge(raw_loaded[2], (l * VISITS + ITERS + 4 + 1) * 16)
                project_out(2, (6, 7, 0, 1, 2, 3, 4, 5), True)
                pe.wait_ge(raw_loaded[3], (l + 1) * 16)
                project_out(3, (6, 7, 0, 1, 2, 3, 4, 5), True)

                ffn(l * 2 + 1, l * SPLIT_UNITS + FFN_UNITS, l * 3 + 2)

        @block.vector
        def _(v):
            def acc(m):
                return bank(m // 2)[:, (m % 2) * T:(m % 2 + 1) * T]

            def split_lo(n, slot):
                v.wait_ge(hi_written, n + 1 + RING)
                v.tensor_tensor(lo[slot][:, :], raw[slot][:, :], hi[slot][:, :].bitcast(F32), ALU.subtract
                                ).then_inc(lo_written, 1)

            def rest_of_x(f, m, gain):
                if f is None:
                    v.wait_ge(h_hi_ready, l * KT + m + 1)
                    v.scalar_tensor_tensor(h_lo[:, m, :], x[:, m, :], gain[:, m:m + 1], h_hi[:, m, :].bitcast(F32),
                                           ALU.mult, ALU.subtract).then_inc(h_lo_ready, 1)
                    return
                v.wait_ge(xg_hi_ready, f * KT + m + 1)
                v.scalar_tensor_tensor(xg_lo[:, m, :], x[:, m, :], gain[:, m:m + 1], xg_hi[:, m, :].bitcast(F32),
                                       ALU.mult, ALU.subtract).then_inc(xg_lo_ready, 1)

            def boundary(wait_acc, scale, f, gain, acc=acc):
                for m in range(KT):
                    wait_acc(m)
                    v.scalar_tensor_tensor(x[:, m, :], acc(m), scale, x[:, m, :], ALU.mult, ALU.add
                                           ).then_inc(x_ready, 1)
                    if m >= 1:
                        rest_of_x(f, m - 1, gain)
                rest_of_x(f, KT - 1, gain)

            def gated(f, i, g, n_up, norm, after_act=lambda: None):
                both = bank(4 + 2 * g, 2).rearrange("p (m s t) -> p m s t", m=2, s=2)
                wide = rstd[:, :].unsqueeze(1).broadcast_to([P, 2, T])
                v.wait_ge(rstd_ready, norm + 1)
                v.wait_ge(units_done, n_up + 1 + RING)
                v.tensor_tensor(gate[:, :, :], both[:, :, 0, :], wide, ALU.mult).then_inc(gate_scaled, 1)
                v.tensor_tensor(up[:, :, :], both[:, :, 1, :], wide, ALU.mult).then_inc(gu_read, 1)
                v.wait_ge(silu_done, f * ITERS + i + 1)
                v.wait_ge(gu_read, f * ITERS + i + 2)
                v.tensor_tensor(act[:, :, :], silu[:, :, :], up[:, :, :], ALU.mult).then_inc(act_ready, 1)
                after_act()
                v.wait_ge(act_hi_ready, f * ITERS + i + 1)
                v.tensor_tensor(act_lo[g][:, :, :], act[:, :, :], act_hi[g][:, :, :].bitcast(F32), ALU.subtract
                                ).then_inc(act_lo_ready, 1)

            def ffn_steps(f, n0, norm, ahead, between=lambda: None):
                def split_three(i, first=False):
                    if not first:
                        split_lo(n0 + i * 3 + 5, 2)
                    split_lo(n0 + i * 3 + 6, 0)
                    split_lo(n0 + i * 3 + 7, 1)

                split_lo(n0 + 2, 2)
                split_lo(n0 + 3, 0)
                gated(f, 0, 0, n0, norm)
                split_lo(n0 + 4, 1)
                split_lo(n0 + 5, 2)
                between()
                split_three(0, first=True)
                with v.Fori(0, (ITERS - 3) // 2) as ii:
                    for g in (1, 0):
                        i = ii * 2 + 2 - g
                        gated(f, i, g, n0 + i * 3, norm)
                        split_three(i)
                gated(f, ITERS - 2, 1, n0 + 3 * (ITERS - 2), norm)
                split_lo(n0 + FFN_UNITS - 1, 2)
                gated(f, ITERS - 1, 0, n0 + 3 * (ITERS - 1), norm,
                      lambda: split_lo(n0 + FFN_UNITS, 0) if ahead else None)
                if ahead:
                    split_lo(n0 + FFN_UNITS + 1, 1)

            v.memset(zero[:, :].bitcast(F32), 0.0).then_inc(zeros_set, 1)
            for m in range(KT):
                rest_of_x(0, m, g0)
            split_lo(0, 0)
            split_lo(1, 1)
            v.wait_ge(consts_loaded, 32)
            v.tensor_copy(mask[:, :], trig_tmp[:, :, :].rearrange("p j t -> p (j t)")).then_inc(mask_ready, 1)
            v.wait_ge(mask_ready, 1)
            with v.Fori(0, DEPTH) as l:
                st = Steps(v, dve_step, l, DVE_STEPS)

                def parameters():
                    lr, li = prm("lam_re"), prm("lam_im")
                    tiny = lambda i: s5s[:, i, :]
                    v.wait_ge(par_loaded, l * 16 + 16)
                    lg = prm("lb_logit").rearrange("p (d h) -> p d h", d=2)
                    st.mark(v.tensor_tensor(lbs[:, 4, :], lg[:, 0, :], lg[:, 1, :], ALU.max))
                    st.wait()
                    st.mark(v.tensor_tensor(lbs[:, 0:2, :], lg, lbs[:, 4:5, :].broadcast_to([P, 2, HEADS]), ALU.subtract))
                    v.wait_ge(s5_dt, l + 1)
                    v.tensor_tensor(tiny(2), li, tiny(0), ALU.mult)
                    st.wait()
                    v.tensor_tensor(tiny(1), lr, tiny(0), ALU.mult).then_inc(s5_args, 1)
                    v.wait_ge(s5_args, l * 2 + 1)
                    st.mark(v.tensor_scalar(tiny(6), tiny(2), 1.0 / TWO_PI, ROUND, ALU.mult, ALU.add))
                    st.wait()
                    st.mark(v.tensor_scalar(tiny(6), tiny(6), ROUND, None, ALU.subtract))
                    for c in (PI_A, PI_B, PI_C):
                        st.wait()
                        st.mark(v.scalar_tensor_tensor(tiny(2), tiny(6), -c, tiny(2), ALU.mult, ALU.add))
                    st.wait()
                    v.tensor_scalar(tiny(3), tiny(2), 3.1415925, -3.1415925, ALU.min, ALU.max).then_inc(s5_args, 1)
                    v.wait_ge(s5_funs, l * 4 + 2)
                    st.mark(v.tensor_tensor(lbs[:, 4, :], lbs[:, 2, :], lbs[:, 3, :], ALU.add))
                    st.wait()
                    st.mark(v.reciprocal(lbs[:, 4, :], lbs[:, 4, :]))
                    st.wait()
                    st.mark(v.tensor_tensor(lbs[:, 2, :], lbs[:, 2, :], lbs[:, 4, :], ALU.mult))
                    st.mark(v.tensor_tensor(lbs[:, 3, :], lbs[:, 3, :], lbs[:, 4, :], ALU.mult))
                    st.wait()
                    st.mark(v.tensor_tensor(lbs[:, 5, :], lbs[:, 2, :], lbs[:, 3, :], ALU.add))
                    st.wait()
                    st.mark(v.tensor_tensor(lbs[:, 5, :], lbs[:, 5, :], lbs[:, 2, :], ALU.subtract))
                    st.wait()
                    st.mark(v.tensor_scalar(lbs[:, 5, :], lbs[:, 5, :], prm("later_layer"), None, ALU.mult))
                    st.wait()
                    st.mark(v.tensor_scalar(lbs[:, 6, :], lbs[:, 5, :], -1.0, 1.0, ALU.mult, ALU.add))
                    v.wait_ge(s5_funs, l * 4 + 4)
                    st.mark(v.tensor_tensor(tiny(6), tiny(5), tiny(5), ALU.mult))
                    st.mark(v.tensor_copy(rot[:, 0, 1, :], tiny(4)))
                    st.wait()
                    st.mark(v.tensor_scalar(rot[:, 0, 0, :], tiny(6), -2.0, 1.0, ALU.mult, ALU.add))
                    st.wait()
                    st.mark(v.tensor_tensor(tiny(7), mag[:, :], rot[:, 0, 0, :], ALU.mult))
                    st.mark(v.tensor_tensor(tiny(8), mag[:, :], tiny(4), ALU.mult))
                    st.mark(v.tensor_tensor(tiny(9), lr, lr, ALU.mult))
                    st.mark(v.tensor_tensor(tiny(10), li, li, ALU.mult))
                    st.wait()
                    st.mark(v.tensor_scalar(tiny(7), tiny(7), -1.0, None, ALU.add))
                    st.mark(v.tensor_tensor(tiny(9), tiny(9), tiny(10), ALU.add))
                    st.wait()
                    st.mark(v.reciprocal(tiny(9), tiny(9)))
                    st.mark(v.tensor_tensor(tiny(0), tiny(7), lr, ALU.mult))
                    st.mark(v.tensor_tensor(tiny(1), tiny(8), li, ALU.mult))
                    st.mark(v.tensor_tensor(tiny(10), tiny(8), lr, ALU.mult))
                    st.mark(v.tensor_tensor(tiny(6), tiny(7), li, ALU.mult))
                    st.wait()
                    st.mark(v.tensor_tensor(tiny(0), tiny(0), tiny(1), ALU.add))
                    st.mark(v.tensor_tensor(tiny(10), tiny(10), tiny(6), ALU.subtract))
                    st.wait()
                    st.mark(v.tensor_tensor(coef[:, 0, :], tiny(0), tiny(9), ALU.mult))
                    st.mark(v.tensor_tensor(coef[:, 1, :], tiny(10), tiny(9), ALU.mult))
                    st.wait()
                    v.tensor_scalar(coef[:, 2, :], coef[:, 1, :], -1.0, None, ALU.mult).then_inc(s5_coef, 1)
                    v.wait_ge(forget_split, l + 1)
                    v.tensor_tensor(forget_lo[:, :], prm("w_forget"), forget_hi[:, :].bitcast(F32), ALU.subtract
                                    ).then_inc(forget_ready, 1)

                ffn_steps(l * 2, l * SPLIT_UNITS, l * 3, False, parameters)

                def wait_ffn1(m):
                    if m < KT - 2:
                        v.wait_ge(acc_done, l * 6 + m // 2 + 1)
                    else:
                        v.wait_ge(units_done, l * SPLIT_UNITS + FFN_UNITS + RING)
                quarter = iter([(n, part) for n in DVE_UNITS for part in range(QUARTERS)])

                def split_in(count):
                    for n, part in (next(quarter) for _ in range(count)):
                        v.wait_ge(in_hi_written, l * IN_QUARTERS + n * QUARTERS + part + 1)
                        v.tensor_tensor(in_lo[part][:, :], raw[n % RING][:, part * 512:(part + 1) * 512],
                                        in_hi[part][:, :].bitcast(F32), ALU.subtract).then_inc(in_lo_dve, 1)

                split_in(4)
                boundary(wait_ffn1, 0.5, None, prm("gain_mix"))

                wide = rstd[:, :].unsqueeze(1).broadcast_to([P, 2, T])

                def take(n, dst):
                    v.wait_ge(in_used, l * IN_QUARTERS + (n + 1) * QUARTERS + QUARTERS)
                    v.tensor_tensor(dst, bank(4 + n % 2).rearrange("p (m t) -> p m t", m=2), wide, ALU.mult
                                    ).then_inc(proj_dve, 1)

                def rotate(j):
                    v.wait_ge(bu_done, l * 8 + j + 1)
                    if j == 0:
                        v.wait_ge(tables_ready, l + 1)
                    if j >= 4:
                        v.wait_ge(xs_ready, l * 8 + j - 3)
                    b = bank(6 + j % 2).rearrange("p (a t) -> p a t", a=2)
                    c = cos[:, j:j + 1, :].broadcast_to([P, 2, T])
                    s = sin[:, j:j + 1, :].broadcast_to([P, 2, T])
                    v.tensor_tensor(s5a[:, j % 4, :, :], b, c, ALU.mult)
                    v.tensor_tensor(s5b[:, j % 4, :, :], b, s, ALU.mult).then_inc(bu_read, 1)

                def scan(j):
                    v.wait_ge(xin_ready, l * 8 + j + 1)
                    decay = mag[:, j:j + 1].broadcast_to([P, T])
                    a, b = s5a[:, j % 4, :, :], s5b[:, j % 4, :, :]
                    v.tensor_tensor_scan(a[:, 0, :], decay, a[:, 0, :], 0.0, ALU.mult, ALU.add)
                    v.tensor_tensor_scan(a[:, 1, :], decay, a[:, 1, :], 0.0, ALU.mult, ALU.add
                                         ).then_inc(scan_done, 1)
                    v.wait_ge(scan_done, l * 8 + j + 1)
                    c = cos[:, j:j + 1, :].broadcast_to([P, 2, T])
                    s = sin[:, j:j + 1, :].broadcast_to([P, 2, T])
                    v.tensor_tensor(b, a, s, ALU.mult)
                    v.tensor_tensor(a, a, c, ALU.mult).then_inc(un_ready, 1)

                def split2(t, size):
                    return t.rearrange("p h (n s k) -> p (h n) s k", s=2, k=size)

                def exponents(n):
                    if n >= 2:
                        v.wait_ge(qk_ready, l * (NSTEP - 1) + n - 1)
                    d = dec[:, n % 2, :, :]
                    b = bc[:, :, :]
                    if n == NSTEP - 2:
                        chunk = lambda t, c: t[:, :, c * CHUNK:(c + 1) * CHUNK]
                        end = lambda c: b[:, :, (c + 1) * CHUNK - 1:(c + 1) * CHUNK].broadcast_to([P, HEADS, CHUNK])
                        v.tensor_tensor(chunk(d, 0), bsum[:, :].unsqueeze(2).broadcast_to([P, HEADS, CHUNK]),
                                        chunk(b, 0), ALU.subtract)
                        v.tensor_tensor(chunk(d, 1), end(1), chunk(b, 1), ALU.subtract)
                        v.tensor_tensor(chunk(d, 3), chunk(b, 3), end(2), ALU.add).then_inc(dec_arg, 1)
                        return
                    size = LEVELS[n]
                    dv, bv = split2(d, size), split2(b, size)
                    ref = bv[:, :, 0, size - 1:size].broadcast_to([P, HEADS * T // (2 * size), size])
                    first = v.tensor_tensor(dv[:, :, 0, :], ref, bv[:, :, 0, :], ALU.subtract)
                    if size < CHUNK:
                        first = v.tensor_tensor(dv[:, :, 1, :], bv[:, :, 1, :], ref, ALU.subtract)
                    first.then_inc(dec_arg, 1)

                def operands(n):
                    v.wait_ge(dec_exp, l * (NSTEP - 1) + n + 1)
                    if n >= 2:
                        v.wait_ge(lev_done, l * NSTEP + n - 1)
                    d, o = dec[:, n % 2, :, :], qk[:, n % 2, :, :]
                    size = P if n == NSTEP - 2 else LEVELS[n]
                    v.tensor_tensor(split2(o, size)[:, :, 0, :], split2(key[:, :, :], size)[:, :, 0, :],
                                    split2(d, size)[:, :, 0, :], ALU.mult)
                    v.tensor_tensor(split2(o, size)[:, :, 1, :], split2(bq[:, :, :], size)[:, :, 1, :],
                                    split2(d, size)[:, :, 1, :], ALU.mult).then_inc(qk_ready, 1)

                def scores(n):
                    v.wait_ge(lev_done, l * NSTEP + n + 1)
                    if n == 0:
                        v.wait_ge(attn_clear, l + 1)
                    if n == NSTEP - 1:
                        v.tensor_copy(attn_x[:, :, :].rearrange("p h t -> p (h t)"), bank(2 * (n % 2))
                                      ).then_inc(lev_read, 1)
                        return
                    if n >= 1:
                        v.wait_ge(lev_read, l * NSTEP + n)
                    v.memset(tick[:, :], 0.0)
                    m = mask[:, n * P:(n + 1) * P]
                    if n == NLEV - 1:
                        v.copy_predicated(attn[:, :, :], m.unsqueeze(1).broadcast_to([P, 2 * HEADS, P]),
                                          bank(2 * (n % 2), 2).rearrange("p (i t) -> p i t", t=P)
                                          ).then_inc(lev_read, 1)
                        return
                    size = LEVELS[n]
                    m = m.rearrange("p (n s k) -> p n s k", s=2, k=size)[:, :, 1, :].unsqueeze(1)
                    v.copy_predicated(attn[:, :, :].rearrange("p i (n s k) -> p i n s k", s=2, k=size)[:, :, :, 1, :],
                                      m.broadcast_to([P, 2 * HEADS, P // (2 * size), size]),
                                      bank(2 * (n % 2)).rearrange("p (i n k) -> p i n k", i=2 * HEADS, k=size)
                                      ).then_inc(lev_read, 1)

                split_in(4)
                v.wait_ge(rstd_ready, l * 3 + 2)
                take(0, u[:, :, :])
                take(1, bf[:, 0:2, :])
                rotate(0)
                split_in(1)
                rotate(1)
                split_in(3)
                take(2, bf[:, 2:4, :])
                rotate(2)
                rotate(3)
                v.wait_ge(bf_sig, l + 1)
                for hd in range(HEADS):
                    last = v.tensor_scalar(bf[:, hd, :], key[:, hd, :], lbs[:, 6, hd:hd + 1], lbs[:, 5, hd:hd + 1],
                                           ALU.mult, ALU.add)
                st.mark(last)
                st.wait()
                st.mark(v.tensor_scalar(key[:, :, :], bf[:, :, :], -1.0, 1.0, ALU.mult, ALU.add))
                st.wait()
                v.tensor_scalar(bf[:, :, :], bf[:, :, :], 2.0 ** -63, None, ALU.max).then_inc(bf_f, 1)
                scan(0)
                scan(1)
                take(3, bq[:, 0:2, :])
                v.wait_ge(bf_log, l + 1)
                for hd in range(HEADS):
                    last = v.tensor_tensor_scan(bc[:, hd, :], carry, bf[:, hd, :], 0.0, ALU.mult, ALU.add)
                st.mark(last)
                st.wait()
                st.mark(v.tensor_tensor(bsum[:, :].unsqueeze(2), bc[:, :, CHUNK - 1:CHUNK],
                                        bc[:, :, 2 * CHUNK - 1:2 * CHUNK], ALU.add))
                exponents(0)
                exponents(1)
                scan(2)
                take(4, bq[:, 2:4, :])
                v.wait_ge(bf_f, l + 1)
                v.wait_ge(proj_dve, l * 9 + 5)
                operands(0)
                rotate(4)
                rotate(5)
                scan(3)
                take(5, fqk[:, 0, :, :])
                operands(1)
                exponents(2)
                scores(0)
                take(6, fqk[:, 1, :, :])
                v.wait_ge(af_done, l + 1)
                st.mark(v.tensor_tensor(fl[:, 0, :], bank(7)[0:4, 0:T], rstd[0:4, :], ALU.mult))
                st.wait()
                st.mark(v.tensor_scalar(fl[:, 0, :], fl[:, 0, :], prm("f_bias")[0:4, :], None, ALU.add))
                st.wait()
                st.mark(v.tensor_scalar(fl[:, 1, :], fl[:, 0, :], -1.0, None, ALU.mult))
                st.wait()
                v.tensor_tensor(fl[:, 1, :], fl[:, 1, :], fl[:, 0, :], ALU.max).then_inc(af_abs, 1)
                rotate(6)
                rotate(7)
                operands(2)
                exponents(3)
                scores(1)
                scan(4)
                v.wait_ge(af_ln, l + 1)
                st.mark(v.tensor_scalar(fl[:, 0, :], fl[:, 0, :], 0.0, None, ALU.min))
                st.wait()
                st.mark(v.tensor_tensor(fl[:, 0, :], fl[:, 0, :], fl[:, 1, :], ALU.subtract))
                st.wait()
                st.mark(v.tensor_tensor_scan(fl[:, 2, :], ones[0:4, 0:1].broadcast_to([4, T]), fl[:, 0, :], 0.0,
                                             ALU.mult, ALU.add))
                st.wait()
                v.tensor_scalar(fl[:, 3, :], fl[:, 2, :], -1.0, None, ALU.mult).then_inc(cum_ready, 1)
                scan(5)
                operands(3)
                exponents(4)
                scores(2)
                scan(6)
                st.mark(v.tensor_scalar(fst[:, 0, 0:1], prm("q_gain"), FOX_DIM ** -0.5, None, ALU.mult))
                st.wait()
                for w in range(2):
                    v.wait_ge(frn_ready, l * 2 + w + 1)
                    t = fqk[:, w, :, :].rearrange("p a t -> p (a t)")
                    v.scalar_tensor_tensor(t, t, fst[:, 0, 0:1] if w == 0 else prm("k_gain"), fsq[:, w, :],
                                           ALU.mult, ALU.mult).then_inc(fqk_ready, 1)

                def fox_mask(t):
                    v.wait_ge(sc_done, l * 2 + 2 - t)
                    at, n = t * P, (t + 1) * P
                    for odd in range(2):
                        last = v.tensor_tensor(sc[:, odd:4:2, at:at + n],
                                               bank(6 + odd)[:, 0:2 * n].rearrange("p (h s) -> p h s", h=2),
                                               cmask[:, at:at + n].unsqueeze(1).broadcast_to([P, 2, n]), ALU.add)
                    last.then_inc(sc_read, 1)
                    v.wait_ge(sc_read, l * 2 + 2 - t)
                    st.mark(v.tensor_reduce(fst[:, 0, t * 4:t * 4 + 4], sc[:, :, at:at + n], AX.X, ALU.max))
                    st.wait()
                    v.tensor_scalar(fst[:, 1, t * 4:t * 4 + 4], fst[:, 0, t * 4:t * 4 + 4], -1.0, None, ALU.mult
                                    ).then_inc(max_ready, 1)

                def fox_probabilities(t):
                    v.wait_ge(exp_done, l * 8 + 8 - 4 * t)
                    at, n = t * P, (t + 1) * P
                    st.mark(v.reciprocal(fst[:, 3, t * 4:t * 4 + 4], fst[:, 2, t * 4:t * 4 + 4]))
                    st.wait()
                    v.tensor_tensor(sc[:, :, at:at + n], sc[:, :, at:at + n],
                                    fst[:, 3, t * 4:t * 4 + 4].unsqueeze(2).broadcast_to([P, 4, n]), ALU.mult
                                    ).then_inc(p_ready, 1)

                operands(4)
                exponents(5)
                scores(3)
                scan(7)
                operands(5)
                exponents(6)
                fox_mask(1)
                scores(4)
                v.wait_ge(y_done, l + 1)
                for m in range(2):
                    last = v.scalar_tensor_tensor(y[:, m, :], u[:, m, :], prm("skip", m, 1),
                                                  bank(4)[:, m * T:(m + 1) * T], ALU.mult, ALU.add)
                last.then_inc(y_ready, 1)
                operands(6)
                exponents(7)
                scores(5)
                fox_probabilities(1)
                operands(7)
                scores(6)
                fox_mask(0)
                take(10, bg[:, 0:2, :])
                v.wait_ge(pt_done, l * 2 + 1)
                v.tensor_copy(pT.rearrange("p (h c) -> p h c", c=384)[:, 2:4, P:384],
                              bank(7).rearrange("p (h c) -> p h c", c=T)).then_inc(pt_dve, 1)
                scores(7)
                scores(8)
                fox_probabilities(0)
                v.wait_ge(sg_ready, l + 1)
                v.tensor_tensor(s5_out, z, y, ALU.mult).then_inc(mix_s5, 1)
                take(11, bg[:, 2:4, :])
                v.wait_ge(orn_ready, l + 1)
                st.mark(v.tensor_tensor(orn[:, :], bank(0, 2), osq[:, :], ALU.mult))
                v.wait_ge(bg_ready, l + 1)
                st.wait()
                for hd in range(HEADS):
                    last = v.scalar_tensor_tensor(hgrn_out[:, hd, :], orn[:, hd * T:(hd + 1) * T], prm("o_gain", hd, 1),
                                                  bg[:, hd, :], ALU.mult, ALU.mult)
                last.then_inc(mix_hgrn, 1)
                st.close()

                split_lo(l * SPLIT_UNITS + FFN_UNITS, 0)
                split_lo(l * SPLIT_UNITS + FFN_UNITS + 1, 1)

                def wait_out(m):
                    if m % 2 == 0:
                        v.wait_ge(out_unit_done, l * OUT_UNITS + m // 2 + 1)
                boundary(wait_out, 1.0, l * 2 + 1, prm("gain_ffn2"),
                         lambda m: out_bank(m // 2)[:, (m % 2) * T:(m % 2 + 1) * T])
                ffn_steps(l * 2 + 1, l * SPLIT_UNITS + FFN_UNITS, l * 3 + 2, True)

                def wait_ffn2(m):
                    if m < KT - 2:
                        v.wait_ge(acc_done, l * 6 + 3 + m // 2 + 1)
                    else:
                        v.wait_ge(units_done, l * SPLIT_UNITS + 2 * FFN_UNITS + RING)
                boundary(wait_ffn2, 0.5, l * 2 + 2, prm("gain_next"))


def _tiles(w, cols):
    k = w.shape[0] // P
    return w.reshape(k, P, cols // 256, 256).transpose(2, 1, 0, 3).reshape(cols // 256, P, k * 256)


def _unit_stream(inputs, l):
    def ffn(name):
        g = _tiles(inputs[name + "_w_gate"][l], FF)
        u = _tiles(inputs[name + "_w_up"][l], FF)
        d = inputs[name + "_w_down"][l].reshape(ITERS, 2, P, D).transpose(0, 2, 1, 3).reshape(ITERS, P, 2 * D)
        order = [g[0], u[0]]
        for i in range(1, ITERS):
            order += [g[i], u[i], d[i - 1]]
        return order + [d[ITERS - 1]]

    w = inputs["w_in"][l]
    a = FOX_HEADS * FOX_DIM
    b = 3 * a + FOX_HEADS
    parts = {"q": w[:, 0:a], "k": w[:, a:2 * a], "v": w[:, 2 * a:3 * a], "bq": w[:, b:b + 512],
             "bf": w[:, b + 512:b + 1024], "bi": w[:, b + 1024:b + 1536], "bg": w[:, b + 1536:b + 2048],
             "u": w[:, b + 2048:b + 2304]}
    cols = np.concatenate([parts[n] for n in ("u", "bf", "bq", "q", "k", "bi", "v", "bg")], axis=1)
    w_in = list(_tiles(cols, IN_UNITS * 256))
    w_out = list(_tiles(inputs["w_out"][l], D))
    return ffn("ffn1") + w_in + w_out + ffn("ffn2")


def _params(inputs, l):
    par = np.zeros((P, NPAR), np.float32)

    def put(name, a):
        at, n = COLS[name]
        par[:a.shape[0], at:at + n] = a

    def cols(v):
        return v.reshape(-1, P).T

    put("gain_mix", cols(inputs["mix_norm"][l]))
    put("gain_ffn2", cols(inputs["ffn2_norm"][l]))
    put("gain_next", cols(inputs["ffn1_norm"][(l + 1) % DEPTH]))
    put("lam_re", cols(inputs["s5_lambda_re"][l].reshape(-1)))
    put("lam_im", cols(inputs["s5_lambda_im"][l].reshape(-1)))
    put("log_step", cols(np.repeat(inputs["s5_log_step"][l], STATE)))
    put("lb_logit", np.concatenate([cols(inputs["hgrn_lb"][d]) for d in range(DEPTH)], axis=1))
    put("later_layer", np.full((P, 1), 1.0 if l else 0.0, np.float32))
    put("o_gain", cols(inputs["hgrn_o_gain"][l]))
    put("skip", cols(inputs["s5_D"][l]))
    put("glu_b", cols(inputs["s5_glu_b"][l]))
    put("q_gain", np.tile(inputs["fox_q_gain"][l], 2)[:, None])
    put("k_gain", np.tile(inputs["fox_k_gain"][l], 2)[:, None])
    put("f_bias", inputs["fox_f_bias"][l][:, None])
    forget = inputs["w_in"][l][:, 3 * 256:3 * 256 + FOX_HEADS]
    put("w_forget", forget.reshape(KT, P, FOX_HEADS).transpose(1, 0, 2).reshape(P, -1))
    put("glu_w", inputs["s5_glu_w"][l].reshape(2, P, 256).transpose(1, 0, 2).reshape(P, -1))
    for name, src in (("b_re", "s5_B_re"), ("b_im", "s5_B_im")):
        w = inputs[src][l]
        a = np.zeros((P, 2, P), np.float32)
        for g in range(GROUPS):
            r, c = (g * GROUP) % P, (g % 2) * STATE
            a[r:r + GROUP, g // 8, c:c + STATE] = w[g].T
        put(name, a.reshape(P, -1))
    for name, src in (("c_re", "s5_C_re"), ("c_im", "s5_C_im")):
        w = inputs[src][l]
        a = np.zeros((P, S5_TILES, 32), np.float32)
        for g in range(GROUPS):
            r, c = (g % 2) * STATE, (g % 2) * GROUP
            a[r:r + STATE, g // 2, c:c + GROUP] = w[g].T
        put(name, a.reshape(P, -1))
    return par


def _constants():
    i = np.arange(P)
    causal = np.where(i[:, None] >= i[None, :], 0.0, -1e30)
    carry = np.tile((np.arange(T) % CHUNK != 0).astype(np.float32), (P, 1))
    con = np.concatenate([np.eye(P), np.ones((P, P)), (i[:, None] // 64 == i[None, :] // 64),
                          causal, np.zeros((P, P)), causal, carry], axis=1).astype(np.float32)
    masks = []
    for size in LEVELS:
        masks.append((i[:, None] // (2 * size) == i[None, :] // (2 * size))
                     & (i[:, None] % (2 * size) < size) & (i[None, :] % (2 * size) >= size))
    masks.append(i[:, None] == i[None, :])
    return con, np.stack(masks, axis=1).astype(np.float32)


def kernel(**inputs):
    import concourse.bacc as bacc
    from concourse.bass_utils import run_bass_kernel_spmd

    inputs = {k: np.asarray(v) for k, v in inputs.items()}
    con, masks = _constants()
    arrays = {
        "xT": np.ascontiguousarray(inputs["x"][0].T.reshape(KT, P, T).transpose(1, 0, 2)),
        "stream": np.stack([u for l in range(DEPTH) for u in _unit_stream(inputs, l)]
                           + [np.zeros((P, 2048), np.float32)] * AHEAD),
        "params": np.stack([_params(inputs, l) for l in range(DEPTH)]),
        "gain0": np.ascontiguousarray(inputs["ffn1_norm"][0].reshape(-1, P).T),
        "consts": con, "masks": masks,
    }
    nc = bacc.Bacc("TRN2", target_bir_lowering=False, num_devices=1)
    args = {n: nc.dram_tensor(n, a.shape, mybir.dt.from_np(a.dtype), kind="ExternalInput").ap()
            for n, a in arrays.items()}
    out = nc.dram_tensor("out", (P, KT, T), F32, kind="ExternalOutput").ap()
    build(nc, out=out, **args)
    got = run_bass_kernel_spmd(nc, [arrays], core_ids=[0]).results[0]["out"]
    return np.ascontiguousarray(got.transpose(1, 0, 2).reshape(D, T).T)[None]
```
